# Optimizing a Trainium2 kernel written in Bass

```python
import math
import jax
import jax.numpy as jnp
from jax import lax
import numpy as np

D_MODEL = 1024
BATCH = 1
SEQ = 512
DEPTH = 2

N_EVEN = (DEPTH + 1) // 2
N_ODD = DEPTH // 2
CHUNK = 64
NORM_EPS = 1e-6
RW_HEADS = 8
RW_HEAD_DIM = 64
RW_DIM = RW_HEADS * RW_HEAD_DIM
R_DECAY = 64
R_AAA = 64
R_GATE = 128
RW_IN = 3 * RW_DIM + R_DECAY + R_AAA + R_GATE
RW_LN_EPS = 64e-5
HG_HEADS = 8
HG_KEY_DIM = 64
HG_VAL_DIM = 64
HG_KDIM = HG_HEADS * HG_KEY_DIM
HG_VDIM = HG_HEADS * HG_VAL_DIM
HG_IN = 2 * HG_KDIM + 2 * HG_VDIM
EVEN_IN = RW_IN + HG_IN
EVEN_MIX = RW_DIM + HG_VDIM
GD_HEADS = 4
GD_HEAD_DIM = 128
GD_DIM = GD_HEADS * GD_HEAD_DIM
CONV_K = 4
GD_IN = 4 * GD_DIM + 2 * GD_HEADS
ML_HEADS = 4
ML_HEAD_DIM = 128
ML_DIM = ML_HEADS * ML_HEAD_DIM
ML_IN = 4 * ML_DIM + 2 * ML_HEADS
ODD_IN = GD_IN + ML_IN
ODD_MIX = GD_DIM + ML_DIM
N_GROUPS = 4
EXPERTS_PER_GROUP = 8
N_EXPERTS = N_GROUPS * EXPERTS_PER_GROUP
TOP_K_FINE = 2
D_EXPERT = 256

kernel_name = 'hybrid_rwkv7_hgrn2_gdn_mlstm_hmoe'

def _rms(x, g, eps=NORM_EPS):
    xf = x.astype(jnp.float32)
    y = xf * lax.rsqrt(jnp.mean(xf * xf, axis=-1, keepdims=True) + eps)
    return (y * g.astype(jnp.float32)).astype(x.dtype)

def _l2n(t):
    return t * lax.rsqrt(jnp.sum(t * t, axis=-1, keepdims=True) + 1e-6)

def _heads(t, h):
    return t.reshape(t.shape[:-1] + (h, t.shape[-1] // h))

def _shift(t):
    return jnp.pad(t[:, :-1], ((0, 0), (1, 0), (0, 0)))

def _to_chunks(t):
    b, s, h = t.shape[:3]
    t = t.reshape((b, s // CHUNK, CHUNK, h) + t.shape[3:])
    return jnp.moveaxis(t, (1, 3), (0, 2))

def _from_chunks(t):
    t = jnp.moveaxis(t, (0, 2), (1, 3))
    return t.reshape((t.shape[0], t.shape[1] * t.shape[2]) + t.shape[3:])

def _causal_conv(t, w):
    k = w.shape[0]
    n = t.shape[1]
    tp = jnp.pad(t, ((0, 0), (k - 1, 0), (0, 0)))
    y = tp[:, 0:n] * w[0]
    for j in range(1, k):
        y = y + tp[:, j:j + n] * w[j]
    return y

def _rwkv7_mix(p, mu, w0, w2, a0, a2, g2, k_k, k_a, r_k, ln_w, ln_b):
    bsz, n, _ = p.shape
    p = p + mu * (_shift(p) - p)
    r = p[..., :RW_DIM]
    k = p[..., RW_DIM:2 * RW_DIM]
    v = p[..., 2 * RW_DIM:3 * RW_DIM]
    o1 = 3 * RW_DIM
    wl = p[..., o1:o1 + R_DECAY]
    al = p[..., o1 + R_DECAY:o1 + R_DECAY + R_AAA]
    gl = p[..., o1 + R_DECAY + R_AAA:]
    w = -jax.nn.softplus(-(w0 + jnp.tanh(wl) @ w2)) - 0.5
    decay = jnp.exp(-jnp.exp(w))
    a = jax.nn.sigmoid(a0 + al @ a2)
    g = jax.nn.sigmoid(gl) @ g2
    kk = _l2n(_heads(k * k_k, RW_HEADS))
    k = k * (1.0 + (a - 1.0) * k_a)
    rh, kh, vh, ah, wh = (_heads(t, RW_HEADS) for t in (r, k, v, a, decay))

    def step(s, inp):
        r_t, w_t, k_t, v_t, kk_t, a_t = inp
        sa = jnp.einsum('bhvk,bhk->bhv', s, -kk_t)
        s = s * w_t[:, :, None, :] + sa[..., None] * (kk_t * a_t)[:, :, None, :] + v_t[..., None] * k_t[:, :, None, :]
        return s, jnp.einsum('bhvk,bhk->bhv', s, r_t)

    tm = lambda t: jnp.moveaxis(t, 1, 0)
    s0 = jnp.zeros((bsz, RW_HEADS, RW_HEAD_DIM, RW_HEAD_DIM), jnp.float32)
    _, y = lax.scan(step, s0, (tm(rh), tm(wh), tm(kh), tm(vh), tm(kk), tm(ah)))
    y = jnp.moveaxis(y, 0, 1)
    mean = jnp.mean(y, axis=-1, keepdims=True)
    var = jnp.mean(jnp.square(y - mean), axis=-1, keepdims=True)
    y = ((y - mean) * lax.rsqrt(var + RW_LN_EPS)).reshape(bsz, n, RW_DIM) * ln_w + ln_b
    bonus = jnp.sum(rh * kh * r_k, axis=-1, keepdims=True) * vh
    return (y + bonus.reshape(bsz, n, RW_DIM)) * g

def _chunk_gla(q, k, v, logf):
    q, k, v, logf = (_to_chunks(t) for t in (q, k, v, logf))
    bcum = jnp.cumsum(logf, axis=-2)
    incl = jnp.tril(jnp.ones((CHUNK, CHUNK), dtype=bool))[:, :, None]

    def step(s, inp):
        qc, kc, vc, bc = inp
        b_last = bc[..., -1, :]
        o_inter = jnp.einsum('bhtd,bhdv->bhtv', qc * jnp.exp(bc), s)
        dec = jnp.exp(jnp.where(incl, bc[..., :, None, :] - bc[..., None, :, :], -jnp.inf))
        attn = jnp.einsum('bhtd,bhsd,bhtsd->bhts', qc, kc, dec)
        o = o_inter + attn @ vc
        s = jnp.exp(b_last)[..., None] * s + jnp.einsum('bhsd,bhsv->bhdv', kc * jnp.exp(b_last[..., None, :] - bc), vc)
        return s, o

    bsz, h = q.shape[1], q.shape[2]
    s0 = jnp.zeros((bsz, h, q.shape[-1], v.shape[-1]), jnp.float32)
    _, o = lax.scan(step, s0, (q, k, v, bcum))
    return _from_chunks(o)

def _hgrn2_mix(p, lb, norm_g):
    bsz, n, _ = p.shape
    q = jax.nn.silu(p[..., :HG_KDIM])
    f = p[..., HG_KDIM:2 * HG_KDIM]
    i = p[..., 2 * HG_KDIM:2 * HG_KDIM + HG_VDIM]
    g = p[..., 2 * HG_KDIM + HG_VDIM:]
    fg = lb + (1.0 - lb) * jax.nn.sigmoid(f)
    o = _chunk_gla(_heads(q, HG_HEADS), _heads(1.0 - fg, HG_HEADS), _heads(i, HG_HEADS), _heads(jnp.log(fg), HG_HEADS))
    o = _rms(o, norm_g).reshape(bsz, n, HG_VDIM)
    return o * jax.nn.silu(g)

def _chunk_gated_delta(q, k, v, g, beta):
    q, k, v, g, beta = (_to_chunks(t) for t in (q, k, v, g, beta))
    gam = jnp.cumsum(g, axis=-1)
    incl = jnp.tril(jnp.ones((CHUNK, CHUNK), dtype=bool))
    strict = jnp.tril(jnp.ones((CHUNK, CHUNK), dtype=bool), -1)
    decay = jnp.exp(jnp.where(incl, gam[..., :, None] - gam[..., None, :], -jnp.inf))
    k_beta = k * beta[..., None]
    m = jnp.where(strict, jnp.einsum('...td,...sd->...ts', k_beta, k) * decay, 0.0)
    eye = jnp.eye(CHUNK, dtype=m.dtype)
    tinv = lax.linalg.triangular_solve(eye + m, jnp.broadcast_to(eye, m.shape), left_side=True, lower=True, unit_diagonal=True)
    u = tinv @ (v * beta[..., None])
    w = tinv @ (k_beta * jnp.exp(gam)[..., None])
    attn = jnp.einsum('...td,...sd->...ts', q, k) * decay
    q_dec = q * jnp.exp(gam)[..., None]
    k_dec = k * jnp.exp(gam[..., -1:] - gam)[..., None]
    g_last = jnp.exp(gam[..., -1])

    def step(s, inp):
        u_c, w_c, a_c, qd, kd, gl = inp
        v_new = u_c - w_c @ s
        o = qd @ s + a_c @ v_new
        s = s * gl[..., None, None] + jnp.einsum('bhsd,bhsv->bhdv', kd, v_new)
        return s, o

    s0 = jnp.zeros((q.shape[1], q.shape[2], q.shape[-1], v.shape[-1]), jnp.float32)
    _, o = lax.scan(step, s0, (u, w, attn, q_dec, k_dec, g_last))
    return _from_chunks(o)

def _gdn_mix(p, conv_w, a_log, dt_bias, norm_g):
    bsz, n, _ = p.shape
    qkv = jax.nn.silu(_causal_conv(p[..., :3 * GD_DIM], conv_w))
    q = _l2n(_heads(qkv[..., :GD_DIM], GD_HEADS)) * GD_HEAD_DIM ** -0.5
    k = _l2n(_heads(qkv[..., GD_DIM:2 * GD_DIM], GD_HEADS))
    v = _heads(qkv[..., 2 * GD_DIM:], GD_HEADS)
    z = p[..., 3 * GD_DIM:4 * GD_DIM]
    beta = jax.nn.sigmoid(p[..., 4 * GD_DIM:4 * GD_DIM + GD_HEADS])
    g = -jnp.exp(a_log) * jax.nn.softplus(p[..., 4 * GD_DIM + GD_HEADS:] + dt_bias)
    o = _chunk_gated_delta(q, k, v, g, beta)
    o = _rms(o, norm_g).reshape(bsz, n, GD_DIM)
    return o * jax.nn.silu(z)

def _chunk_mlstm(q, k, v, ig, logf):
    q, k, v, ig, logf = (_to_chunks(t) for t in (q, k, v, ig, logf))
    bcum = jnp.cumsum(logf, axis=-1)
    incl = jnp.tril(jnp.ones((CHUNK, CHUNK), dtype=bool))

    def step(carry, inp):
        c, nvec, m = carry
        qc, kc, vc, igc, bc = inp
        b_last = bc[..., -1]
        d_log = jnp.where(incl, bc[..., :, None] - bc[..., None, :] + igc[..., None, :], -jnp.inf)
        inter_log = bc + m[..., None]
        m_t = jnp.maximum(inter_log, jnp.max(d_log, axis=-1))
        d_w = jnp.exp(d_log - m_t[..., None])
        inter_w = jnp.exp(inter_log - m_t)
        sc = jnp.einsum('bhtd,bhsd->bhts', qc, kc) * d_w
        num = inter_w[..., None] * jnp.einsum('bhtd,bhdv->bhtv', qc, c) + sc @ vc
        den = inter_w * jnp.einsum('bhtd,bhd->bht', qc, nvec) + jnp.sum(sc, axis=-1)
        h = num / jnp.maximum(jnp.abs(den), jnp.exp(-m_t))[..., None]
        upd_log = b_last[..., None] - bc + igc
        m_new = jnp.maximum(b_last + m, jnp.max(upd_log, axis=-1))
        w_s = jnp.exp(upd_log - m_new[..., None])
        dec = jnp.exp(b_last + m - m_new)
        c = dec[..., None, None] * c + jnp.einsum('bhs,bhsd,bhsv->bhdv', w_s, kc, vc)
        nvec = dec[..., None] * nvec + jnp.einsum('bhs,bhsd->bhd', w_s, kc)
        return (c, nvec, m_new), h

    bsz, h = q.shape[1], q.shape[2]
    c0 = jnp.zeros((bsz, h, q.shape[-1], v.shape[-1]), jnp.float32)
    n0 = jnp.zeros((bsz, h, q.shape[-1]), jnp.float32)
    m0 = jnp.zeros((bsz, h), jnp.float32)
    _, o = lax.scan(step, (c0, n0, m0), (q, k, v, ig, bcum))
    return _from_chunks(o)

def _mlstm_mix(p, i_bias, f_bias, norm_g):
    bsz, n, _ = p.shape
    q = _heads(p[..., :ML_DIM], ML_HEADS)
    k = _heads(p[..., ML_DIM:2 * ML_DIM], ML_HEADS) * ML_HEAD_DIM ** -0.5
    v = _heads(p[..., 2 * ML_DIM:3 * ML_DIM], ML_HEADS)
    o_gate = jax.nn.sigmoid(p[..., 3 * ML_DIM:4 * ML_DIM])
    ig = p[..., 4 * ML_DIM:4 * ML_DIM + ML_HEADS] + i_bias
    logf = jax.nn.log_sigmoid(p[..., 4 * ML_DIM + ML_HEADS:] + f_bias)
    h = _chunk_mlstm(q, k, v, ig, logf)
    h = _rms(h, norm_g.reshape(ML_HEADS, ML_HEAD_DIM)).reshape(bsz, n, ML_DIM)
    return o_gate * h

def _hmoe(x, w_group, b_group, w_router, b_router, w_gate, w_up, w_down):
    bsz, n, d = x.shape
    xt = x.reshape(-1, d)
    ntok = xt.shape[0]
    grp_logits = (xt @ w_group).astype(jnp.float32) + b_group.astype(jnp.float32)
    p_grp = jax.nn.softmax(grp_logits, axis=-1)
    p_top, g_idx = lax.top_k(p_grp, 1)
    fine = ((xt @ w_router).astype(jnp.float32) + b_router.astype(jnp.float32)).reshape(ntok, N_GROUPS, EXPERTS_PER_GROUP)
    fine_sel = fine[jnp.arange(ntok), g_idx[:, 0]]
    f_val, f_idx = lax.top_k(fine_sel, TOP_K_FINE)
    gate = p_top * jax.nn.softmax(f_val, axis=-1)
    eid = g_idx * EXPERTS_PER_GROUP + f_idx
    combine = jnp.sum(jax.nn.one_hot(eid, N_EXPERTS, dtype=jnp.float32) * gate[..., None], axis=1)
    y = jnp.zeros((ntok, d), jnp.float32)
    for grp in range(N_GROUPS):
        sl = slice(grp * EXPERTS_PER_GROUP, (grp + 1) * EXPERTS_PER_GROUP)
        hid = jax.nn.silu(jnp.einsum('nd,edf->nef', xt, w_gate[sl])) * jnp.einsum('nd,edf->nef', xt, w_up[sl])
        hid = hid * combine[:, sl, None].astype(hid.dtype)
        y = y + jnp.einsum('nef,efd->nd', hid, w_down[sl]).astype(jnp.float32)
    return y.reshape(bsz, n, d)

def setup_inputs(seed: int = 0) -> dict:
    key = jax.random.key(seed)
    keys = iter(jax.random.split(key, 48))
    f32 = jnp.float32

    def nrm(shape, scale):
        return jax.random.normal(next(keys), shape, f32) * scale

    def unif(shape, lo, hi):
        return jax.random.uniform(next(keys), shape, f32, lo, hi)

    ne, no = N_EVEN, N_ODD
    x = nrm((BATCH, SEQ, D_MODEL), 1.0)
    norm_mix = 1.0 + nrm((DEPTH, D_MODEL), 0.05)
    norm_ffn = 1.0 + nrm((DEPTH, D_MODEL), 0.05)
    norm_final = 1.0 + nrm((D_MODEL,), 0.05)
    ev_w_in = nrm((ne, D_MODEL, EVEN_IN), D_MODEL ** -0.5)
    ev_mu = unif((ne, RW_IN), 0.0, 1.0)
    rw_w0 = -1.0 + nrm((ne, RW_DIM), 0.5)
    rw_w2 = nrm((ne, R_DECAY, RW_DIM), 0.5 * R_DECAY ** -0.5)
    rw_a0 = nrm((ne, RW_DIM), 0.1)
    rw_a2 = nrm((ne, R_AAA, RW_DIM), 0.5 * R_AAA ** -0.5)
    rw_g2 = nrm((ne, R_GATE, RW_DIM), R_GATE ** -0.5)
    rw_k_k = 0.85 + nrm((ne, RW_DIM), 0.05)
    rw_k_a = 1.0 + nrm((ne, RW_DIM), 0.05)
    rw_r_k = nrm((ne, RW_HEADS, RW_HEAD_DIM), 0.1)
    rw_ln_w = 1.0 + nrm((ne, RW_DIM), 0.05)
    rw_ln_b = nrm((ne, RW_DIM), 0.02)
    hg_lb_logits = nrm((ne + 1, HG_KDIM), 0.5)
    hg_norm = 1.0 + nrm((ne, HG_VAL_DIM), 0.05)
    ev_w_out = nrm((ne, EVEN_MIX, D_MODEL), EVEN_MIX ** -0.5)
    od_w_in = nrm((no, D_MODEL, ODD_IN), D_MODEL ** -0.5)
    gd_conv = nrm((no, CONV_K, 3 * GD_DIM), CONV_K ** -0.5)
    gd_a_log = jnp.log(unif((no, GD_HEADS), 1.0, 16.0))
    dt = jnp.exp(unif((no, GD_HEADS), math.log(1e-3), math.log(1e-1)))
    gd_dt_bias = dt + jnp.log(-jnp.expm1(-dt))
    gd_norm = 1.0 + nrm((no, GD_HEAD_DIM), 0.05)
    ml_i_bias = nrm((no, ML_HEADS), 0.1)
    ml_f_bias = jnp.linspace(3.0, 6.0, ML_HEADS, dtype=f32) + nrm((no, ML_HEADS), 0.1)
    ml_norm = 1.0 + nrm((no, ML_DIM), 0.05)
    od_w_out = nrm((no, ODD_MIX, D_MODEL), ODD_MIX ** -0.5)
    moe_w_group = nrm((DEPTH, D_MODEL, N_GROUPS), D_MODEL ** -0.5)
    moe_b_group = nrm((DEPTH, N_GROUPS), 0.01)
    moe_w_router = nrm((DEPTH, D_MODEL, N_EXPERTS), D_MODEL ** -0.5)
    moe_b_router = nrm((DEPTH, N_EXPERTS), 0.01)
    moe_w_gate = nrm((DEPTH, N_EXPERTS, D_MODEL, D_EXPERT), D_MODEL ** -0.5)
    moe_w_up = nrm((DEPTH, N_EXPERTS, D_MODEL, D_EXPERT), D_MODEL ** -0.5)
    moe_w_down = nrm((DEPTH, N_EXPERTS, D_EXPERT, D_MODEL), D_EXPERT ** -0.5)
    return {'x': x, 'norm_mix': norm_mix, 'norm_ffn': norm_ffn, 'norm_final': norm_final,
            'ev_w_in': ev_w_in, 'ev_mu': ev_mu, 'rw_w0': rw_w0, 'rw_w2': rw_w2, 'rw_a0': rw_a0,
            'rw_a2': rw_a2, 'rw_g2': rw_g2, 'rw_k_k': rw_k_k, 'rw_k_a': rw_k_a, 'rw_r_k': rw_r_k,
            'rw_ln_w': rw_ln_w, 'rw_ln_b': rw_ln_b, 'hg_lb_logits': hg_lb_logits, 'hg_norm': hg_norm,
            'ev_w_out': ev_w_out, 'od_w_in': od_w_in, 'gd_conv': gd_conv, 'gd_a_log': gd_a_log,
            'gd_dt_bias': gd_dt_bias, 'gd_norm': gd_norm, 'ml_i_bias': ml_i_bias, 'ml_f_bias': ml_f_bias,
            'ml_norm': ml_norm, 'od_w_out': od_w_out, 'moe_w_group': moe_w_group, 'moe_b_group': moe_b_group,
            'moe_w_router': moe_w_router, 'moe_b_router': moe_b_router, 'moe_w_gate': moe_w_gate,
            'moe_w_up': moe_w_up, 'moe_w_down': moe_w_down}

def reference(x, norm_mix, norm_ffn, norm_final, ev_w_in, ev_mu, rw_w0, rw_w2, rw_a0, rw_a2, rw_g2,
              rw_k_k, rw_k_a, rw_r_k, rw_ln_w, rw_ln_b, hg_lb_logits, hg_norm, ev_w_out, od_w_in,
              gd_conv, gd_a_log, gd_dt_bias, gd_norm, ml_i_bias, ml_f_bias, ml_norm, od_w_out,
              moe_w_group, moe_b_group, moe_w_router, moe_b_router, moe_w_gate, moe_w_up, moe_w_down):
    lb_table = jnp.cumsum(jax.nn.softmax(hg_lb_logits.astype(jnp.float32), axis=0), axis=0)
    h = x
    for layer in range(DEPTH):
        hn = _rms(h, norm_mix[layer])
        j = layer // 2
        if layer % 2 == 0:
            p = jnp.matmul(hn, ev_w_in[j]).astype(jnp.float32)
            ya = _rwkv7_mix(p[..., :RW_IN], ev_mu[j], rw_w0[j], rw_w2[j], rw_a0[j], rw_a2[j], rw_g2[j],
                            rw_k_k[j], rw_k_a[j], rw_r_k[j], rw_ln_w[j], rw_ln_b[j])
            yb = _hgrn2_mix(p[..., RW_IN:], lb_table[j], hg_norm[j])
            mix = jnp.matmul(jnp.concatenate([ya, yb], axis=-1), ev_w_out[j])
        else:
            p = jnp.matmul(hn, od_w_in[j]).astype(jnp.float32)
            yc = _gdn_mix(p[..., :GD_IN], gd_conv[j], gd_a_log[j], gd_dt_bias[j], gd_norm[j])
            yd = _mlstm_mix(p[..., GD_IN:], ml_i_bias[j], ml_f_bias[j], ml_norm[j])
            mix = jnp.matmul(jnp.concatenate([yc, yd], axis=-1), od_w_out[j])
        h = h + mix.astype(h.dtype)
        ffn = _hmoe(_rms(h, norm_ffn[layer]), moe_w_group[layer], moe_b_group[layer], moe_w_router[layer],
                    moe_b_router[layer], moe_w_gate[layer], moe_w_up[layer], moe_w_down[layer])
        h = h + ffn.astype(h.dtype)
    return _rms(h, norm_final)


_drawn_inputs = setup_inputs


def setup_inputs(seed=0):
    import zlib

    import numpy as np

    out = dict(_drawn_inputs(seed))
    spreads = {}
    factors = {'rw_k_k': 2.94,
     'ml_i_bias': 64.0,
     'ml_norm': 2.775,
     'moe_b_router': 3.188,
     'gd_a_log': 2.755,
     'gd_norm': 3.118}
    for name, (base, spread) in spreads.items():
        noise = np.random.default_rng([zlib.crc32(name.encode()), seed]).standard_normal(out[name].shape)
        drawn = base * np.exp(spread * noise) if base else spread * noise
        out[name] = jnp.asarray(drawn.astype(out[name].dtype))
    for name, factor in factors.items():
        out[name] = (out[name] * factor).astype(out[name].dtype)
    return out
```

```python
from contextlib import ExitStack
import math

import concourse.bass as bass
from concourse import mybir

F32 = mybir.dt.float32
I32 = mybir.dt.int32
ALU = mybir.AluOpType
ACT = mybir.ActivationFunctionType
AX = mybir.AxisListType

P = 128
D = 1024
T = 512
NT = T // P
KD = D // P
NORM_EPS = 1e-6
RW_LN_EPS = 64e-5
E = 32
GROUPS = 4
EPG = E // GROUPS
DE = 256
SLOTS = 2 * T
WIN = 64
BIG = 1e30

PAR_ROWS = [
    ("ev_mu", 14), ("rw_w0", 4), ("rw_a0", 4), ("rw_k_k", 4), ("rw_k_a", 4), ("rw_r_k", 4),
    ("rw_ln_w", 4), ("rw_ln_b", 4), ("hg_lb_logits", 8), ("hg_norm", 1), ("gd_norm", 1), ("ml_norm", 4),
    ("norm_mix", 16), ("norm_ffn", 16), ("gd_conv", 48),
]
PAR_AT = {}
_at = 0
for _name, _n in PAR_ROWS:
    if _name == "gd_conv":
        _at = P
    PAR_AT[_name] = _at
    _at += _n
PAR_COLS = 2 * P


def chained(eng, sem, count):

    def link(ins):
        count[0] += 1
        ins.then_inc(sem, 1)
        eng.wait_ge(sem, count[0])
        return count[0]

    return link


class Build:

    def __init__(self, nc, dram, out, ctx):
        self.nc, self.dram, self.out, self.ctx = nc, dram, out, ctx
        self.sems = {}
        self.layer = 0
        self.counts = {}
        self.h = self.sb(ctx, "h", [P, NT, D])
        self.par = self.sb(ctx, "par", [P, PAR_COLS])
        self.ident = self.sb(ctx, "ident", [P, P])
        self.causal = self.sb(ctx, "causal", [P, P])
        self.before = self.sb(ctx, "before", [P, P])
        self.ones = self.sb(ctx, "ones", [P, P])
        self.halves = self.sb(ctx, "halves", [P, P])
        self.level = self.sb(ctx, "level", [P, 7, P])
        self.level0T = self.sb(ctx, "level0T", [P, P])
        self.small = self.sb(ctx, "small", [P, 64])
        self.eps = self.sb(ctx, "eps", [P, 4])
        self.psum = ctx.enter_context(nc.psum_tensor("psum", [P, 8, 512], F32))
        self.bank = [self.psum[:, i, :] for i in range(8)]

    def sb(self, ctx, name, shape, dt=F32):
        return ctx.enter_context(self.nc.sbuf_tensor(name, shape, dt))

    def sem(self, name):
        if name not in self.sems:
            self.sems[name] = self.nc.alloc_semaphore(name=f"{name}_{self.layer}")
        return self.sems[name]

    def end_layer(self):
        self.nc.clear_and_free_semaphores(list(self.sems.values()))
        self.nc.all_engine_barrier()
        self.layer += 1
        self.sems.clear()
        self.counts.clear()

    def link(self, eng, name):
        return chained(eng, self.sem(name), self.counts.setdefault(name, [0]))

    def col(self, name, i=0):
        c = PAR_AT[name] + i
        return self.par[:, c:c + 1]


def constants(b):
    nc, d = b.nc, b.dram
    with ExitStack() as ctx:
        rows = b.sb(ctx, "par_rows", [P, 2, P])
        block = ctx.enter_context(nc.Block())
        rows_in, rows_zero, x_in = b.sem("rows_in"), b.sem("rows_zero"), b.sem("x_in")
        masks, rows_turned = b.sem("masks"), b.sem("rows_turned")
        where = []
        for name, n in PAR_ROWS:
            at = PAR_AT[name]
            if name in ("norm_mix", "norm_ffn"):
                continue
            src = d[name]
            if name == "hg_norm":
                for half in range(2):
                    where.append((rows[at:at + 1, 0, 64 * half:64 * half + 64], src))
                continue
            if len(src.shape) == 3:
                src = src.rearrange("a b c -> a (b c)")
            src = src.rearrange("a (n p) -> (a n) p", p=P)
            where.append((rows[at % P:at % P + n, at // P, :], src))

        @block.sync
        def _(sp):
            for i in range(NT):
                sp.dma_start(b.h[:, i, :], d["x"][0, P * i:P * i + P, :]).then_inc(x_in, 16)
            sp.wait_ge(rows_zero, 1)
            for dst, src in where:
                sp.dma_start(dst, src).then_inc(rows_in, 16)

        @block.gpsimd
        def _(pool):
            link = b.link(pool, "pool_steps")
            nc.gpsimd.memset(b.eps[:, 0:1], 1e-6)
            nc.gpsimd.memset(b.eps[:, 1:2], RW_LN_EPS)
            nc.gpsimd.memset(b.eps[:, 2:3], -0.5 * math.log(128.0))
            nc.gpsimd.memset(b.eps[:, 3:4], 0.0)
            nc.gpsimd.memset(b.ident[:, :], 0.0)
            nc.gpsimd.memset(b.causal[:, :], 0.0)
            nc.gpsimd.memset(b.before[:, :], 0.0)
            nc.gpsimd.memset(b.halves[:, :], 0.0)
            nc.gpsimd.memset(b.level[:, :, :], 0.0)
            link(nc.gpsimd.memset(b.ones[:, :], 1.0))
            link(nc.gpsimd.memset(b.halves[0:64, 0:64], 1.0))
            link(nc.gpsimd.memset(b.halves[64:128, 64:128], 1.0))
            nc.gpsimd.affine_select(out=b.ident[:, :], in_=b.ident[:, :], compare_op=ALU.not_equal, fill=1.0,
                                    base=0, pattern=[[-1, P]], channel_multiplier=1)
            nc.gpsimd.affine_select(out=b.causal[:, :], in_=b.ones[:, :], compare_op=ALU.is_ge, fill=0.0,
                                    base=0, pattern=[[1, P]], channel_multiplier=-1)
            nc.gpsimd.affine_select(out=b.before[:, :], in_=b.ones[:, :], compare_op=ALU.is_ge, fill=0.0,
                                    base=-1, pattern=[[1, P]], channel_multiplier=-1)
            for l in range(7):
                m = 1 << l
                n = P // (2 * m)
                v = b.level[:, l, :].rearrange("p (n two m) -> p n two m", two=2, m=m)
                src = b.ones[:, :].rearrange("p (n two m) -> p n two m", two=2, m=m)
                link(nc.gpsimd.affine_select(out=v[:, :, 0, :], in_=src[:, :, 0, :], compare_op=ALU.is_ge, fill=0.0,
                                             base=-m, pattern=[[-2 * m, n], [0, m]], channel_multiplier=1))
                link(nc.gpsimd.affine_select(out=v[:, :, 0, :], in_=v[:, :, 0, :], compare_op=ALU.is_ge, fill=0.0,
                                             base=2 * m - 1, pattern=[[2 * m, n], [0, m]], channel_multiplier=-1))
            nc.gpsimd.memset(b.small[:, :], 0.0).then_inc(masks, 1)

        @block.scalar
        def _(act):
            for name in ("norm_mix", "norm_ffn"):
                at = PAR_AT[name]
                for layer in range(2):
                    act.dma_start(b.par[:, at + 8 * layer:at + 8 * layer + 8],
                                  d[name][layer].rearrange("(p k) -> p k", k=KD)).then_inc(b.sem("gains_in"), 16)
            act.wait_ge(b.sem("gains_in"), 64)
            act.wait_ge(x_in, 16 * NT)

        @block.vector
        def _(dve):
            nc.vector.memset(rows[:, :, :], 0.0).then_inc(rows_zero, 1)
            dve.wait_ge(rows_turned, 3)
            nc.vector.tensor_copy(b.level0T[:, :], b.bank[2][:, 0:P])
            n = PAR_AT["norm_mix"]
            nc.vector.tensor_copy(b.par[:, 0:n], b.bank[0][:, 0:n])
            nc.vector.tensor_copy(b.par[:, P:2 * P], b.bank[1][:, 0:P])

        @block.tensor
        def _(pe):
            pe.wait_ge(masks, 1)
            pe.wait_ge(b.sem("pool_steps"), 17)
            pe.wait_ge(rows_in, 16 * len(where))
            for i in range(2):
                nc.tensor.transpose(b.bank[i][:, 0:P], rows[:, i, :], b.ident[:, :]).then_inc(rows_turned, 1)
            nc.tensor.transpose(b.bank[2][:, 0:P], b.level[:, 0, :], b.ident[:, :]).then_inc(rows_turned, 1)


def norm_into(b, tag, gain_at, xn, waste, hT):
    nc = b.nc
    with ExitStack() as ctx:
        ss = b.sb(ctx, f"ss_{tag}", [P, NT])
        rstd = b.sb(ctx, f"rstd_{tag}", [P, NT])
        block = ctx.enter_context(nc.Block())
        squares, root, scaled = b.sem(f"squares_{tag}"), b.sem(f"root_{tag}"), b.sem(f"scaled_{tag}")
        mean_ready, turned, evac = b.sem(f"mean_{tag}"), b.sem(f"turned_{tag}"), b.sem(f"evac_{tag}")

        @block.scalar
        def _(act):
            for i in range(NT):
                if i:
                    act.wait_ge(squares, i)
                nc.scalar.activation(waste[:, :], b.h[:, i, :], ACT.Square, accum_out=ss[:, i:i + 1]).then_inc(squares, 1)
            act.wait_ge(mean_ready, 1)
            nc.scalar.activation(ss[:, :], ss[:, :], ACT.Sqrt).then_inc(root, 1)
            for k in range(1, KD, 2):
                act.wait_ge(turned, k + 1)
                nc.scalar.activation(hT[:, k, :], b.bank[k % 4][:, :], ACT.Copy,
                                     scale=b.par[:, gain_at + k:gain_at + k + 1]).then_inc(evac, 1)

        @block.vector
        def _(dve):
            dve.wait_ge(squares, NT)
            nc.vector.tensor_scalar(ss[:, :], ss[:, :], 1.0 / D, NORM_EPS, ALU.mult, ALU.add).then_inc(mean_ready, 1)
            dve.wait_ge(root, 1)
            link = b.link(dve, "dve_steps")
            link(nc.vector.reciprocal(rstd[:, :], ss[:, :]))
            for i in range(NT):
                nc.vector.tensor_scalar(xn[:, i, :], b.h[:, i, :], rstd[:, i:i + 1], None, ALU.mult).then_inc(scaled, 1)
            for k in range(0, KD, 2):
                dve.wait_ge(turned, k + 1)
                nc.vector.tensor_scalar(hT[:, k, :], b.bank[k % 4][:, :], b.par[:, gain_at + k:gain_at + k + 1], None,
                                        ALU.mult).then_inc(b.sem(f"evac_even_{tag}"), 1)

        @block.tensor
        def _(pe):
            by_k = xn[:, :, :].rearrange("p i (q k) -> p i k q", k=KD)
            for k in range(KD):
                if k >= 4:
                    pe.wait_ge(evac if k % 2 else b.sem(f"evac_even_{tag}"), (k - 4) // 2 + 1)
                for i in range(NT):
                    if k == 0:
                        pe.wait_ge(scaled, i + 1)
                    last = nc.tensor.transpose(b.bank[k % 4][:, P * i:P * i + P], by_k[:, i, k, :], b.ident[:, :])
                last.then_inc(turned, 1)


RW_H, RW_F = 8, 64
DECAY_RATE = math.exp(-0.5)
EVEN_LOADS = [(0, 512), (512, 512), (1024, 512), (1536, 256), (1792, 512), (2304, 512), (2816, 512), (3328, 512)]


def flat(t):
    return t[:, :, :].rearrange("p a t -> p (a t)")


class Order:

    def __init__(self, fills, acts, dves, filled, by_act, by_dve):
        self.fills, self.acts, self.dves = fills, acts, dves
        self.filled, self.by_act, self.by_dve = filled, by_act, by_dve

    def wait_filled(self, eng, c, f):
        eng.wait_ge(self.filled, c * len(self.fills) + self.fills.index(f) + 1)

    def wait_taken(self, eng, c, f):
        if f in self.acts:
            eng.wait_ge(self.by_act, c * len(self.acts) + self.acts.index(f) + 1)
        else:
            eng.wait_ge(self.by_dve, c * len(self.dves) + self.dves.index(f) + 1)


def doubling_fills():
    fills = []
    for l in range(1, 7):
        fills += [(f"P{l}", 0), (f"P{l}", 1)]
        for g in range(2):
            fills += ([(f"X{l}", g)] if l < 6 else []) + [(f"XT{l}", g)]
    return fills


def doubling_bank(name):
    return 4 if name.startswith("XT") else 2 if name.startswith("X") else 0


def first_inverse(nc, b, link, MT, XT):
    def four(mask):
        return mask.rearrange("p (o s) -> p o s", o=1).broadcast_to([P, 4, P])

    link(nc.vector.tensor_tensor(XT, MT, four(b.level0T[:, :]), ALU.mult))
    return nc.vector.tensor_tensor(XT, XT, four(b.ident[:, :]), ALU.add)


def take_doubling(nc, b, name, g, bank, X, XT, PR):
    hs = slice(4 * g, 4 * g + 4)
    if name[0] == "P":
        mask = b.level[:, int(name[1:]), :].rearrange("p (o s) -> p o s", o=1).broadcast_to([P, 4, P])
        return nc.vector.tensor_tensor(PR[:, hs, :], bank, mask, ALU.mult)
    dst = (XT if name.startswith("XT") else X)[:, hs, :]
    return nc.vector.tensor_tensor(dst, bank, dst, ALU.add)


def pe_doubling(nc, pe, order, c, bank_of, MT, X, XT, PR):
    for l in range(1, 7):
        for g in range(2):
            order.wait_taken(pe, c, ("X0", g) if l == 1 else (f"X{l - 1}", g))
            for i in range(4 * g, 4 * g + 4):
                last = nc.tensor.matmul(bank_of("P", g)[:, P * (i % 4):P * (i % 4) + P], MT[:, i, :], X[:, i, :],
                                        start=True, stop=True)
            last.then_inc(order.filled, 1)
        for g in range(2):
            order.wait_taken(pe, c, (f"P{l}", g))
            if l > 1:
                order.wait_taken(pe, c, (f"XT{l - 1}", g))
            if l < 6:
                for i in range(4 * g, 4 * g + 4):
                    last = nc.tensor.matmul(bank_of("X", g)[:, P * (i % 4):P * (i % 4) + P], XT[:, i, :], PR[:, i, :],
                                            start=True, stop=True)
                last.then_inc(order.filled, 1)
            for i in range(4 * g, 4 * g + 4):
                last = nc.tensor.matmul(bank_of("XT", g)[:, P * (i % 4):P * (i % 4) + P], PR[:, i, :], XT[:, i, :],
                                        start=True, stop=True)
            last.then_inc(order.filled, 1)


def chunks(t):
    return t[:, :, :].rearrange("p a (c t) -> p a c t", c=NT)


class Even:

    def __init__(self, b, ctx):
        def sb(name, *shape):
            return b.sb(ctx, name, [P, *shape])

        self.w = sb("w_even", 2, KD, 512)
        self.hT = sb("hT_even", KD, T)
        self.RKx = sb("RKx", 8, T)
        self.R, self.K = self.RKx[:, 0:4, :], self.RKx[:, 4:8, :]
        self.xn = self.RKx[:, :, :].rearrange("p (i a) t -> p i (a t)", i=NT)
        self.V = sb("V", 4, T)
        self.WA, self.GL = sb("WA", T), sb("GL", T)
        self.DEC, self.A, self.G, self.KK = sb("DEC", 4, T), sb("A", 4, T), sb("G", 4, T), sb("KK", 4, T)
        self.BON = self.DEC
        self.TMP, self.TMP2 = sb("TMP", 4, T), sb("TMP2", 4, T)
        self.EP, self.EN, self.EA = sb("EP", 4, T), sb("EN", 4, T), sb("EA", 4, T)
        self.Q, self.F, self.I, self.GG = sb("Q", 4, T), sb("F", 4, T), sb("I", 4, T), sb("GG", 4, T)
        self.Vt = self.EP
        self.EM, self.EL, self.ELM = sb("EM", 4, NT), sb("EL", 4, NT), sb("ELM", 4, NT)
        self.raw = flat(self.GG)[:, 0:2 * (T + 1)].rearrange("p (a t) -> p a t", a=2)
        self.lora2 = self.I[:, 0, :]
        self.g2 = self.I[:, 1, :]
        self.stat = sb("stat", 32)
        self.lb = sb("lb", 4)
        self.oml = sb("oml", 4)


def even_project(b, m):
    nc, d = b.nc, b.dram
    w_in = d["ev_w_in"][0].rearrange("(p k) n -> p k n", k=KD)

    items = [(kind, j) for kind in ("r", "k", "v") for j in range(4)] + [("wa", 0), ("gl", 0)]
    items += [(kind, j) for kind in ("q", "lw", "la", "lg", "f", "kk", "i", "bonus", "vt", "g") for j in range(4)]
    at = {it: n for n, it in enumerate(items)}
    by_dve = [at["bonus", j] for j in range(4)]
    loads = ["r", "k", "v", "wa", "q", "f", "i", "g"]
    last_of_load = [at[kind, 3] if kind != "wa" else at["gl", 0] for kind in loads]

    with nc.Block() as block:
        w_sem = [b.sem("even_w_in0"), b.sem("even_w_in1")]
        lora_sem = b.sem("even_lora_in")
        made, evac, evac_dve = b.sem("even_made"), b.sem("even_evac"), b.sem("even_evac_dve")
        mixed, kkr_ready, squares = b.sem("even_mixed"), b.sem("even_kkr"), b.sem("even_squares")
        lora_act, rk_ready, exponents = b.sem("even_lora_act"), b.sem("even_rk"), b.sem("even_exponents")
        r_decayed = b.sem("even_r_decayed")
        exps, ln_done = b.sem("even_exps"), b.sem("even_ln")

        def evacuated(eng, n):
            if n in by_dve:
                eng.wait_ge(evac_dve, by_dve.index(n) + 1)
            else:
                eng.wait_ge(evac, n + 1 - sum(x < n for x in by_dve))

        @block.sync
        def _(sp):
            for n, (c, width) in enumerate(EVEN_LOADS):
                if n >= 2:
                    sp.wait_ge(made, last_of_load[n - 2] + 1)
                sp.dma_start(m.w[:, n % 2, :, 0:width], w_in[:, :, c:c + width]).then_inc(w_sem[n % 2], 16)
                if n == 1:
                    sp.dma_start(m.lora2[0:64, :], d["rw_w2"][0]).then_inc(lora_sem, 16)
                    sp.dma_start(m.lora2[64:128, :], d["rw_a2"][0]).then_inc(lora_sem, 16)
                    sp.dma_start(m.g2[:, :], d["rw_g2"][0]).then_inc(lora_sem, 16)

        @block.tensor
        def _(pe):
            for n, (kind, j) in enumerate(items):
                bank = b.bank[n % 8][:, :]
                if n >= 8:
                    evacuated(pe, n - 8)
                if kind in ("r", "k", "v", "wa", "gl", "q", "f", "i", "g"):
                    load = loads.index("wa" if kind == "gl" else kind)
                    if j == 0:
                        pe.wait_ge(w_sem[load % 2], 16 * (load // 2 + 1))
                    w = m.w[:, load % 2, :, :]
                    jj = 1 if kind == "gl" else j
                    for k in range(KD):
                        if kind == "i":
                            last = nc.tensor.matmul(bank, m.hT[:, k, P * j:P * j + P], w[:, k, :],
                                                    start=(k == 0), stop=(k == KD - 1))
                        else:
                            last = nc.tensor.matmul(bank, w[:, k, P * jj:P * jj + P], m.hT[:, k, :],
                                                    start=(k == 0), stop=(k == KD - 1))
                elif kind == "lw":
                    pe.wait_ge(lora_sem, 48)
                    pe.wait_ge(lora_act, 1)
                    last = nc.tensor.matmul(bank, m.lora2[0:64, P * j:P * j + P], m.WA[0:64, :], start=True, stop=True)
                elif kind == "la":
                    last = nc.tensor.matmul(bank, m.lora2[64:128, P * j:P * j + P], m.WA[64:128, :],
                                            start=True, stop=True)
                elif kind == "lg":
                    pe.wait_ge(lora_act, 2)
                    last = nc.tensor.matmul(bank, m.g2[:, P * j:P * j + P], m.GL[:, :], start=True, stop=True)
                elif kind == "kk":
                    pe.wait_ge(squares, j + 1)
                    last = nc.tensor.matmul(bank, b.halves[:, :], m.TMP[:, j, :], start=True, stop=True)
                elif kind == "bonus":
                    pe.wait_ge(rk_ready, j + 1)
                    last = nc.tensor.matmul(bank, b.halves[:, :], m.TMP2[:, j, :], start=True, stop=True)
                elif kind == "vt":
                    pe.wait_ge(mixed, 12)
                    for c in range(NT):
                        last = nc.tensor.transpose(bank[:, P * c:P * c + P], m.V[:, j, P * c:P * c + P], b.ident[:, :])
                last.then_inc(made, 1)

        @block.scalar
        def _(act):
            def evacuate(n):
                kind, j = items[n]
                bank = b.bank[n % 8][:, :]
                act.wait_ge(made, n + 1)
                if n < 14:
                    if n >= 2:
                        act.wait_ge(mixed, n - 1)
                    ins = nc.scalar.activation(m.raw[:, n % 2, 1:T + 1], bank, ACT.Copy)
                elif kind in ("q", "g"):
                    ins = nc.scalar.activation((m.Q if kind == "q" else m.GG)[:, j, :], bank, ACT.Silu)
                elif kind == "f":
                    ins = nc.scalar.activation(m.F[:, j, :], bank, ACT.Sigmoid)
                elif kind == "lw":
                    ins = nc.scalar.activation(m.DEC[:, j, :], bank, ACT.Sigmoid, bias=b.col("rw_w0", j))
                elif kind == "la":
                    ins = nc.scalar.activation(m.A[:, j, :], bank, ACT.Sigmoid, bias=b.col("rw_a0", j))
                elif kind == "kk":
                    nc.scalar.activation(m.TMP[:, j, :], bank, ACT.Ln, bias=b.eps[:, 0:1]).then_inc(ln_done, 1)
                    act.wait_ge(ln_done, j + 1)
                    ins = nc.scalar.activation(m.TMP[:, j, :], m.TMP[:, j, :], ACT.Exp, scale=-0.5)
                elif kind == "vt":
                    act.wait_ge(r_decayed, 1)
                    ins = nc.scalar.activation(m.Vt[:, :, P * j:P * j + P],
                                               bank.rearrange("p (c f) -> p c f", c=NT), ACT.Copy)
                else:
                    ins = nc.scalar.activation((m.G if kind == "lg" else m.I)[:, j, :], bank, ACT.Copy)
                ins.then_inc(evac, 1)

            for n in range(at["q", 1]):
                evacuate(n)
            act.wait_ge(mixed, 13)
            nc.scalar.activation(m.WA[0:64, :], m.WA[0:64, :], ACT.Tanh).then_inc(lora_act, 1)
            act.wait_ge(mixed, 14)
            nc.scalar.activation(m.GL[:, :], m.GL[:, :], ACT.Sigmoid).then_inc(lora_act, 1)
            act.wait_ge(kkr_ready, 4)
            for j in range(4):
                nc.scalar.activation(m.TMP[:, j, :], m.KK[:, j, :], ACT.Square).then_inc(squares, 1)
            for n in range(at["q", 1], at["f", 0]):
                evacuate(n)
            act.wait_ge(exponents, 2)
            nc.scalar.activation(flat(m.EP), flat(m.EN), ACT.Exp, scale=-DECAY_RATE).then_inc(exps, 1)
            act.wait_ge(exps, 1)
            nc.scalar.activation(flat(m.EN), flat(m.EN), ACT.Exp, scale=DECAY_RATE).then_inc(exps, 1)
            nc.scalar.activation(flat(m.EA), flat(m.EA), ACT.Exp, scale=-DECAY_RATE).then_inc(exps, 1)
            nc.scalar.activation(m.EM[:, :, :], chunks(m.TMP2)[:, :, :, 63], ACT.Exp, scale=-DECAY_RATE).then_inc(exps, 1)
            nc.scalar.activation(m.EL[:, :, :], chunks(m.TMP2)[:, :, :, 127], ACT.Exp, scale=-DECAY_RATE).then_inc(exps, 1)
            nc.scalar.activation(m.ELM[:, :, :], chunks(m.EP)[:, :, :, 127], ACT.Copy).then_inc(exps, 1)
            for n in range(at["f", 0], len(items)):
                if n not in by_dve:
                    evacuate(n)

        @block.vector
        def _(dve):
            link = b.link(dve, "dve_steps")
            link(nc.vector.memset(m.raw[:, :, 0:1], 0.0))
            dsts = [m.R[:, j, :] for j in range(4)] + [m.K[:, j, :] for j in range(4)]
            dsts += [m.V[:, j, :] for j in range(4)] + [m.WA[:, :], m.GL[:, :]]
            for n, dst in enumerate(dsts):
                dve.wait_ge(evac, n + 1)
                raw = m.raw[:, n % 2, :]
                link(nc.vector.tensor_tensor(dst, raw[:, 0:T], raw[:, 1:T + 1], ALU.subtract))
                nc.vector.scalar_tensor_tensor(dst, dst, b.col("ev_mu", n), raw[:, 1:T + 1], ALU.mult,
                                               ALU.add).then_inc(mixed, 1)
                if 4 <= n < 8:
                    dve.wait_ge(mixed, n + 1)
                    nc.vector.tensor_scalar(m.KK[:, n - 4, :], dst, b.col("rw_k_k", n - 4), None,
                                            ALU.mult).then_inc(kkr_ready, 1)
            for j in range(4):
                evacuated(dve, at["lw", j])
                for c in range(NT):
                    last = nc.vector.tensor_tensor_scan(m.TMP2[:, j, P * c:P * c + P], b.ones[:, :],
                                                        m.DEC[:, j, P * c:P * c + P], 0.0, ALU.mult, ALU.add)
                link(last)
            middle = chunks(m.TMP2)[:, :, :, 63:64].broadcast_to([P, 4, NT, P])
            for j in range(4):
                last = nc.vector.tensor_tensor(chunks(m.EN)[:, j, :, :], chunks(m.TMP2)[:, j, :, :],
                                               middle[:, j, :, :], ALU.subtract)
            last.then_inc(exponents, 1)
            dve.wait_ge(exponents, 1)
            nc.vector.tensor_tensor(flat(m.EA), flat(m.EN), flat(m.DEC), ALU.subtract).then_inc(exponents, 1)
            evacuated(dve, at["la", 3])
            dve.wait_ge(exps, 6)
            for j in range(4):
                link(nc.vector.tensor_scalar(m.TMP2[:, j, :], m.A[:, j, :], 1.0, b.col("rw_k_a", j),
                                             ALU.subtract, ALU.mult))
                link(nc.vector.scalar_tensor_tensor(m.K[:, j, :], m.TMP2[:, j, :], 1.0, m.K[:, j, :],
                                                    ALU.add, ALU.mult))
                nc.vector.scalar_tensor_tensor(m.TMP2[:, j, :], m.R[:, j, :], b.col("rw_r_k", j), m.K[:, j, :],
                                               ALU.mult, ALU.mult).then_inc(rk_ready, 1)
            dve.wait_ge(rk_ready, 4)
            nc.vector.tensor_tensor(flat(m.R), flat(m.R), flat(m.EP), ALU.mult).then_inc(r_decayed, 1)
            nc.vector.tensor_tensor(flat(m.K), flat(m.K), flat(m.EN), ALU.mult)
            evacuated(dve, at["kk", 3])
            link(nc.vector.tensor_tensor(flat(m.KK), flat(m.KK), flat(m.TMP), ALU.mult))
            nc.vector.scalar_tensor_tensor(flat(m.EA), flat(m.KK), -1.0, flat(m.EA), ALU.mult, ALU.mult)
            link(nc.vector.tensor_tensor(flat(m.A), flat(m.A), flat(m.KK), ALU.mult))
            nc.vector.tensor_tensor(flat(m.A), flat(m.A), flat(m.EN), ALU.mult)
            for j in range(4):
                dve.wait_ge(made, at["bonus", j] + 1)
                nc.vector.tensor_tensor(m.BON[:, j, :], b.bank[at["bonus", j] % 8][:, :], m.V[:, j, :],
                                        ALU.mult).then_inc(evac_dve, 1)


def rwkv_chunks(b, m):
    nc = b.nc
    w = m.w[:, :, :, :].rearrange("p a k n -> p (a k n)")

    def mats(i):
        return w[:, 8 * P * i:8 * P * (i + 1)].rearrange("p (h s) -> p h s", h=RW_H)

    MT, X, XT, PR, AkT, RbT, RkT = (mats(i) for i in range(7))
    Bs, SAs = w[:, 7 * 1024:7 * 1024 + 512], w[:, 7 * 1024 + 512:8 * 1024]
    Bt = m.hT[:, 0:4, :]
    Kt = m.hT[:, 4:8, :]
    Yt = m.Yt = m.TMP
    S = m.TMP2[:, 0, 0:256].rearrange("p (j v) -> p j v", j=4)
    SP = m.TMP2[:, 1, 0:256].rearrange("p (j v) -> p j v", j=4)
    NEW = m.TMP2[:, 2, 0:256].rearrange("p (j v) -> p j v", j=4)
    alpha, beta, k_, r_ = m.EA, m.A, m.K, m.R

    fills = [(name, g) for name in ("MT", "AkT", "RbT", "RkT", "X0") for g in range(2)] + doubling_fills()
    fills += [("B", 0), ("B", 1), ("SA", 0), ("Y", 0), ("Y", 1), ("dS", 0)]
    acts = [f for f in fills if f[0] in ("X0", "B", "SA", "Y")]
    dves = [f for f in fills if f not in acts]

    def bank_of(name, g):
        first = {"MT": 0, "AkT": 2, "RbT": 4, "RkT": 6, "X0": 2, "B": 6, "Y": 6, "SA": 0, "dS": 1}
        if name in first:
            return b.bank[first[name] + g]
        return b.bank[doubling_bank(name) + g]

    with nc.Block() as block:
        turned, turned_out = b.sem("rw_turned"), b.sem("rw_turned_out")
        filled, by_act, by_dve = b.sem("rw_filled"), b.sem("rw_by_act"), b.sem("rw_by_dve")
        first_x, state_ready = b.sem("rw_first_x"), b.sem("rw_state_ready")
        order = Order(fills, acts, dves, filled, by_act, by_dve)
        wait_filled, wait_taken = order.wait_filled, order.wait_taken

        @block.tensor
        def _(pe):
            for i in range(8):
                for c in range(NT):
                    src = (beta if i < 4 else k_)[:, i % 4, P * c:P * c + P]
                    last = nc.tensor.transpose(b.bank[i][:, P * c:P * c + P], src, b.ident[:, :])
                last.then_inc(turned, 1)
            pe.wait_ge(turned_out, 8)
            for c in range(NT):
                tok = slice(P * c, P * c + P)

                def fm(t, g, i):
                    return t[64 * g:64 * g + 64, i, tok]

                def vt(g, i):
                    h = 2 * i + g
                    return m.Vt[:, c, 64 * h:64 * h + 64]

                before = {"MT": (("SA", 0), ("dS", 0)), "AkT": (("X5", 0), ("X5", 1)),
                          "RbT": (("XT6", 0), ("XT6", 1)), "RkT": (("Y", 0), ("Y", 1))}
                for name, left, right in (("MT", beta, alpha), ("AkT", k_, alpha), ("RbT", beta, r_), ("RkT", k_, r_)):
                    if c:
                        for f in before[name]:
                            wait_taken(pe, c - 1, f)
                    for i in range(4):
                        for g in range(2):
                            last = nc.tensor.matmul(bank_of(name, g)[:, P * i:P * i + P], fm(left, g, i),
                                                    fm(right, g, i), start=True, stop=True)
                            if i == 3:
                                last.then_inc(filled, 1)
                for g in range(2):
                    pe.wait_ge(first_x, 2 * c + g + 1)
                    wait_taken(pe, c, ("AkT", g))
                    for i in range(4):
                        last = nc.tensor.transpose(bank_of("X0", g)[:, P * i:P * i + P], XT[:, 4 * g + i, :], b.ident[:, :])
                    last.then_inc(filled, 1)
                wait_taken(pe, c, ("RbT", 0))
                wait_taken(pe, c, ("RbT", 1))
                pe_doubling(nc, pe, order, c, bank_of, MT, X, XT, PR)
                pe.wait_ge(state_ready, c + 1)
                wait_taken(pe, c, ("RkT", 0))
                wait_taken(pe, c, ("RkT", 1))
                for i in range(4):
                    for g in range(2):
                        nc.tensor.matmul(bank_of("B", g)[:, 64 * i:64 * i + 64], fm(alpha, g, i),
                                         SP[64 * g:64 * g + 64, i, :], start=True, stop=False)
                    for g in range(2):
                        last = nc.tensor.matmul(bank_of("B", g)[:, 64 * i:64 * i + 64], AkT[:, 4 * g + i, :], vt(g, i),
                                                start=False, stop=True)
                        if i == 3:
                            last.then_inc(filled, 1)
                wait_taken(pe, c, ("P6", 0))
                wait_taken(pe, c, ("XT6", 1))
                for g in range(2):
                    wait_taken(pe, c, ("B", g))
                    for i in range(4):
                        at = 64 * (4 * g + i)
                        last = nc.tensor.matmul(bank_of("SA", 0)[:, at:at + 64], XT[:, 4 * g + i, :], Bs[:, at:at + 64],
                                                start=True, stop=True)
                last.then_inc(filled, 1)
                wait_taken(pe, c, ("SA", 0))
                for i in range(4):
                    for g in range(2):
                        nc.tensor.matmul(bank_of("Y", g)[:, 64 * i:64 * i + 64], fm(r_, g, i),
                                         SP[64 * g:64 * g + 64, i, :], start=True, stop=False)
                    for g in range(2):
                        o = bank_of("Y", g)[:, 64 * i:64 * i + 64]
                        at = 64 * (4 * g + i)
                        nc.tensor.matmul(o, RkT[:, 4 * g + i, :], vt(g, i), start=False, stop=False)
                        last = nc.tensor.matmul(o, RbT[:, 4 * g + i, :], SAs[:, at:at + 64], start=False, stop=True)
                        if i == 3:
                            last.then_inc(filled, 1)
                for i in range(4):
                    for g in range(2):
                        h = 2 * i + g
                        at = 64 * (4 * g + i)
                        o = bank_of("dS", 0)[64 * g:64 * g + 64, 64 * i:64 * i + 64]
                        nc.tensor.matmul(o, Kt[:, c, 64 * h:64 * h + 64], vt(g, i), start=True, stop=False)
                        last = nc.tensor.matmul(o, Bt[:, c, 64 * h:64 * h + 64], SAs[:, at:at + 64],
                                                start=False, stop=True)
                last.then_inc(filled, 1)

        @block.scalar
        def _(act):
            for i in range(1, 8, 2):
                act.wait_ge(turned, i + 1)
                nc.scalar.activation((Bt if i < 4 else Kt)[:, :, P * (i % 4):P * (i % 4) + P],
                                     b.bank[i][:, :].rearrange("p (c f) -> p c f", c=NT), ACT.Copy).then_inc(turned_out, 1)
            for c in range(NT):
                for f in acts:
                    name, g = f
                    wait_filled(act, c, f)
                    bank = bank_of(name, g)
                    if name == "X0":
                        dst, src = X[:, 4 * g:4 * g + 4, :].rearrange("p h s -> p (h s)"), bank[:, :]
                    elif name == "B":
                        dst, src = Bs[:, 256 * g:256 * g + 256], bank[:, 0:256]
                    elif name == "SA":
                        dst, src = SAs, bank[:, :]
                    else:
                        dst = Yt[:, c, :].rearrange("p (i g v) -> p g i v", g=2, v=64)[:, g, :, :]
                        src = bank[:, 0:256].rearrange("p (i v) -> p i v", v=64)
                    nc.scalar.activation(dst, src, ACT.Copy).then_inc(by_act, 1)

        @block.vector
        def _(dve):
            link = b.link(dve, "dve_steps")
            for i in range(0, 8, 2):
                dve.wait_ge(turned, i + 1)
                nc.vector.tensor_copy((Bt if i < 4 else Kt)[:, :, P * (i % 4):P * (i % 4) + P],
                                      b.bank[i][:, :].rearrange("p (c f) -> p c f", c=NT)).then_inc(turned_out, 1)
            link(nc.vector.memset(S, 0.0))
            nc.vector.memset(SP, 0.0).then_inc(state_ready, 1)

            def all_heads(mask):
                return mask.rearrange("p (o s) -> p o s", o=1).broadcast_to([P, 4, P])

            for c in range(NT):
                for f in dves:
                    name, g = f
                    bank = bank_of(name, g)
                    four = bank[:, :].rearrange("p (h s) -> p h s", h=4)
                    hs = slice(4 * g, 4 * g + 4)
                    wait_filled(dve, c, f)
                    if name == "dS":
                        link(nc.vector.tensor_tensor(NEW, bank[:, 0:256].rearrange("p (j v) -> p j v", j=4),
                                                     m.ELM[:, :, c:c + 1].broadcast_to([P, 4, 64]), ALU.mult))
                        link(nc.vector.tensor_tensor(S, S, m.EL[:, :, c:c + 1].broadcast_to([P, 4, 64]), ALU.mult))
                        nc.vector.tensor_tensor(S, S, NEW, ALU.add).then_inc(by_dve, 1)
                        if c + 1 < NT:
                            wait_taken(dve, c, f)
                            nc.vector.tensor_tensor(SP, S, m.EM[:, :, c + 1:c + 2].broadcast_to([P, 4, 64]),
                                                    ALU.mult).then_inc(state_ready, 1)
                        continue
                    if name in ("MT", "AkT"):
                        ins = nc.vector.tensor_tensor((MT if name == "MT" else AkT)[:, hs, :], four,
                                                      all_heads(b.before[:, :]), ALU.mult)
                    elif name in ("RbT", "RkT"):
                        ins = nc.vector.tensor_tensor((RbT if name == "RbT" else RkT)[:, hs, :], four,
                                                      all_heads(b.causal[:, :]), ALU.mult)
                    else:
                        ins = take_doubling(nc, b, name, g, four, X, XT, PR)
                    ins.then_inc(by_dve, 1)
                    if name == "MT":
                        wait_taken(dve, c, f)
                        first_inverse(nc, b, link, MT[:, hs, :], XT[:, hs, :]).then_inc(first_x, 1)


def rwkv_out(b, m):
    nc = b.nc
    Yt, YA = m.Yt, m.KK
    m.YA = YA
    mean = m.TMP2[:, 0, 0:32]
    var = m.TMP2[:, 1, 0:32]
    y3 = flat(Yt).rearrange("p (g v) -> p g v", v=64)
    sq = m.EN
    with nc.Block() as block:
        centred, squared, var_in, var_out = (b.sem(f"rwo_{x}") for x in ("centred", "squared", "var_in", "var_out"))
        normed, turned = b.sem("rwo_normed"), b.sem("rwo_turned")

        @block.vector
        def _(dve):
            link = b.link(dve, "dve_steps")
            link(nc.vector.reduce_sum(mean, y3, AX.X))
            link(nc.vector.tensor_scalar(mean, mean, 1.0 / 64, None, ALU.mult))
            nc.vector.tensor_tensor(y3, y3, mean.rearrange("p (g o) -> p g o", o=1).broadcast_to([P, 32, 64]),
                                    ALU.subtract).then_inc(centred, 1)
            dve.wait_ge(squared, 1)
            link(nc.vector.reduce_sum(var, flat(sq).rearrange("p (g v) -> p g v", v=64), AX.X))
            nc.vector.tensor_scalar(var, var, 1.0 / 64, RW_LN_EPS, ALU.mult, ALU.add).then_inc(var_in, 1)
            dve.wait_ge(var_out, 1)
            link(nc.vector.reciprocal(var, var))
            nc.vector.tensor_tensor(y3, y3, var.rearrange("p (g o) -> p g o", o=1).broadcast_to([P, 32, 64]),
                                    ALU.mult).then_inc(normed, 1)
            for j in range(4):
                dve.wait_ge(turned, j + 1)
                link(nc.vector.tensor_scalar(YA[:, j, :], b.bank[j][:, :], b.col("rw_ln_w", j), b.col("rw_ln_b", j),
                                             ALU.mult, ALU.add))
                link(nc.vector.tensor_tensor(YA[:, j, :], YA[:, j, :], m.BON[:, j, :], ALU.add))
                nc.vector.tensor_tensor(YA[:, j, :], YA[:, j, :], m.G[:, j, :], ALU.mult)

        @block.scalar
        def _(act):
            act.wait_ge(centred, 1)
            nc.scalar.activation(flat(sq), flat(Yt), ACT.Square).then_inc(squared, 1)
            act.wait_ge(var_in, 1)
            nc.scalar.activation(var, var, ACT.Sqrt).then_inc(var_out, 1)

        @block.tensor
        def _(pe):
            pe.wait_ge(normed, 1)
            for j in range(4):
                for c in range(NT):
                    last = nc.tensor.transpose(b.bank[j][:, P * c:P * c + P], Yt[:, c, P * j:P * j + P], b.ident[:, :])
                last.then_inc(turned, 1)


EXP_TOP = 80.0


def hgrn(b, m):
    nc, d = b.nc, b.dram
    w_out = d["ev_w_out"][0].rearrange("(k p) n -> p k n", p=P)
    KH, LF, CB, DIF = m.K, m.R, m.TMP, m.EN
    QD, KD, S32, S64, QE, KE = m.A, m.EA, m.TMP2, m.EP, m.DEC, m.V
    KEt = m.hT[:, 0:4, :]
    AT = m.hT[:, 4:8, :].rearrange("p (two a) (i s) -> p two (a i) s", two=2, s=P)
    S = m.WA[:, 0:256].rearrange("p (i v) -> p i v", i=4)
    Ot = m.G
    m.YB = m.F
    EL = m.EL
    sq, ss = m.A, m.stat[:, :]

    def block_view(t, n, size):
        return flat(t).rearrange("p (n s) -> p n s", s=size)

    with nc.Block() as block:
        bound_in, bound, logs_in, logs = (b.sem(f"hg_{x}") for x in ("bound_in", "bound", "logs_in", "logs"))
        exponent, exped, q_ready, ke_ready = (b.sem(f"hg_{x}") for x in ("exponent", "exped", "q_ready", "ke_ready"))
        turned, turned_out, zeroed = (b.sem(f"hg_{x}") for x in ("turned", "turned_out", "zeroed"))
        at_made, at_taken, o_made, o_taken = (b.sem(f"hg_{x}") for x in ("at_made", "at_taken", "o_made", "o_taken"))
        ds_made, state = b.sem("hg_ds_made"), b.sem("hg_state")
        squared, var_in, var_out, normed, y_turned = (b.sem(f"hg_{x}") for x in ("sq", "var_in", "var_out", "normed", "yt"))
        w_out_in = b.sem("even_w_out_in")

        @block.sync
        def _(sp):
            for i in range(2):
                sp.dma_start(m.w[:, i, :, :], w_out[:, :, 512 * i:512 * i + 512]).then_inc(w_out_in, 16)

        @block.scalar
        def _(act):
            act.wait_ge(bound_in, 1)
            nc.scalar.activation(m.lb[:, :], m.lb[:, :], ACT.Sigmoid).then_inc(bound, 1)
            act.wait_ge(logs_in, 1)
            nc.scalar.activation(flat(LF), flat(m.F), ACT.Ln).then_inc(logs, 1)
            act.wait_ge(exponent, 1)
            nc.scalar.activation(flat(QD), flat(QD), ACT.Exp).then_inc(exped, 1)
            act.wait_ge(exponent, 2)
            nc.scalar.activation(flat(KD), flat(KD), ACT.Exp).then_inc(exped, 1)
            for n, (t, size) in enumerate(((S32, 64), (S64, 128))):
                act.wait_ge(exponent, 3 + n)
                v = block_view(t, None, size)
                nc.scalar.activation(v[:, :, 0:size // 2], v[:, :, 0:size // 2], ACT.Exp, scale=-1.0).then_inc(exped, 1)
                nc.scalar.activation(v[:, :, size // 2:size], v[:, :, size // 2:size], ACT.Exp).then_inc(exped, 1)
            nc.scalar.activation(flat(QE), flat(CB), ACT.Exp).then_inc(exped, 1)
            act.wait_ge(exponent, 5)
            nc.scalar.activation(flat(KE), flat(KE), ACT.Exp, scale=-1.0).then_inc(exped, 1)
            nc.scalar.activation(EL[:, :, :], chunks(CB)[:, :, :, 127], ACT.Exp).then_inc(exped, 1)
            for j in range(4):
                act.wait_ge(turned, j + 1)
                nc.scalar.activation(KEt[:, :, P * j:P * j + P], b.bank[6 + j % 2][:, :].rearrange("p (c f) -> p c f", c=NT),
                                     ACT.Copy).then_inc(turned_out, 1)
            for c in range(NT):
                for g in range(2):
                    act.wait_ge(o_made, 2 * c + g + 1)
                    nc.scalar.activation(Ot[:, c, :].rearrange("p (i g v) -> p g i v", g=2, v=64)[:, g, :, :],
                                         b.bank[4 + g][:, 0:256].rearrange("p (i v) -> p i v", v=64),
                                         ACT.Copy).then_inc(o_taken, 1)
            act.wait_ge(o_taken, 2 * NT)
            nc.scalar.activation(flat(sq), flat(Ot), ACT.Square).then_inc(squared, 1)
            act.wait_ge(var_in, 1)
            nc.scalar.activation(ss, ss, ACT.Sqrt).then_inc(var_out, 1)

        @block.vector
        def _(dve):
            link = b.link(dve, "dve_steps")
            for i in range(4):
                last = nc.vector.memset(b.bank[i][:, :], 0.0)
            last.then_inc(zeroed, 1)
            nc.vector.memset(S, 0.0).then_inc(state, 1)
            at = PAR_AT["hg_lb_logits"]
            nc.vector.tensor_tensor(m.lb[:, :], b.par[:, at:at + 4], b.par[:, at + 4:at + 8], ALU.subtract).then_inc(bound_in, 1)
            dve.wait_ge(bound, 1)
            link(nc.vector.tensor_scalar(m.oml[:, :], m.lb[:, :], -1.0, 1.0, ALU.mult, ALU.add))
            for j in range(4):
                last = nc.vector.tensor_scalar(m.F[:, j, :], m.F[:, j, :], m.oml[:, j:j + 1], m.lb[:, j:j + 1],
                                               ALU.mult, ALU.add)
            last.then_inc(logs_in, 1)
            dve.wait_ge(logs_in, 1)
            nc.vector.tensor_scalar(flat(KH), flat(m.F), -1.0, 1.0, ALU.mult, ALU.add)
            dve.wait_ge(logs, 1)
            for j in range(4):
                for c in range(NT):
                    last = nc.vector.tensor_tensor_scan(CB[:, j, P * c:P * c + P], b.ones[:, :],
                                                        LF[:, j, P * c:P * c + P], 0.0, ALU.mult, ALU.add)
            link(last)

            def minus_at(dst, size, place):
                v = block_view(CB, None, size)
                n = 4 * T // size
                return nc.vector.tensor_tensor(block_view(dst, None, size), v,
                                               v[:, :, place:place + 1].broadcast_to([P, n, size]), ALU.subtract)

            link(minus_at(DIF, 32, 15))
            nc.vector.tensor_scalar(flat(QD), flat(DIF), EXP_TOP, None, ALU.min).then_inc(exponent, 1)
            nc.vector.tensor_scalar(flat(KD), flat(DIF), -1.0, EXP_TOP, ALU.mult, ALU.min).then_inc(exponent, 1)
            minus_at(S32, 64, 31).then_inc(exponent, 1)
            minus_at(S64, 128, 63).then_inc(exponent, 1)
            minus_at(KE, 128, 127).then_inc(exponent, 1)
            dve.wait_ge(exped, 1)
            nc.vector.tensor_tensor(flat(QD), flat(QD), flat(m.Q), ALU.mult)
            dve.wait_ge(exped, 2)
            nc.vector.tensor_tensor(flat(KD), flat(KD), flat(KH), ALU.mult)
            for n, (t, size) in enumerate(((S32, 64), (S64, 128))):
                v, q, k = block_view(t, None, size), block_view(m.Q, None, size), block_view(KH, None, size)
                dve.wait_ge(exped, 3 + 2 * n)
                nc.vector.tensor_tensor(v[:, :, 0:size // 2], v[:, :, 0:size // 2], k[:, :, 0:size // 2], ALU.mult)
                dve.wait_ge(exped, 4 + 2 * n)
                nc.vector.tensor_tensor(v[:, :, size // 2:], v[:, :, size // 2:], q[:, :, size // 2:],
                                        ALU.mult).then_inc(q_ready, 1)
            dve.wait_ge(exped, 7)
            nc.vector.tensor_tensor(flat(QE), flat(QE), flat(m.Q), ALU.mult)
            dve.wait_ge(exped, 8)
            nc.vector.tensor_tensor(flat(KE), flat(KE), flat(KH), ALU.mult).then_inc(ke_ready, 1)
            dve.wait_ge(exped, 9)
            mask = b.causal[:, :].rearrange("p (o s) -> p o s", o=1).broadcast_to([P, 4, P])

            def take_weights(c):
                for g in range(2):
                    dve.wait_ge(at_made, c + 1)
                    if c >= 2:
                        dve.wait_ge(ds_made, c - 1)
                    nc.vector.tensor_tensor(AT[:, c % 2, 4 * g:4 * g + 4, :],
                                            b.bank[2 * (c % 2) + g][:, :].rearrange("p (i s) -> p i s", i=4), mask,
                                            ALU.mult).then_inc(at_taken, 1)

            take_weights(0)
            for c in range(NT):
                if c + 1 < NT:
                    take_weights(c + 1)
                dve.wait_ge(ds_made, c + 1)
                link(nc.vector.tensor_tensor(S, S, EL[:, :, c:c + 1].broadcast_to([P, 4, 64]), ALU.mult))
                nc.vector.tensor_tensor(S, S, b.bank[6][:, 0:256].rearrange("p (i v) -> p i v", i=4),
                                        ALU.add).then_inc(state, 1)
                dve.wait_ge(state, c + 2)
            dve.wait_ge(squared, 1)
            ss32 = ss.rearrange("p (g o) -> p g o", o=1)
            link(nc.vector.reduce_sum(ss, flat(sq).rearrange("p (g v) -> p g v", v=64), AX.X))
            nc.vector.tensor_scalar(ss, ss, 1.0 / 64, NORM_EPS, ALU.mult, ALU.add).then_inc(var_in, 1)
            dve.wait_ge(var_out, 1)
            link(nc.vector.reciprocal(ss, ss))
            o3 = flat(Ot).rearrange("p (g v) -> p g v", v=64)
            nc.vector.tensor_tensor(o3, o3, ss32.broadcast_to([P, 32, 64]), ALU.mult).then_inc(normed, 1)
            for j in range(4):
                dve.wait_ge(y_turned, j + 1)
                nc.vector.scalar_tensor_tensor(m.YB[:, j, :], b.bank[j][:, :], b.col("hg_norm"), m.GG[:, j, :],
                                               ALU.mult, ALU.mult)

        @block.tensor
        def _(pe):
            pe.wait_ge(ke_ready, 1)
            for j in range(4):
                if j >= 2:
                    pe.wait_ge(turned_out, j - 1)
                for c in range(NT):
                    last = nc.tensor.transpose(b.bank[6 + j % 2][:, P * c:P * c + P], KE[:, j, P * c:P * c + P], b.ident[:, :])
                last.then_inc(turned, 1)

            def weights(c):
                if c >= 2:
                    pe.wait_ge(at_taken, 2 * (c - 1))
                banks = [b.bank[2 * (c % 2) + g] for g in range(2)]

                def square(t_left, t_right, i, g, s0, t0, size):
                    rows = slice(64 * g, 64 * g + 64)
                    return nc.tensor.matmul(banks[g][s0:s0 + size, P * i + t0:P * i + t0 + size],
                                            t_left[rows, i, P * c + s0:P * c + s0 + size],
                                            t_right[rows, i, P * c + t0:P * c + t0 + size], start=True, stop=True)

                for i in range(4):
                    for g in range(2):
                        for s0 in range(0, P, 32):
                            square(KD, QD, i, g, s0, s0, 32)
                        for s0 in (0, 64):
                            square(S32, S32, i, g, s0, s0 + 32, 32)
                for i in range(4):
                    for g in range(2):
                        last = square(S64, S64, i, g, 0, 64, 64)
                last.then_inc(at_made, 1)

            pe.wait_ge(zeroed, 1)
            weights(0)
            pe.wait_ge(turned_out, 4)
            for c in range(NT):
                if c + 1 < NT:
                    weights(c + 1)
                pe.wait_ge(at_taken, 2 * c + 2)
                pe.wait_ge(state, c + 1)
                if c:
                    pe.wait_ge(o_taken, 2 * c)
                for i in range(4):
                    for g in range(2):
                        nc.tensor.matmul(b.bank[4 + g][:, 64 * i:64 * i + 64], QE[64 * g:64 * g + 64, i, P * c:P * c + P],
                                         S[64 * g:64 * g + 64, i, :], start=True, stop=False)
                    for g in range(2):
                        h = 2 * i + g
                        last = nc.tensor.matmul(b.bank[4 + g][:, 64 * i:64 * i + 64], AT[:, c % 2, 4 * g + i, :],
                                                m.I[:, c, 64 * h:64 * h + 64], start=False, stop=True)
                        if i == 3:
                            last.then_inc(o_made, 1)
                for i in range(4):
                    for g in range(2):
                        h = 2 * i + g
                        last = nc.tensor.matmul(b.bank[6][64 * g:64 * g + 64, 64 * i:64 * i + 64],
                                                KEt[:, c, 64 * h:64 * h + 64], m.I[:, c, 64 * h:64 * h + 64],
                                                start=True, stop=True)
                last.then_inc(ds_made, 1)
            pe.wait_ge(normed, 1)
            for j in range(4):
                for c in range(NT):
                    last = nc.tensor.transpose(b.bank[j][:, P * c:P * c + P], Ot[:, c, P * j:P * j + P], b.ident[:, :])
                last.then_inc(y_turned, 1)


def project_out(b, tag, w, w_in, y):
    nc = b.nc
    with nc.Block() as block:
        made = b.sem(f"out_made_{tag}")

        @block.tensor
        def _(pe):
            pe.wait_ge(w_in, 32)
            for n in range(2):
                for i in range(NT):
                    for k in range(KD):
                        last = nc.tensor.matmul(b.bank[4 * n + i][:, :], y(k)[:, P * i:P * i + P], w[:, n, k, :],
                                                start=(k == 0), stop=(k == KD - 1))
                    last.then_inc(made, 1)

        @block.vector
        def _(dve):
            for n in range(2):
                for i in range(NT):
                    dve.wait_ge(made, 4 * n + i + 1)
                    part = b.h[:, i, 512 * n:512 * n + 512]
                    nc.vector.tensor_tensor(part, part, b.bank[4 * n + i][:, :], ALU.add)


def even_layer(b):
    with ExitStack() as ctx:
        m = Even(b, ctx)
        norm_into(b, "mix0", PAR_AT["norm_mix"], m.xn, flat(m.TMP)[:, 0:D], m.hT)
        even_project(b, m)
        rwkv_chunks(b, m)
        rwkv_out(b, m)
        hgrn(b, m)
        project_out(b, "even", m.w, b.sem("even_w_out_in"), lambda k: (m.YA if k < 4 else m.YB)[:, k % 4, :])


NW = 4 + E


def moe(b, layer):
    nc, d = b.nc, b.dram
    tag = f"moe{layer}"
    sem = lambda name: b.sem(f"{tag}_{name}")
    with ExitStack() as ctx:
        def sb(name, *shape, dt=F32):
            return b.sb(ctx, f"{tag}_{name}", [P, *shape], dt)

        xn, hT = sb("xn", NT, D), sb("hT", KD, T)
        w_gate, w_up, w_down = sb("w_gate", 2, KD, DE), sb("w_up", 2, KD, DE), sb("w_down", 2, 2, D)
        xs = sb("xs", KD, SLOTS + WIN)
        ys = sb("ys", KD, SLOTS + WIN)
        hot = sb("hot", NT, SLOTS)
        gates_T = w_gate[:, :, :, :].rearrange("p s k f -> p (s k f)").rearrange("p (n t) -> p n t", n=2 * NT)
        router, bias = sb("router", KD, NW), sb("bias", NW)
        slot_ids, ids_int = sb("slot_ids", SLOTS), hot[:, 0, :].bitcast(I32)
        logits, fine, key = sb("logits", NT, NW), sb("fine", NT, E), sb("key", NT, E)
        one1, one2, both = sb("one1", NT, E), sb("one2", NT, E), sb("both", NT, E)
        rev = sb("rev", E)
        gmax, gsum, gone, best1, best2 = (sb(n, NT) for n in ("gmax", "gsum", "gone", "best1", "best2"))
        gexp, grp = sb("gexp", NT, GROUPS), sb("grp", NT, GROUPS)
        e2, gate1, gate2, slot1, slot2, kmax = (sb(n, NT) for n in ("e2", "gate1", "gate2", "slot1", "slot2", "kmax"))
        count, incl, off = sb("count", E), sb("incl", E), sb("off", E)
        edges, over = sb("edges", 8), sb("over", E, 8)
        table_f, table = sb("table_f", 4 * E), sb("table", 4 * E, dt=I32)
        OFF, CNT, BASE = 0, E, 2 * E
        silu, hid, xw = sb("silu", 2, WIN), sb("hid", 2, WIN), sb("xw", KD, WIN)

        norm_into(b, tag, PAR_AT["norm_ffn"] + 8 * layer, xn, ys[:, 0, 0:D], hT)
        gain = lambda k: b.par[:, PAR_AT["norm_ffn"] + 8 * layer + k:PAR_AT["norm_ffn"] + 8 * layer + k + 1]

        def weights_of(e):
            return (d["moe_w_gate"][layer, e].rearrange("(p k) f -> p k f", k=KD),
                    d["moe_w_up"][layer, e].rearrange("(p k) f -> p k f", k=KD),
                    d["moe_w_down"][layer, e].rearrange("(j p) n -> p j n", p=P))

        places = (w_gate, w_up, w_down)
        arrived = [[sem(f"{n}{s}_in") for n in ("gate", "up", "down")] for s in range(2)]
        with nc.Block() as block:
            router_in, ids, scored, exps, r_ready, ranked = (sem(n) for n in ("router_in", "ids", "scored", "exps", "r_ready", "ranked"))
            chosen, hot_ready, gathered, taken_a, taken_v, e1 = (sem(n) for n in ("chosen", "hot_ready", "gathered", "taken_a", "taken_v", "e1"))

            @block.sync
            def _(sp):
                sp.dma_start(router[:, :, 0:4], d["moe_w_group"][layer].rearrange("(p k) n -> p k n", k=KD)).then_inc(router_in, 16)
                sp.dma_start(router[:, :, 4:NW], d["moe_w_router"][layer].rearrange("(p k) n -> p k n", k=KD)).then_inc(router_in, 16)
                for n, name, c, width in ((0, "moe_b_group", 0, 4), (1, "moe_b_router", 4, E)):
                    sp.dma_start(bias[:, c:c + width],
                                 d[name][layer].rearrange("(o n) -> o n", o=1).broadcast_to([P, width])).then_inc(router_in, 16)
                for s in range(2):
                    for part, src in enumerate(weights_of(s)):
                        sp.dma_start(places[part][:, s], src).then_inc(arrived[s][part], 16)

            @block.gpsimd
            def _(pool):
                link = b.link(pool, "pool_steps")
                nc.gpsimd.iota(ids_int, [[1, SLOTS]], base=0, channel_multiplier=0).then_inc(ids, 1)
                nc.gpsimd.iota(key[:, 0, :].bitcast(I32), [[-1, E]], base=E, channel_multiplier=0).then_inc(ids, 1)
                nc.gpsimd.iota(key[:, 1, 0:8].bitcast(I32), [[WIN, 8]], base=0, channel_multiplier=0).then_inc(ids, 1)
                nc.gpsimd.memset(xs[:, :, SLOTS:], 0.0).then_inc(ids, 1)

            @block.tensor
            def _(pe):
                pe.wait_ge(router_in, 64)
                for i in range(NT):
                    for k in range(KD):
                        last = nc.tensor.matmul(b.bank[0][:, NW * i:NW * i + NW], hT[:, k, P * i:P * i + P], router[:, k, :],
                                                start=(k == 0), stop=(k == KD - 1))
                last.then_inc(scored, 1)
                pe.wait_ge(chosen, 1)
                for i in range(NT):
                    for n in range(i + 1):
                        nc.tensor.matmul(b.bank[1][:, E * i:E * i + E], (b.before if n == i else b.ones)[:, :], both[:, n, :],
                                         start=(n == 0), stop=(n == i))
                for n in range(NT):
                    last = nc.tensor.matmul(b.bank[1][:, E * NT:E * NT + E], b.ones[:, :], both[:, n, :],
                                            start=(n == 0), stop=(n == NT - 1))
                last.then_inc(ranked, 1)
                pe.wait_ge(hot_ready, 1)
                for k in range(KD):
                    for half in range(2):
                        n = 2 * k + half
                        if n >= 6:
                            pe.wait_ge((taken_a, taken_v)[n % 2], (n - 6) // 2 + 1)
                        for i in range(NT):
                            last = nc.tensor.matmul(b.bank[2 + n % 6], xn[:, i, :].rearrange("p (q k) -> p k q", k=KD)[:, k, :],
                                                    hot[:, i, 512 * half:512 * half + 512], start=(i == 0), stop=(i == NT - 1))
                        last.then_inc(gathered, 1)

            @block.scalar
            def _(act):
                act.wait_ge(e1, 1)
                nc.scalar.activation(gexp[:, :, :], gexp[:, :, :], ACT.Exp).then_inc(exps, 1)
                act.wait_ge(e1, 2)
                nc.scalar.activation(e2[:, :], e2[:, :], ACT.Exp).then_inc(exps, 1)
                for n in range(0, 16, 2):
                    act.wait_ge(gathered, n + 1)
                    nc.scalar.activation(xs[:, n // 2, 0:512], b.bank[2 + n % 6], ACT.Copy, scale=gain(n // 2)).then_inc(taken_a, 1)

            @block.vector
            def _(dve):
                link = b.link(dve, "dve_steps")
                V = nc.vector

                def spread(t, n):
                    return t[:, :].rearrange("p (i o) -> p i o", o=1).broadcast_to([P, NT, n])

                def over_tiles(t, n):
                    return t.rearrange("p (o e) -> p o e", o=1).broadcast_to([P, NT, n])

                dve.wait_ge(ids, 4)
                V.tensor_copy(slot_ids[:, :], ids_int)
                V.tensor_copy(rev[:, :], key[:, 0, :].bitcast(I32))
                link(V.tensor_copy(edges[:, :], key[:, 1, 0:8].bitcast(I32)))
                link(V.tensor_scalar(edges[:, 0:1], edges[:, 0:1], 1.0, None, ALU.subtract))
                dve.wait_ge(scored, 1)
                link(V.tensor_tensor(logits[:, :, :], b.bank[0][:, 0:NT * NW].rearrange("p (i n) -> p i n", i=NT),
                                     over_tiles(bias[:, :], NW), ALU.add))
                groups = logits[:, :, 0:GROUPS]
                link(V.reduce_max(gmax[:, :], groups, AX.X))
                V.tensor_tensor(gexp[:, :, :], groups, spread(gmax, GROUPS), ALU.subtract).then_inc(e1, 1)

                def first_of_largest(dst, values, largest, keys, n):
                    link(V.tensor_tensor(keys, values, spread(largest, n), ALU.is_equal))
                    link(V.tensor_tensor(keys, keys, over_tiles(rev[:, 0:n], n), ALU.mult))
                    link(V.reduce_max(kmax[:, :], keys, AX.X))
                    link(V.tensor_tensor(dst, keys, spread(kmax, n), ALU.is_equal))

                first_of_largest(grp[:, :, :], groups, gmax, key[:, :, 0:GROUPS], GROUPS)
                link(V.tensor_scalar(grp[:, :, :], grp[:, :, :], 1.0, BIG, ALU.subtract, ALU.mult))
                link(V.tensor_tensor(fine[:, :, :].rearrange("p i (g e) -> p i g e", g=GROUPS),
                                     logits[:, :, GROUPS:NW].rearrange("p i (g e) -> p i g e", g=GROUPS),
                                     grp[:, :, :].rearrange("p i (g o) -> p i g o", o=1).broadcast_to([P, NT, GROUPS, EPG]),
                                     ALU.add))
                link(V.reduce_max(best1[:, :], fine[:, :, :], AX.X))
                first_of_largest(one1[:, :, :], fine[:, :, :], best1, key[:, :, :], E)
                link(V.scalar_tensor_tensor(fine[:, :, :], one1[:, :, :], -2.0 * BIG, fine[:, :, :], ALU.mult, ALU.add))
                link(V.reduce_max(best2[:, :], fine[:, :, :], AX.X))
                V.tensor_tensor(e2[:, :], best2[:, :], best1[:, :], ALU.subtract).then_inc(e1, 1)
                first_of_largest(one2[:, :, :], fine[:, :, :], best2, key[:, :, :], E)
                V.tensor_tensor(both[:, :, :], one1[:, :, :], one2[:, :, :], ALU.add).then_inc(chosen, 1)
                dve.wait_ge(exps, 2)
                link(V.reduce_sum(gsum[:, :], gexp[:, :, :], AX.X))
                link(V.tensor_scalar(gone[:, :], e2[:, :], 1.0, None, ALU.add))
                link(V.tensor_tensor(gone[:, :], gone[:, :], gsum[:, :], ALU.mult))
                link(V.reciprocal(gate1[:, :], gone[:, :]))
                link(V.tensor_tensor(gate2[:, :], gate1[:, :], e2[:, :], ALU.mult))
                dve.wait_ge(ranked, 1)
                link(V.tensor_copy(count[:, :], b.bank[1][:, E * NT:E * NT + E]))
                link(V.tensor_tensor_scan(incl[:, :], b.ones[:, 0:E], count[:, :], 0.0, ALU.mult, ALU.add))
                link(V.tensor_tensor(off[:, :], incl[:, :], count[:, :], ALU.subtract))
                link(V.tensor_tensor(fine[:, :, :], b.bank[1][:, 0:E * NT].rearrange("p (i e) -> p i e", i=NT),
                                     over_tiles(off[:, :], E), ALU.add))
                for one, slot in ((one1, slot1), (one2, slot2)):
                    link(V.tensor_tensor(key[:, :, :], one[:, :, :], fine[:, :, :], ALU.mult))
                    link(V.reduce_sum(slot[:, :], key[:, :, :], AX.X))
                for i in range(NT):
                    link(V.tensor_scalar(hot[:, i, :], slot_ids[:, :], slot1[:, i:i + 1], None, ALU.is_equal))
                    last = V.scalar_tensor_tensor(hot[:, i, :], slot_ids[:, :], slot2[:, i:i + 1], hot[:, i, :],
                                                  ALU.is_equal, ALU.add)
                last.then_inc(hot_ready, 1)
                V.tensor_copy(table_f[:, OFF:OFF + E], off[:, :])
                link(V.tensor_tensor(over[:, :, :], count[:, :].rearrange("p (e o) -> p e o", o=1).broadcast_to([P, E, 8]),
                                     edges[:, :].rearrange("p (o j) -> p o j", o=1).broadcast_to([P, E, 8]), ALU.is_gt))
                link(V.reduce_sum(table_f[:, CNT:CNT + E], over[:, :, :], AX.X))
                link(V.tensor_tensor_scan(incl[:, :], b.ones[:, 0:E], table_f[:, CNT:CNT + E], 0.0, ALU.mult, ALU.add))
                link(V.tensor_tensor(table_f[:, BASE:BASE + E], incl[:, :], table_f[:, CNT:CNT + E], ALU.subtract))
                V.tensor_copy(table[:, 0:3 * E], table_f[:, 0:3 * E])
                for n in range(1, 16, 2):
                    dve.wait_ge(gathered, n + 1)
                    V.tensor_scalar(xs[:, n // 2, 512:1024], b.bank[2 + n % 6], gain(n // 2), None, ALU.mult).then_inc(taken_v, 1)

        with nc.Block() as block:
            xw_ready, gu_made, silu_ready, hid_ready, y_made, y_taken = (
                sem(n) for n in ("xw_ready", "gu_made", "silu_ready", "hid_ready", "y_made", "y_taken"))

            def look_up(eng, at, e, low, high):
                return eng.value_load(table[0:1, bass.ds(at + e, 1)], min_val=low, max_val=high)

            @block.sync
            def _(sp):
                with sp.Fori(1, E // 2) as i:
                    for s in range(2):
                        used = look_up(sp, BASE, 2 * i + (s - 1), 1, E * 8)
                        src = weights_of(2 * i + s)
                        sp.wait_ge(gu_made, used + 1)
                        sp.dma_start(w_gate[:, s], src[0]).then_inc(arrived[s][0], 16)
                        sp.dma_start(w_up[:, s], src[1]).then_inc(arrived[s][1], 16)
                        sp.wait_ge(y_made, used)
                        sp.dma_start(w_down[:, s], src[2]).then_inc(arrived[s][2], 16)

            @block.gpsimd
            def _(pool):
                with pool.Fori(0, E) as e:
                    first, base = look_up(pool, OFF, e, 0, SLOTS), look_up(pool, BASE, e, 0, E * 8)
                    count_ = look_up(pool, CNT, e, 1, 8)
                    with pool.Fori(0, count_) as n:
                        pool.wait_ge(gu_made, base + n + 1)
                        at = nc.s_assert_within(first + n * WIN, 0, SLOTS, skip_runtime_bounds_check_because=
                                                "a window starts before its expert's last slot or is its first")
                        nc.gpsimd.tensor_copy(xw[:, :, :], xs[:, :, bass.ds(at, WIN)]).then_inc(xw_ready, 1)

            @block.tensor
            def _(pe):
                pe.sem_inc(gu_made, 1)
                with pe.Fori(0, E // 2) as i:
                    for s in range(2):
                        base, count_ = look_up(pe, BASE, 2 * i + s, 0, E * 8), look_up(pe, CNT, 2 * i + s, 1, 8)
                        arrival = pe.snap(16 * i + 16)
                        with pe.Fori(0, count_) as n:
                            here = pe.snap(base + n + 1)
                            pe.wait_ge(arrived[s][0], arrival)
                            pe.wait_ge(arrived[s][1], arrival)
                            pe.wait_ge(xw_ready, here)
                            for q, (w, f) in enumerate(((w_gate, 0), (w_gate, 1), (w_up, 0), (w_up, 1))):
                                for k in range(KD):
                                    last = nc.tensor.matmul(b.bank[q][:, 0:WIN], w[:, s, k, P * f:P * f + P], xw[:, k, :],
                                                            start=(k == 0), stop=(k == KD - 1))
                            last.then_inc(gu_made, 1)
                            pe.wait_ge(arrived[s][2], arrival)
                            pe.wait_ge(y_taken, here)
                            pe.wait_ge(hid_ready, here)
                            for k in range(KD):
                                for f in range(2):
                                    last = nc.tensor.matmul(b.bank[4][:, WIN * k:WIN * k + WIN], w_down[:, s, f, P * k:P * k + P],
                                                            hid[:, f, :], start=(f == 0), stop=(f == 1))
                            last.then_inc(y_made, 1)

            @block.scalar
            def _(act):
                act.sem_inc(y_taken, 1)
                with act.Fori(0, E) as e:
                    first, base = look_up(act, OFF, e, 0, SLOTS), look_up(act, BASE, e, 0, E * 8)
                    count_ = look_up(act, CNT, e, 1, 8)
                    with act.Fori(0, count_) as n:
                        act.wait_ge(gu_made, base + n + 2)
                        nc.scalar.activation(silu[:, :, :], b.psum[:, 0:2, 0:WIN], ACT.Silu).then_inc(silu_ready, 1)
                        act.wait_ge(y_made, base + n + 1)
                        act.wait_ge(y_taken, base + n + 1)
                        at = nc.s_assert_within(first + n * WIN, 0, SLOTS, skip_runtime_bounds_check_because=
                                                "a window starts before its expert's last slot or is its first")
                        nc.scalar.activation(ys[:, :, bass.ds(at, WIN)],
                                             b.bank[4].rearrange("p (k s) -> p k s", k=KD), ACT.Copy).then_inc(y_taken, 1)

            @block.vector
            def _(dve):
                with dve.Fori(0, E) as e:
                    base, count_ = look_up(dve, BASE, e, 0, E * 8), look_up(dve, CNT, e, 1, 8)
                    with dve.Fori(0, count_) as n:
                        dve.wait_ge(silu_ready, base + n + 1)
                        nc.vector.tensor_tensor(hid[:, :, :], silu[:, :, :], b.psum[:, 2:4, 0:WIN], ALU.mult).then_inc(hid_ready, 1)

        slots = xs[:, :, 0:SLOTS]
        with nc.Block() as block:
            turned, turned_a, turned_v = sem("turned"), sem("turned_a"), sem("turned_v")
            gates, gates_turned, gates_out, made = sem("gates"), sem("gates_turned"), sem("gates_out"), sem("made")
            @block.tensor
            def _(pe):
                for n in range(16):
                    if n >= 8:
                        pe.wait_ge((turned_a, turned_v)[n % 2], (n - 8) // 2 + 1)
                    for q in range(4):
                        k = 4 * (n % 2) + q
                        last = nc.tensor.transpose(b.bank[n % 8][:, P * q:P * q + P], ys[:, k, P * (n // 2):P * (n // 2) + P],
                                                   b.ident[:, :])
                    last.then_inc(turned, 1)
                for n in range(8):
                    pe.wait_ge(gates, 1)
                    pe.wait_ge((turned_a, turned_v)[n % 2], 4 + n // 2 + 1)
                    for i in range(NT):
                        last = nc.tensor.transpose(b.bank[n][:, P * i:P * i + P], hot[:, i, P * n:P * n + P], b.ident[:, :])
                    last.then_inc(gates_turned, 1)
                pe.wait_ge(gates_out, 8)
                for n in range(8):
                    half, i = n // 4, n % 4
                    for s in range(8):
                        last = nc.tensor.matmul(b.bank[n], gates_T[:, s, P * i:P * i + P], slots[:, s, 512 * half:512 * half + 512],
                                                start=(s == 0), stop=(s == 7))
                    last.then_inc(made, 1)

            @block.scalar
            def _(act):
                for n in range(0, 16, 2):
                    act.wait_ge(turned, n + 1)
                    nc.scalar.activation(slots[:, n // 2, 0:512], b.bank[n % 8], ACT.Copy).then_inc(turned_a, 1)
                for n in range(8):
                    act.wait_ge(gates_turned, n + 1)
                    nc.scalar.activation(gates_T[:, n, :], b.bank[n], ACT.Copy).then_inc(gates_out, 1)

            @block.vector
            def _(dve):
                link = b.link(dve, "dve_steps")
                V = nc.vector
                for n in range(1, 16, 2):
                    dve.wait_ge(turned, n + 1)
                    V.tensor_copy(slots[:, n // 2, 512:1024], b.bank[n % 8]).then_inc(turned_v, 1)
                tmp = hT[:, 0:2, :].rearrange("p a t -> p (a t)")
                for i in range(NT):
                    V.tensor_scalar(hot[:, i, :], slot_ids[:, :], slot1[:, i:i + 1], gate1[:, i:i + 1], ALU.is_equal, ALU.mult)
                    link(V.tensor_scalar(tmp, slot_ids[:, :], slot2[:, i:i + 1], gate2[:, i:i + 1], ALU.is_equal, ALU.mult))
                    last = link(V.tensor_tensor(hot[:, i, :], hot[:, i, :], tmp, ALU.add)) if i < NT - 1 else \
                        V.tensor_tensor(hot[:, i, :], hot[:, i, :], tmp, ALU.add).then_inc(gates, 1)
                for n in range(8):
                    half, i = n // 4, n % 4
                    dve.wait_ge(made, n + 1)
                    part = b.h[:, i, 512 * half:512 * half + 512]
                    V.tensor_tensor(part, part, b.bank[n], ALU.add)


NH, HD = 4, 128
CONV_K = 4
GD_IN = 4 * NH * HD + 2 * NH
BETA, DECAY, IGATE, FGATE = 0, 32, 64, 96
ODD_LOADS = [0, 512, 1024, 1536, GD_IN, GD_IN + 512, GD_IN + 1024, GD_IN + 1536]


class Odd:

    def __init__(self, b, ctx):
        def sb(name, *shape):
            return b.sb(ctx, name, [P, *shape])

        self.w = sb("w_odd", 2, KD, 512)
        self.hT = sb("hT_odd", KD, T)
        self.QKx = sb("QKx", 8, T)
        self.Q, self.K = self.QKx[:, 0:4, :], self.QKx[:, 4:8, :]
        self.xn = self.QKx[:, :, :].rearrange("p (i a) t -> p i (a t)", i=NT)
        self.V, self.Z = sb("Vo", 4, T), sb("Z", 4, T)
        self.BB, self.EG, self.GM = sb("BB", 4, T), sb("EG", 4, T), sb("GM", 4, T)
        self.KB, self.KW, self.QG, self.KD = sb("KB", 4, T), sb("KW", 4, T), sb("QG", 4, T), sb("KDc", 4, T)
        self.mq, self.mk, self.og, self.GB = sb("mq", 4, T), sb("mk", 4, T), sb("og", 4, T), sb("GB", 4, T)
        self.raw = flat(self.og)[:, 0:2 * (T + 3)].rearrange("p (a t) -> p a t", a=2)
        self.VO = sb("VO", NT, NH, HD + 1)
        self.wg = flat(self.GB)[:, 0:KD * P].rearrange("p (k f) -> p k f", k=KD)
        self.rows, self.grow = sb("rows", T), sb("grow", T)
        self.Y = self.Z[:, 0, :]
        self.cols = sb("cols", NT, P)
        self.gcol = sb("gcol", 8)
        self.gl = sb("gl", 4, NT)
        self.stat = sb("stat_o", 64)


def odd_project(b, m):
    nc, d = b.nc, b.dram
    w_all = d["od_w_in"][0].rearrange("(p k) n -> p k n", k=KD)
    items = [("gates", 0)] + [(kind, j) for kind in ("gq", "gk", "gv", "z") for j in range(4)] + [("cols", 0)]
    items += [(kind, j) for kind in ("bb", "gb", "Gb", "nq", "nk", "mq", "mk", "mv", "mo") for j in range(4)]
    at = {it: n for n, it in enumerate(items)}
    loads = ["gq", "gk", "gv", "z", "mq", "mk", "mv", "mo"]
    bias, sign, coef, alog = (m.gcol[:, i:i + 1] for i in range(4))

    with nc.Block() as block:
        w_sem = [b.sem("odd_w_in0"), b.sem("odd_w_in1")]
        wg_zero, wg_in, bias_zero, bias_in = (b.sem(f"odd_{x}") for x in ("wg_zero", "wg_in", "bias_zero", "bias_in"))
        made, evac, conved, silued = (b.sem(f"odd_{x}") for x in ("made", "evac", "conved", "silued"))
        y_ready, row_act, row_dve, squares = (b.sem(f"odd_{x}") for x in ("y_ready", "row_act", "row_dve", "squares"))
        ln_done, kd_in, kd_out, raw_zero, alog_exp = (b.sem(f"odd_{x}") for x in ("ln_done", "kd_in", "kd_out", "raw_zero", "alog_exp"))

        def evacuated(eng, n):
            if n == 0:
                eng.wait_ge(y_ready, 1)
            else:
                eng.wait_ge(evac, n)

        @block.sync
        def _(sp):
            for n, c in enumerate(ODD_LOADS):
                if n >= 2:
                    sp.wait_ge(made, at[loads[n - 2], 3] + 1)
                sp.dma_start(m.w[:, n % 2, :, :], w_all[:, :, c:c + 512]).then_inc(w_sem[n % 2], 16)

        @block.gpsimd
        def _(pool):
            nc.gpsimd.memset(m.wg[:, :, :], 0.0).then_inc(wg_zero, 1)
            pool.wait_ge(wg_zero, 1)
            with nc.allow_non_contiguous_dma(reason="gate columns"):
                for row, c in ((BETA, 2048), (DECAY, 2052), (IGATE, GD_IN + 2048), (FGATE, GD_IN + 2052)):
                    pool.dma_start(m.wg[:, :, row:row + NH], w_all[:, :, c:c + NH]).then_inc(wg_in, 16)
                pool.wait_ge(bias_zero, 1)
                for row, name, col in ((DECAY, "gd_dt_bias", bias), (IGATE, "ml_i_bias", bias), (FGATE, "ml_f_bias", bias),
                                       (DECAY, "gd_a_log", alog)):
                    pool.dma_start(col[row:row + NH, :], d[name][0].rearrange("(p o) -> p o", o=1)).then_inc(bias_in, 16)
            nc.gpsimd.memset(m.VO[:, :, :, HD:HD + 1], 1.0)

        @block.tensor
        def _(pe):
            for n, (kind, j) in enumerate(items):
                bank = b.bank[n % 8]
                if n >= 8:
                    evacuated(pe, n - 8)
                if kind == "gates":
                    pe.wait_ge(wg_in, 64)
                    for k in range(KD):
                        last = nc.tensor.matmul(bank, m.wg[:, k, :], m.hT[:, k, :], start=(k == 0), stop=(k == KD - 1))
                elif kind in loads:
                    load = loads.index(kind)
                    if j == 0:
                        pe.wait_ge(w_sem[load % 2], 16 * (load // 2 + 1))
                    w = m.w[:, load % 2, :, :]
                    for k in range(KD):
                        if kind == "mv":
                            last = nc.tensor.matmul(bank, m.hT[:, k, P * j:P * j + P], w[:, k, :],
                                                    start=(k == 0), stop=(k == KD - 1))
                        else:
                            last = nc.tensor.matmul(bank, w[:, k, P * j:P * j + P], m.hT[:, k, :],
                                                    start=(k == 0), stop=(k == KD - 1))
                elif kind == "cols":
                    pe.wait_ge(row_dve, 3)
                    pe.wait_ge(row_act, 5)
                    for c in range(NT):
                        last = nc.tensor.transpose(bank[:, P * c:P * c + P], m.rows[:, P * c:P * c + P], b.ident[:, :])
                elif kind in ("bb", "gb", "Gb"):
                    row = {"bb": BETA, "gb": DECAY, "Gb": FGATE}[kind] + j
                    src = m.grow if kind == "Gb" else m.rows
                    last = nc.tensor.matmul(bank, b.ident[:, row:row + 1].broadcast_to([P, P]), src[:, :],
                                            start=True, stop=True)
                else:
                    pe.wait_ge(squares, (0 if kind == "nq" else 4) + j + 1)
                    src = m.KD if kind == "nq" else m.KW
                    last = nc.tensor.matmul(bank, b.ones[:, :], src[:, j, :], start=True, stop=True)
                last.then_inc(made, 1)

        @block.scalar
        def _(act):
            def evacuate(n):
                kind, j = items[n]
                bank = b.bank[n % 8]
                act.wait_ge(made, n + 1)
                if kind in ("gq", "gk", "gv"):
                    if n <= 2:
                        act.wait_ge(raw_zero, 1)
                    else:
                        act.wait_ge(conved, n - 2)
                    ins = nc.scalar.activation(m.raw[:, (n - 1) % 2, 3:T + 3], bank, ACT.Copy)
                elif kind == "z":
                    ins = nc.scalar.activation(m.Z[:, j, :], bank, ACT.Silu)
                elif kind == "mo":
                    ins = nc.scalar.activation(m.og[:, j, :], bank, ACT.Sigmoid)
                elif kind == "gb":
                    nc.scalar.activation(m.GM[:, j, :], bank, ACT.Copy)
                    ins = nc.scalar.activation(m.EG[:, j, :], bank, ACT.Exp)
                elif kind in ("nq", "nk"):
                    t = (m.KD if kind == "nq" else m.KW)[:, j, :]
                    nc.scalar.activation(t, bank, ACT.Ln, bias=b.eps[:, 0:1]).then_inc(ln_done, 1)
                    act.wait_ge(ln_done, (0 if kind == "nq" else 4) + j + 1)
                    ins = nc.scalar.activation(t, t, ACT.Exp, scale=-0.5, bias=b.eps[:, 2:3] if kind == "nq" else 0.0)
                elif kind == "cols":
                    ins = nc.scalar.activation(m.cols[:, :, :].rearrange("p c f -> p (c f)"), bank, ACT.Copy)
                elif kind == "mv":
                    ins = nc.scalar.activation(m.VO[:, j, :, 0:HD], bank.rearrange("p (h v) -> p h v", h=NH), ACT.Copy)
                else:
                    dst = {"bb": m.BB, "Gb": m.GB, "mq": m.mq, "mk": m.mk}[kind]
                    ins = nc.scalar.activation(dst[:, j, :], bank, ACT.Copy)
                ins.then_inc(evac, 1)

            def silu(i):
                t = (m.Q, m.K, m.V)[i // 4][:, i % 4, :]
                act.wait_ge(conved, i + 1)
                nc.scalar.activation(t, t, ACT.Silu).then_inc(silued, 1)

            act.wait_ge(bias_in, 64)
            nc.scalar.activation(alog[DECAY:DECAY + NH, :], alog[DECAY:DECAY + NH, :], ACT.Exp).then_inc(alog_exp, 1)
            act.wait_ge(y_ready, 2)
            nc.scalar.activation(m.rows[0:32, :], m.Y[0:32, :], ACT.Sigmoid).then_inc(row_act, 1)
            nc.scalar.activation(m.grow[:, :], m.grow[:, :], ACT.Exp, scale=-1.0).then_inc(row_act, 1)
            act.wait_ge(row_act, 2)
            nc.scalar.activation(m.grow[:, :], m.grow[:, :], ACT.Ln, bias=b.ones[:, 0:1]).then_inc(row_act, 1)
            for n in range(1, 13):
                evacuate(n)
                if n >= 2:
                    silu(n - 2)
            silu(11)
            for j in range(4):
                act.wait_ge(silued, 8)
                nc.scalar.activation(m.KD[:, j, :], m.Q[:, j, :], ACT.Square).then_inc(squares, 1)
            for j in range(4):
                nc.scalar.activation(m.KW[:, j, :], m.K[:, j, :], ACT.Square).then_inc(squares, 1)
            nc.scalar.activation(m.KB[FGATE:P, 0, :], m.Y[IGATE:IGATE + 32, :], ACT.Copy).then_inc(row_act, 1)
            act.wait_ge(row_dve, 4)
            nc.scalar.activation(m.rows[IGATE:IGATE + 32, :], m.KB[FGATE:P, 1, :], ACT.Exp, scale=-1.0).then_inc(row_act, 1)
            for n in range(13, at["mq", 0]):
                evacuate(n)
            act.wait_ge(kd_in, 1)
            nc.scalar.activation(flat(m.KD), flat(m.KD), ACT.Exp, scale=-1.0).then_inc(kd_out, 1)
            for n in range(at["mq", 0], len(items)):
                evacuate(n)

        @block.vector
        def _(dve):
            link = b.link(dve, "dve_steps")
            V = nc.vector
            link(V.memset(m.gcol[:, :], 0.0))
            V.memset(coef, -1.0)
            V.memset(sign[0:FGATE, :], 1.0)
            V.memset(sign[FGATE:P, :], -1.0).then_inc(bias_zero, 1)
            V.memset(m.raw[:, :, 0:3], 0.0).then_inc(raw_zero, 1)
            V.memset(m.rows[:, :], 0.0)
            dve.wait_ge(alog_exp, 1)
            dve.wait_ge(bias_zero, 1)
            link(V.tensor_scalar(coef[DECAY:DECAY + NH, :], alog[DECAY:DECAY + NH, :], -1.0, None, ALU.mult))
            dve.wait_ge(made, 1)
            V.tensor_scalar(m.Y[:, :], b.bank[0], bias, sign, ALU.add, ALU.mult).then_inc(y_ready, 1)
            dve.wait_ge(y_ready, 1)
            V.scalar_tensor_tensor(m.grow[:, :], m.Y[:, :], -1.0, m.Y[:, :], ALU.mult, ALU.max).then_inc(y_ready, 1)
            for i in range(12):
                dst = (m.Q, m.K, m.V)[i // 4][:, i % 4, :]
                raw = m.raw[:, i % 2, :]
                dve.wait_ge(evac, i + 1)
                link(V.tensor_scalar(dst, raw[:, 0:T], b.col("gd_conv", i), None, ALU.mult))
                for tap in range(1, CONV_K):
                    ins = V.scalar_tensor_tensor(dst, raw[:, tap:tap + T], b.col("gd_conv", 12 * tap + i), dst, ALU.mult, ALU.add)
                    if tap < CONV_K - 1:
                        link(ins)
                ins.then_inc(conved, 1)
                if i == 1:
                    dve.wait_ge(row_act, 3)
                    sp_ = m.Y[:, :]
                    link(V.tensor_scalar(m.KB[:, 2, :], sp_, 0.0, None, ALU.max))
                    link(V.tensor_tensor(m.KB[:, 2, :], m.KB[:, 2, :], m.grow[:, :], ALU.add))
                    link(V.tensor_scalar(m.KB[:, 2, :], m.KB[:, 2, :], coef, None, ALU.mult))
                    for c in range(NT):
                        ins = V.tensor_tensor_scan(m.rows[DECAY:DECAY + 32, P * c:P * c + P], b.ones[DECAY:DECAY + 32, :],
                                                   m.KB[DECAY:DECAY + 32, 2, P * c:P * c + P], 0.0, ALU.mult, ALU.add)
                    ins.then_inc(row_dve, 1)
            f = slice(FGATE, P)
            B_ = m.KB[f, 3, :]
            one = b.ones[f, 0:1].broadcast_to([32, T])
            link(V.tensor_tensor_scan(B_, one, m.KB[f, 2, :], 0.0, ALU.mult, ALU.add))
            dve.wait_ge(row_act, 4)
            V.tensor_tensor(m.rows[f, :], m.KB[f, 0, :], B_, ALU.subtract).then_inc(row_dve, 1)
            dve.wait_ge(row_dve, 2)
            link(V.memset(m.grow[0:FGATE, :], 0.0))
            V.tensor_tensor_scan(m.grow[f, :], m.rows[f, :], m.rows[f, :], 0.0, ALU.max, ALU.max).then_inc(row_dve, 1)
            dve.wait_ge(row_dve, 3)
            V.tensor_tensor(m.KB[f, 1, :], B_, m.grow[f, :], ALU.add).then_inc(row_dve, 1)
            dve.wait_ge(silued, 12)
            evacuated(dve, at["nk", 3])
            V.tensor_tensor(flat(m.V), flat(m.V), flat(m.BB), ALU.mult)
            V.tensor_tensor(flat(m.Q), flat(m.Q), flat(m.KD), ALU.mult)
            link(V.tensor_tensor(flat(m.K), flat(m.K), flat(m.KW), ALU.mult))
            gm = m.GM[:, :, :].rearrange("p h (c t) -> p (h c) t", c=NT)
            V.tensor_tensor(m.KD[:, :, :].rearrange("p h (c t) -> p (h c) t", c=NT), gm,
                            gm[:, :, P - 1:P].broadcast_to([P, 4 * NT, P]), ALU.subtract).then_inc(kd_in, 1)
            link(V.tensor_tensor(flat(m.KB), flat(m.K), flat(m.BB), ALU.mult))
            V.scalar_tensor_tensor(flat(m.KW), flat(m.KB), -1.0, flat(m.EG), ALU.mult, ALU.mult)
            V.tensor_tensor(flat(m.QG), flat(m.Q), flat(m.EG), ALU.mult)
            V.tensor_copy(m.gl[:, :, :], chunks(m.EG)[:, :, :, P - 1])
            dve.wait_ge(kd_out, 1)
            V.tensor_tensor(flat(m.KD), flat(m.KD), flat(m.K), ALU.mult)


def delta_chunks(b, m):
    nc = b.nc
    w = m.w[:, :, :, :].rearrange("p a k n -> p (a k n)")

    def mats(i):
        return w[:, 8 * P * i:8 * P * (i + 1)].rearrange("p (h s) -> p h s", h=8)

    MT, X, XT, PR, AT, DC, DS = (mats(i) for i in range(7))
    VBt, KDt = m.hT[:, 0:4, :], m.hT[:, 4:8, :]
    Ot = m.Ot = m.BB
    S = m.EG[:, 0, :]
    RHS, VN = m.EG[:, 1, :], m.EG[:, 2, :]

    fills = [("MT", 0), ("MT", 1), ("AT", 0), ("AT", 1), ("X0", 0), ("X0", 1)] + doubling_fills()
    for g in range(2):
        fills += [("KS", g), ("VN", g), ("O", g), ("dS", g)]
    acts = [f for f in fills if f[0] in ("X0", "VN", "O")]
    dves = [f for f in fills if f not in acts]

    def bank_of(name, g):
        first = {"MT": 0, "AT": 6, "X0": 2, "KS": 0, "VN": 2, "O": 4, "dS": 6}
        if name in first:
            return b.bank[first[name] + g]
        return b.bank[doubling_bank(name) + g]

    with nc.Block() as block:
        turned, turned_out = b.sem("gd_turned"), b.sem("gd_turned_out")
        filled, by_act, by_dve = b.sem("gd_filled"), b.sem("gd_by_act"), b.sem("gd_by_dve")
        first_x, state, d_in, d_exp = (b.sem(f"gd_{x}") for x in ("first_x", "state", "d_in", "d_exp"))
        order = Order(fills, acts, dves, filled, by_act, by_dve)

        @block.tensor
        def _(pe):
            for i in range(8):
                src = (m.V if i < 4 else m.KD)[:, i % 4, :]
                for c in range(NT):
                    last = nc.tensor.transpose(b.bank[i][:, P * c:P * c + P], src[:, P * c:P * c + P], b.ident[:, :])
                last.then_inc(turned, 1)
            pe.wait_ge(turned_out, 8)
            for c2 in range(NT // 2):
                for name, right in (("MT", m.KB), ("AT", m.Q)):
                    for g in range(2):
                        if c2:
                            order.wait_taken(pe, c2 - 1, {"MT": ("KS", g), "AT": ("dS", g)}[name])
                        tok = slice(P * (2 * c2 + g), P * (2 * c2 + g) + P)
                        for h in range(NH):
                            last = nc.tensor.matmul(bank_of(name, g)[:, P * h:P * h + P], m.K[:, h, tok], right[:, h, tok],
                                                    start=True, stop=True)
                        last.then_inc(filled, 1)
                for g in range(2):
                    pe.wait_ge(first_x, 2 * c2 + g + 1)
                    if c2:
                        order.wait_taken(pe, c2 - 1, ("VN", g))
                    for h in range(NH):
                        last = nc.tensor.transpose(bank_of("X0", g)[:, P * h:P * h + P], XT[:, 4 * g + h, :], b.ident[:, :])
                    last.then_inc(filled, 1)
                if c2:
                    order.wait_taken(pe, c2 - 1, ("O", 1))
                pe_doubling(nc, pe, order, c2, bank_of, MT, X, XT, PR)
                for g in range(2):
                    c = 2 * c2 + g
                    tok = slice(P * c, P * c + P)
                    pe.wait_ge(state, c + 1)
                    order.wait_taken(pe, c2, ("P6", g))
                    for h in range(NH):
                        last = nc.tensor.matmul(bank_of("KS", g)[:, P * h:P * h + P], m.KW[:, h, tok], S[:, P * h:P * h + P],
                                                start=True, stop=True)
                    last.then_inc(filled, 1)
                    order.wait_taken(pe, c2, ("KS", g))
                    order.wait_taken(pe, c2, ("XT6", g))
                    for h in range(NH):
                        last = nc.tensor.matmul(bank_of("VN", g)[:, P * h:P * h + P], XT[:, 4 * g + h, :], RHS[:, P * h:P * h + P],
                                                start=True, stop=True)
                    last.then_inc(filled, 1)
                    order.wait_taken(pe, c2, ("AT", g))
                    order.wait_taken(pe, c2, ("VN", g))
                    for h in range(NH):
                        o = bank_of("O", g)[:, P * h:P * h + P]
                        nc.tensor.matmul(o, m.QG[:, h, tok], S[:, P * h:P * h + P], start=True, stop=False)
                        last = nc.tensor.matmul(o, AT[:, 4 * g + h, :], VN[:, P * h:P * h + P], start=False, stop=True)
                    last.then_inc(filled, 1)
                    for h in range(NH):
                        last = nc.tensor.matmul(bank_of("dS", g)[:, P * h:P * h + P], KDt[:, c, P * h:P * h + P],
                                                VN[:, P * h:P * h + P], start=True, stop=True)
                    last.then_inc(filled, 1)

        @block.scalar
        def _(act):
            for i in range(1, 8, 2):
                act.wait_ge(turned, i + 1)
                nc.scalar.activation((VBt if i < 4 else KDt)[:, :, P * (i % 4):P * (i % 4) + P],
                                     b.bank[i].rearrange("p (c f) -> p c f", c=NT), ACT.Copy).then_inc(turned_out, 1)
            for c2 in range(NT // 2):
                act.wait_ge(d_in, c2 + 1)
                nc.scalar.activation(flat(DC), flat(DC), ACT.Exp).then_inc(d_exp, 1)
                for f in acts:
                    name, g = f
                    order.wait_filled(act, c2, f)
                    dst = {"X0": X[:, 4 * g:4 * g + 4, :].rearrange("p h s -> p (h s)"), "VN": VN,
                           "O": Ot[:, 2 * c2 + g, :]}[name]
                    nc.scalar.activation(dst, bank_of(name, g), ACT.Copy).then_inc(by_act, 1)

        @block.vector
        def _(dve):
            link = b.link(dve, "dve_steps")
            V = nc.vector
            for i in range(0, 8, 2):
                dve.wait_ge(turned, i + 1)
                V.tensor_copy((VBt if i < 4 else KDt)[:, :, P * (i % 4):P * (i % 4) + P],
                              b.bank[i].rearrange("p (c f) -> p c f", c=NT)).then_inc(turned_out, 1)
            V.memset(S, 0.0).then_inc(state, 1)

            def eight(mask):
                return mask.rearrange("p (o s) -> p o s", o=1).broadcast_to([P, 8, P])

            for c2 in range(NT // 2):
                for g in range(2):
                    c = 2 * c2 + g
                    for h in range(NH):
                        last = V.tensor_scalar(DC[:, 4 * g + h, :], m.GM[:, h, P * c:P * c + P],
                                               m.cols[:, c, DECAY + h:DECAY + h + 1], 0.0, ALU.subtract, ALU.min)
                last.then_inc(d_in, 1)
                dve.wait_ge(d_exp, c2 + 1)
                link(V.scalar_tensor_tensor(DS, DC, -1.0, eight(b.before[:, :]), ALU.mult, ALU.mult))
                link(V.tensor_tensor(DC, DC, eight(b.causal[:, :]), ALU.mult))
                for f in dves:
                    name, g = f
                    bank = bank_of(name, g)
                    four = bank.rearrange("p (h s) -> p h s", h=4)
                    hs = slice(4 * g, 4 * g + 4)
                    order.wait_filled(dve, c2, f)
                    if name == "MT":
                        V.tensor_tensor(MT[:, hs, :], four, DS[:, hs, :], ALU.mult).then_inc(by_dve, 1)
                        order.wait_taken(dve, c2, f)
                        first_inverse(nc, b, link, MT[:, hs, :], XT[:, hs, :]).then_inc(first_x, 1)
                    elif name == "AT":
                        V.tensor_tensor(AT[:, hs, :], four, DC[:, hs, :], ALU.mult).then_inc(by_dve, 1)
                    elif name == "KS":
                        V.tensor_tensor(RHS, bank, VBt[:, 2 * c2 + g, :], ALU.add).then_inc(by_dve, 1)
                    elif name == "dS":
                        c = 2 * c2 + g
                        for h in range(NH):
                            s = S[:, P * h:P * h + P]
                            last = V.scalar_tensor_tensor(s, s, m.gl[:, h, c:c + 1], bank[:, P * h:P * h + P],
                                                          ALU.mult, ALU.add)
                        last.then_inc(by_dve, 1)
                        order.wait_taken(dve, c2, f)
                        V.tensor_copy(m.stat[:, 0:1], S[:, 0:1]).then_inc(state, 1)
                    else:
                        take_doubling(nc, b, name, g, four, X, XT, PR).then_inc(by_dve, 1)


def mlstm(b, m):
    nc, d = b.nc, b.dram
    w_out = d["od_w_out"][0].rearrange("(k p) n -> p k n", p=P)
    at, n = {}, 0
    for h in range(NH):
        for j in range(NT):
            at[h, j] = n
            n += NT - j
    SC = m.QKx[:, :, :].rearrange("p a t -> p (a t)")
    SC2 = flat(m.KB)

    def weights(h, j, i, width=1):
        if h < 3:
            return SC[:, P * (at[h, j] + i - j):P * (at[h, j] + i - j + width)]
        return SC2[:, P * (at[h, j] - 30 + i - j):P * (at[h, j] - 30 + i - j + width)]

    D_ = flat(m.KW)
    NUM = m.hT[:, :, :].rearrange("p k t -> p (k t)")[:, 0:NT * NH * (HD + 1)].rearrange("p (c h v) -> p c h v", c=NT, h=NH)
    Ht = m.QG[:, :, :]
    den = m.stat[:, 0:16].rearrange("p (c h) -> p c h", c=NT)
    m.YC, m.YD = m.GM, m.V
    pairs = [(h, j) for h in range(NH) for j in range(NT)]
    with nc.Block() as block:
        s_made, s_taken, d_in, d_exp, n_made, n_taken = (b.sem(f"ml_{x}") for x in ("s", "s_taken", "d_in", "d_exp", "n", "n_taken"))
        squared, var_in, var_out, normed, turned, turned_taken, h_ready = (
            b.sem(f"ml_{x}") for x in ("squared", "var_in", "var_out", "normed", "turned", "turned_taken", "h_ready"))
        w_out_in = b.sem("odd_w_out_in")

        @block.sync
        def _(sp):
            for i in range(2):
                sp.dma_start(m.w[:, i, :, :], w_out[:, :, 512 * i:512 * i + 512]).then_inc(w_out_in, 16)

        @block.tensor
        def _(pe):
            for n, (h, j) in enumerate(pairs):
                if n >= 4:
                    pe.wait_ge(s_taken, n - 3)
                nc.tensor.matmul(b.bank[n % 4][:, 0:T - P * j], m.mk[:, h, P * j:P * j + P], m.mq[:, h, P * j:T],
                                 start=True, stop=True).then_inc(s_made, 1)
            for i in range(NT):
                for half in range(2):
                    n = 2 * i + half
                    if n >= 4:
                        pe.wait_ge(n_taken, n - 3)
                    pe.wait_ge(s_taken, 16)
                    for hh in range(2):
                        h = 2 * half + hh
                        for j in range(i + 1):
                            last = nc.tensor.matmul(b.bank[4 + n % 4][:, (HD + 1) * hh:(HD + 1) * (hh + 1)], weights(h, j, i),
                                                    m.VO[:, j, h, :], start=(j == 0), stop=(j == i))
                    last.then_inc(n_made, 1)
            for n in range(8):
                pe.wait_ge(normed, 1 if n < 4 else 2)
                src = m.Ot if n < 4 else Ht
                if n >= 4:
                    pe.wait_ge(n_taken, 8)
                for c in range(NT):
                    last = nc.tensor.transpose(b.bank[n][:, P * c:P * c + P], src[:, c, P * (n % 4):P * (n % 4) + P], b.ident[:, :])
                last.then_inc(turned, 1)

        @block.scalar
        def _(act):
            nc.scalar.activation(flat(m.KD), flat(m.Ot),
                                 ACT.Square).then_inc(squared, 1)
            for n, (h, j) in enumerate(pairs):
                act.wait_ge(d_in, n + 1)
                t = D_[:, 512 * (n % 4):512 * (n % 4) + T - P * j]
                nc.scalar.activation(t, t, ACT.Exp, scale=-1.0).then_inc(d_exp, 1)
            for n in range(8):
                act.wait_ge(n_made, n + 1)
                nc.scalar.activation(NUM[:, n // 2, 2 * (n % 2):2 * (n % 2) + 2, :],
                                     b.bank[4 + n % 4][:, 0:2 * (HD + 1)].rearrange("p (h v) -> p h v", h=2), ACT.Copy).then_inc(n_taken, 1)
            act.wait_ge(h_ready, 1)
            nc.scalar.activation(m.mq[:, :, :].rearrange("p a t -> p (a t)"), flat(Ht), ACT.Square).then_inc(squared, 1)
            act.wait_ge(var_in, 1)
            nc.scalar.activation(m.stat[:, 16:48], m.stat[:, 16:48], ACT.Sqrt).then_inc(var_out, 1)

        @block.vector
        def _(dve):
            link = b.link(dve, "dve_steps")
            V = nc.vector
            lag = 2

            def exponent(n):
                h, j = pairs[n]
                if n >= 4:
                    dve.wait_ge(s_taken, n - 3)
                V.tensor_scalar(D_[:, 512 * (n % 4):512 * (n % 4) + T - P * j], m.GB[:, h, P * j:T],
                                m.cols[:, j, FGATE + h:FGATE + h + 1], 0.0, ALU.subtract, ALU.max).then_inc(d_in, 1)

            for n in range(lag):
                exponent(n)
            for n, (h, j) in enumerate(pairs):
                if n + lag < 16:
                    exponent(n + lag)
                dve.wait_ge(d_exp, n + 1)
                dve.wait_ge(s_made, n + 1)
                t = D_[:, 512 * (n % 4):512 * (n % 4) + T - P * j]
                link(V.tensor_tensor(t[:, 0:P], t[:, 0:P], b.causal[:, :], ALU.mult))
                V.scalar_tensor_tensor(weights(h, j, j, NT - j), b.bank[n % 4][:, 0:T - P * j], HD ** -0.5, t,
                                       ALU.mult, ALU.mult).then_inc(s_taken, 1)
            dve.wait_ge(squared, 1)
            ssq = m.stat[:, 16:32]
            link(V.reduce_sum(ssq, flat(m.KD).rearrange("p (g v) -> p g v", v=HD), AX.X))
            dve.wait_ge(n_taken, 8)
            dn = NUM[:, :, :, HD]
            link(V.scalar_tensor_tensor(den, dn, -1.0, dn, ALU.mult, ALU.max))
            link(V.tensor_tensor(den, den, m.cols[:, :, IGATE:IGATE + NH], ALU.max))
            link(V.reciprocal(den, den))
            V.tensor_tensor(Ht.rearrange("p c (h v) -> p c h v", h=NH), NUM[:, :, :, 0:HD],
                            m.stat[:, 0:16].rearrange("p (c h o) -> p c h o", c=NT, o=1).broadcast_to([P, NT, NH, HD]),
                            ALU.mult).then_inc(h_ready, 1)
            dve.wait_ge(squared, 2)
            link(V.reduce_sum(m.stat[:, 32:48], flat(m.mq).rearrange("p (g v) -> p g v", v=HD), AX.X))
            V.tensor_scalar(m.stat[:, 16:48], m.stat[:, 16:48], 1.0 / HD, NORM_EPS, ALU.mult, ALU.add).then_inc(var_in, 1)
            dve.wait_ge(var_out, 1)
            link(V.reciprocal(m.stat[:, 16:48], m.stat[:, 16:48]))
            for i, t in enumerate((m.Ot, Ht)):
                t3 = flat(t).rearrange("p (g v) -> p g v", v=HD)
                r = m.stat[:, 16 + 16 * i:32 + 16 * i].rearrange("p (g o) -> p g o", o=1).broadcast_to([P, 16, HD])
                V.tensor_tensor(t3, t3, r, ALU.mult).then_inc(normed, 1)
            for n in range(8):
                dve.wait_ge(turned, n + 1)
                if n < 4:
                    V.scalar_tensor_tensor(m.YC[:, n, :], b.bank[n], b.col("gd_norm"), m.Z[:, n, :], ALU.mult, ALU.mult)
                else:
                    V.scalar_tensor_tensor(m.YD[:, n - 4, :], b.bank[n], b.col("ml_norm", n - 4), m.og[:, n - 4, :],
                                           ALU.mult, ALU.mult)


def odd_layer(b):
    with ExitStack() as ctx:
        m = Odd(b, ctx)
        norm_into(b, "mix1", PAR_AT["norm_mix"] + 8, m.xn, flat(m.KB)[:, 0:D], m.hT)
        odd_project(b, m)
        delta_chunks(b, m)
        mlstm(b, m)
        project_out(b, "odd", m.w, b.sem("odd_w_out_in"), lambda k: (m.YC if k < 4 else m.YD)[:, k % 4, :])


def final_norm(b):
    nc, d = b.nc, b.dram
    with ExitStack() as ctx:
        gain, y = b.sb(ctx, "final_gain", [P, D]), b.sb(ctx, "final_y", [P, NT, D])
        ss = b.sb(ctx, "final_ss", [P, NT])
        with nc.Block() as block:
            gain_in, squares, mean, root, ready, stored = (
                b.sem(f"final_{x}") for x in ("gain_in", "squares", "mean", "root", "ready", "stored"))

            @block.sync
            def _(sp):
                sp.dma_start(gain[:, :], d["norm_final"].rearrange("(o n) -> o n", o=1).broadcast_to([P, D])).then_inc(gain_in, 16)
                for i in range(NT):
                    sp.wait_ge(ready, i + 1)
                    sp.dma_start(b.out[0, P * i:P * i + P, :], y[:, i, :]).then_inc(stored, 16)
                sp.wait_ge(stored, 16 * NT)

            @block.scalar
            def _(act):
                for i in range(NT):
                    nc.scalar.activation(y[:, i, :], b.h[:, i, :], ACT.Square, accum_out=ss[:, i:i + 1]).then_inc(squares, 1)
                act.wait_ge(mean, 1)
                nc.scalar.activation(ss[:, :], ss[:, :], ACT.Sqrt).then_inc(root, 1)

            @block.vector
            def _(dve):
                link = b.link(dve, "dve_steps")
                dve.wait_ge(squares, NT)
                nc.vector.tensor_scalar(ss[:, :], ss[:, :], 1.0 / D, NORM_EPS, ALU.mult, ALU.add).then_inc(mean, 1)
                dve.wait_ge(root, 1)
                link(nc.vector.reciprocal(ss[:, :], ss[:, :]))
                dve.wait_ge(gain_in, 16)
                for i in range(NT):
                    nc.vector.scalar_tensor_tensor(y[:, i, :], b.h[:, i, :], ss[:, i:i + 1], gain[:, :],
                                                   ALU.mult, ALU.mult).then_inc(ready, 1)


def program(nc, dram, out):
    with ExitStack() as ctx:
        b = Build(nc, dram, out, ctx)
        constants(b)
        even_layer(b)
        b.end_layer()
        moe(b, 0)
        b.end_layer()
        odd_layer(b)
        b.end_layer()
        moe(b, 1)
        b.end_layer()
        final_norm(b)
        b.end_layer()


def kernel(**inputs):
    import numpy as _np
    import concourse.bacc as _bacc
    from concourse import mybir as _mybir
    from concourse.bass_utils import run_bass_kernel_spmd as _run

    nc = _bacc.Bacc("TRN2", target_bir_lowering=False, num_devices=1)
    arrays, dram = {}, {}
    for name in inputs:
        a = _np.ascontiguousarray(inputs[name])
        arrays[f"in_{name}"] = a
        dram[name] = nc.dram_tensor(f"in_{name}", a.shape, _mybir.dt.from_np(a.dtype), kind="ExternalInput").ap()
    out = nc.dram_tensor("out_0", (1, T, D), F32, kind="ExternalOutput").ap()
    program(nc, dram, out)
    r = _run(nc, [arrays], core_ids=[0])
    return r.results[0]["out_0"]
```

```python
from contextlib import ExitStack
import math

import concourse.bass as bass
from concourse import mybir

F32 = mybir.dt.float32
I32 = mybir.dt.int32
BF16 = mybir.dt.bfloat16
U32 = mybir.dt.uint32
ALU = mybir.AluOpType
ACT = mybir.ActivationFunctionType
AX = mybir.AxisListType

P = 128
D = 1024
T = 512
NT = T // P
KD = D // P
NORM_EPS = 1e-6
RW_LN_EPS = 64e-5
E = 32
GROUPS = 4
EPG = E // GROUPS
DE = 256
SLOTS = 2 * T
WIN = 64
RING = 4
BIG = 1e30

PAR_ROWS = [
    ("ev_mu", 14), ("rw_w0", 4), ("rw_a0", 4), ("rw_k_k", 4), ("rw_k_a", 4), ("rw_r_k", 4),
    ("rw_ln_w", 4), ("rw_ln_b", 4), ("hg_lb_logits", 8), ("hg_norm", 1), ("gd_norm", 1), ("ml_norm", 4),
    ("norm_mix", 16), ("norm_ffn", 16), ("gd_conv", 48),
]
PAR_AT = {}
_at = 0
for _name, _n in PAR_ROWS:
    if _name == "gd_conv":
        _at = P
    PAR_AT[_name] = _at
    _at += _n
PAR_COLS = 2 * P


def chained(eng, sem, count):

    def link(ins):
        count[0] += 1
        ins.then_inc(sem, 1)
        eng.wait_ge(sem, count[0])
        return count[0]

    return link


class Build:

    def __init__(self, nc, dram, out, ctx):
        self.nc, self.dram, self.out, self.ctx = nc, dram, out, ctx
        self.sems = {}
        self.layer = 0
        self.counts = {}
        self.h = self.sb(ctx, "h", [P, NT, D])
        self.par = self.sb(ctx, "par", [P, PAR_COLS])
        self.ident = self.sb(ctx, "ident", [P, P])
        self.causal = self.sb(ctx, "causal", [P, P])
        self.before = self.sb(ctx, "before", [P, P])
        self.ones = self.sb(ctx, "ones", [P, P])
        self.halves = self.sb(ctx, "halves", [P, P])
        self.level = self.sb(ctx, "level", [P, 7, P])
        self.level0T = self.sb(ctx, "level0T", [P, P])
        self.small = self.sb(ctx, "small", [P, 64])
        self.ss = self.sb(ctx, "ss", [P, NT])
        self.eps = self.sb(ctx, "eps", [P, 4])
        self.ring = self.sb(ctx, "ring", [P, RING * 3 * KD * DE])
        self.arrived = {}
        self.psum = ctx.enter_context(nc.psum_tensor("psum", [P, 8, 512], F32))
        self.bank = [self.psum[:, i, :] for i in range(8)]

    def sb(self, ctx, name, shape, dt=F32):
        return ctx.enter_context(self.nc.sbuf_tensor(name, shape, dt))

    def carver(self):
        at = [0]

        def carve(rows, cols):
            first = at[0]
            at[0] += rows * cols
            assert at[0] <= RING * 3 * KD * DE
            return self.ring[:, first:at[0]].rearrange("p (r c) -> p r c", r=rows)

        return carve

    def sem(self, name):
        if name not in self.sems:
            self.sems[name] = self.nc.alloc_semaphore(name=f"{name}_{self.layer}")
        return self.sems[name]

    def end_layer(self):
        self.nc.clear_and_free_semaphores(list(self.sems.values()))
        self.nc.all_engine_barrier()
        self.layer += 1
        self.sems.clear()
        self.counts.clear()

    def link(self, eng, name):
        return chained(eng, self.sem(name), self.counts.setdefault(name, [0]))

    def col(self, name, i=0):
        c = PAR_AT[name] + i
        return self.par[:, c:c + 1]


def constants(b):
    nc, d = b.nc, b.dram
    with ExitStack() as ctx:
        rows, waste = b.sb(ctx, "par_rows", [P, 2, P]), b.sb(ctx, "waste", [P, 2, D])
        block = ctx.enter_context(nc.Block())
        rows_in, rows_zero, x_in = b.sem("rows_in"), b.sem("rows_zero"), b.sem("x_in")
        masks, rows_turned, squared = b.sem("masks"), b.sem("rows_turned"), b.sem("squared")
        where = []
        for name, n in PAR_ROWS:
            at = PAR_AT[name]
            if name in ("norm_mix", "norm_ffn"):
                continue
            src = d[name]
            if name == "hg_norm":
                for half in range(2):
                    where.append((rows[at:at + 1, 0, 64 * half:64 * half + 64], src))
                continue
            if len(src.shape) == 3:
                src = src.rearrange("a b c -> a (b c)")
            src = src.rearrange("a (n p) -> (a n) p", p=P)
            where.append((rows[at % P:at % P + n, at // P, :], src))

        @block.sync
        def _(sp):
            for i in range(NT):
                sp.dma_start(b.h[:, i, :], d["x"][0, P * i:P * i + P, :]).then_inc(x_in, 16)
            sp.wait_ge(rows_zero, 1)
            for dst, src in where:
                sp.dma_start(dst, src).then_inc(rows_in, 16)

        @block.gpsimd
        def _(pool):
            link = b.link(pool, "pool_steps")
            nc.gpsimd.memset(b.eps[:, 0:1], 1e-6)
            nc.gpsimd.memset(b.eps[:, 1:2], RW_LN_EPS)
            nc.gpsimd.memset(b.eps[:, 2:3], -0.5 * math.log(128.0))
            nc.gpsimd.memset(b.eps[:, 3:4], 0.0)
            nc.gpsimd.memset(b.ident[:, :], 0.0)
            nc.gpsimd.memset(b.causal[:, :], 0.0)
            nc.gpsimd.memset(b.before[:, :], 0.0)
            nc.gpsimd.memset(b.halves[:, :], 0.0)
            nc.gpsimd.memset(b.level[:, :, :], 0.0)
            link(nc.gpsimd.memset(b.ones[:, :], 1.0))
            link(nc.gpsimd.memset(b.halves[0:64, 0:64], 1.0))
            link(nc.gpsimd.memset(b.halves[64:128, 64:128], 1.0))
            nc.gpsimd.affine_select(out=b.ident[:, :], in_=b.ident[:, :], compare_op=ALU.not_equal, fill=1.0,
                                    base=0, pattern=[[-1, P]], channel_multiplier=1)
            nc.gpsimd.affine_select(out=b.causal[:, :], in_=b.ones[:, :], compare_op=ALU.is_ge, fill=0.0,
                                    base=0, pattern=[[1, P]], channel_multiplier=-1)
            nc.gpsimd.affine_select(out=b.before[:, :], in_=b.ones[:, :], compare_op=ALU.is_ge, fill=0.0,
                                    base=-1, pattern=[[1, P]], channel_multiplier=-1)
            for l in range(7):
                m = 1 << l
                n = P // (2 * m)
                v = b.level[:, l, :].rearrange("p (n two m) -> p n two m", two=2, m=m)
                src = b.ones[:, :].rearrange("p (n two m) -> p n two m", two=2, m=m)
                link(nc.gpsimd.affine_select(out=v[:, :, 0, :], in_=src[:, :, 0, :], compare_op=ALU.is_ge, fill=0.0,
                                             base=-m, pattern=[[-2 * m, n], [0, m]], channel_multiplier=1))
                link(nc.gpsimd.affine_select(out=v[:, :, 0, :], in_=v[:, :, 0, :], compare_op=ALU.is_ge, fill=0.0,
                                             base=2 * m - 1, pattern=[[2 * m, n], [0, m]], channel_multiplier=-1))
            nc.gpsimd.memset(b.small[:, :], 0.0).then_inc(masks, 1)

        @block.scalar
        def _(act):
            for name in ("norm_mix", "norm_ffn"):
                at = PAR_AT[name]
                for layer in range(2):
                    act.dma_start(b.par[:, at + 8 * layer:at + 8 * layer + 8],
                                  d[name][layer].rearrange("(p k) -> p k", k=KD)).then_inc(b.sem("gains_in"), 16)
            act.wait_ge(x_in, 16 * NT)
            for i in range(NT):
                square_tile(b, i, waste[:, i % 2, :]).then_inc(squared, 1)
                if i % 2:
                    act.wait_ge(squared, i + 1)
            act.wait_ge(b.sem("gains_in"), 64)

        @block.vector
        def _(dve):
            nc.vector.memset(rows[:, :, :], 0.0).then_inc(rows_zero, 1)
            dve.wait_ge(rows_turned, 3)
            nc.vector.tensor_copy(b.level0T[:, :], b.bank[2][:, 0:P])
            n = PAR_AT["norm_mix"]
            nc.vector.tensor_copy(b.par[:, 0:n], b.bank[0][:, 0:n])
            nc.vector.tensor_copy(b.par[:, P:2 * P], b.bank[1][:, 0:P])

        @block.tensor
        def _(pe):
            pe.wait_ge(masks, 1)
            pe.wait_ge(b.sem("pool_steps"), 17)
            pe.wait_ge(rows_in, 16 * len(where))
            for i in range(2):
                nc.tensor.transpose(b.bank[i][:, 0:P], rows[:, i, :], b.ident[:, :]).then_inc(rows_turned, 1)
            nc.tensor.transpose(b.bank[2][:, 0:P], b.level[:, 0, :], b.ident[:, :]).then_inc(rows_turned, 1)


def square_tile(b, i, waste):
    return b.nc.scalar.activation(waste, b.h[:, i, :], ACT.Square, accum_out=b.ss[:, i:i + 1])


def norm_into(b, tag, gain_at, xn, hT, first_loads, clear=None):
    nc = b.nc
    with ExitStack() as ctx:
        ss = b.ss
        rstd = b.sb(ctx, f"rstd_{tag}", [P, NT])
        block = ctx.enter_context(nc.Block())
        root, scaled = b.sem(f"root_{tag}"), b.sem(f"scaled_{tag}")
        mean_ready, turned, evac = b.sem(f"mean_{tag}"), b.sem(f"turned_{tag}"), b.sem(f"evac_{tag}")

        @block.sync
        def _(sp):
            first_loads(sp)

        if clear:
            @block.gpsimd
            def _(pool):
                clear()

        @block.scalar
        def _(act):
            act.wait_ge(mean_ready, 1)
            nc.scalar.activation(ss[:, :], ss[:, :], ACT.Sqrt).then_inc(root, 1)
            for k in range(1, KD, 2):
                act.wait_ge(turned, k + 1)
                nc.scalar.activation(hT[:, k, :], b.bank[k % 4][:, :], ACT.Copy,
                                     scale=b.par[:, gain_at + k:gain_at + k + 1]).then_inc(evac, 1)

        @block.vector
        def _(dve):
            nc.vector.tensor_scalar(ss[:, :], ss[:, :], 1.0 / D, NORM_EPS, ALU.mult, ALU.add).then_inc(mean_ready, 1)
            dve.wait_ge(root, 1)
            link = b.link(dve, "dve_steps")
            link(nc.vector.reciprocal(rstd[:, :], ss[:, :]))
            for i in range(NT):
                nc.vector.tensor_scalar(xn[:, i, :], b.h[:, i, :], rstd[:, i:i + 1], None, ALU.mult).then_inc(scaled, 1)
            for k in range(0, KD, 2):
                dve.wait_ge(turned, k + 1)
                nc.vector.tensor_scalar(hT[:, k, :], b.bank[k % 4][:, :], b.par[:, gain_at + k:gain_at + k + 1], None,
                                        ALU.mult).then_inc(b.sem(f"evac_even_{tag}"), 1)

        @block.tensor
        def _(pe):
            by_k = xn[:, :, :].rearrange("p i (q k) -> p i k q", k=KD)
            for k in range(KD):
                if k >= 4:
                    pe.wait_ge(evac if k % 2 else b.sem(f"evac_even_{tag}"), (k - 4) // 2 + 1)
                for i in range(NT):
                    if k == 0:
                        pe.wait_ge(scaled, i + 1)
                    last = nc.tensor.transpose(b.bank[k % 4][:, P * i:P * i + P], by_k[:, i, k, :], b.ident[:, :])
                last.then_inc(turned, 1)


RW_H, RW_F = 8, 64
DECAY_RATE = math.exp(-0.5)
EVEN_LOADS = [(0, 512), (512, 512), (1024, 512), (1536, 256), (1792, 512), (2304, 512), (2816, 512), (3328, 512)]


def flat(t):
    return t[:, :, :].rearrange("p a t -> p (a t)")


class Order:

    def __init__(self, fills, acts, dves, filled, by_act, by_dve):
        self.fills, self.acts, self.dves = fills, acts, dves
        self.filled, self.by_act, self.by_dve = filled, by_act, by_dve

    def wait_filled(self, eng, c, f):
        eng.wait_ge(self.filled, c * len(self.fills) + self.fills.index(f) + 1)

    def wait_taken(self, eng, c, f):
        if f in self.acts:
            eng.wait_ge(self.by_act, c * len(self.acts) + self.acts.index(f) + 1)
        else:
            eng.wait_ge(self.by_dve, c * len(self.dves) + self.dves.index(f) + 1)


def doubling_fills():
    fills = []
    for l in range(1, 7):
        fills += [(f"P{l}", 0), (f"P{l}", 1)]
        for g in range(2):
            fills += ([(f"X{l}", g)] if l < 6 else []) + [(f"XT{l}", g)]
    return fills


def doubling_bank(name):
    return 4 if name.startswith("XT") else 2 if name.startswith("X") else 0


def first_inverse(nc, b, link, MT, XT):
    def four(mask):
        return mask.rearrange("p (o s) -> p o s", o=1).broadcast_to([P, 4, P])

    link(nc.vector.tensor_tensor(XT, MT, four(b.level0T[:, :]), ALU.mult))
    return nc.vector.tensor_tensor(XT, XT, four(b.ident[:, :]), ALU.add)


def take_doubling(nc, b, name, g, bank, X, XT, PR):
    hs = slice(4 * g, 4 * g + 4)
    if name == "P6":
        return nc.vector.tensor_copy(PR[64:P, hs, 0:64], bank[64:P, :, 0:64])
    if name == "XT6":
        return nc.vector.tensor_tensor(XT[0:64, hs, 64:P], bank[0:64, :, 64:P], XT[0:64, hs, 64:P], ALU.add)
    if name[0] == "P":
        mask = b.level[:, int(name[1:]), :].rearrange("p (o s) -> p o s", o=1).broadcast_to([P, 4, P])
        return nc.vector.tensor_tensor(PR[:, hs, :], bank, mask, ALU.mult)
    dst = (XT if name.startswith("XT") else X)[:, hs, :]
    return nc.vector.tensor_tensor(dst, bank, dst, ALU.add)


def pe_doubling(nc, pe, order, c, bank_of, MT, X, XT, PR):
    for l in range(1, 7):
        for g in range(2):
            order.wait_taken(pe, c, ("X0", g) if l == 1 else (f"X{l - 1}", g))
            for i in range(4 * g, 4 * g + 4):
                o = bank_of("P", g)[:, P * (i % 4):P * (i % 4) + P]
                if l < 6:
                    last = nc.tensor.matmul(o, MT[:, i, :], X[:, i, :], start=True, stop=True)
                else:
                    last = nc.tensor.matmul(o[64:P, 0:64], MT[0:64, i, 64:P], X[0:64, i, 0:64], start=True, stop=True)
            last.then_inc(order.filled, 1)
        for g in range(2):
            order.wait_taken(pe, c, (f"P{l}", g))
            if l > 1:
                order.wait_taken(pe, c, (f"XT{l - 1}", g))
            if l < 6:
                for i in range(4 * g, 4 * g + 4):
                    last = nc.tensor.matmul(bank_of("X", g)[:, P * (i % 4):P * (i % 4) + P], XT[:, i, :], PR[:, i, :],
                                            start=True, stop=True)
                last.then_inc(order.filled, 1)
            for i in range(4 * g, 4 * g + 4):
                o = bank_of("XT", g)[:, P * (i % 4):P * (i % 4) + P]
                if l < 6:
                    last = nc.tensor.matmul(o, PR[:, i, :], XT[:, i, :], start=True, stop=True)
                else:
                    last = nc.tensor.matmul(o[0:64, 64:P], PR[64:P, i, 0:64], XT[64:P, i, 64:P], start=True, stop=True)
            last.then_inc(order.filled, 1)


def chunks(t):
    return t[:, :, :].rearrange("p a (c t) -> p a c t", c=NT)


class Even:

    def __init__(self, b, ctx):
        def sb(name, *shape):
            return b.sb(ctx, name, [P, *shape])

        self.w = sb("w_even", 2, KD, 512)
        in_ring = b.carver()
        self.hT = in_ring(KD, T)
        self.RKx = in_ring(8, T)
        self.R, self.K = self.RKx[:, 0:4, :], self.RKx[:, 4:8, :]
        self.xn = self.RKx[:, :, :].rearrange("p (i a) t -> p i (a t)", i=NT)
        self.V = in_ring(4, T)
        self.WA, self.GL = sb("WA", T), sb("GL", T)
        self.DEC, self.A, self.G, self.KK = (in_ring(4, T) for _ in range(4))
        self.BON = self.DEC
        self.TMP, self.TMP2 = sb("TMP", 4, T), in_ring(4, T)
        self.EP, self.EN, self.EA = in_ring(4, T), in_ring(4, T), sb("EA", 4, T)
        self.Q, self.F, self.I, self.GG = sb("Q", 4, T), sb("F", 4, T), sb("I", 4, T), sb("GG", 4, T)
        self.Vt = self.EP
        self.KH, self.LF, self.CB, self.QD, self.KD_ = self.F, self.KK, self.EN, self.KK, self.V
        self.EM, self.EL, self.ELM = sb("EM", 4, NT), sb("EL", 4, NT), sb("ELM", 4, NT)
        self.raw = flat(self.GG)[:, 0:2 * (T + 1)].rearrange("p (a t) -> p a t", a=2)
        self.lora2 = self.I[:, 0, :]
        self.g2 = self.I[:, 1, :]
        self.stat = sb("stat", 32)
        self.lb = sb("lb", 4)
        self.oml = sb("oml", 4)


def even_load(b, sp, m, n):
    c, width = EVEN_LOADS[n]
    w_in = b.dram["ev_w_in"][0].rearrange("(p k) n -> p k n", k=KD)
    sp.dma_start(m.w[:, n % 2, :, 0:width], w_in[:, :, c:c + width]).then_inc(b.sem(f"even_w_in{n % 2}"), 16)


def even_first_loads(b, sp, m):
    even_load(b, sp, m, 0)
    even_load(b, sp, m, 1)
    for dst, name in ((m.lora2[0:64, :], "rw_w2"), (m.lora2[64:128, :], "rw_a2"), (m.g2[:, :], "rw_g2")):
        sp.dma_start(dst, b.dram[name][0]).then_inc(b.sem("even_lora_in"), 16)


def even_project(b, m):
    nc, d = b.nc, b.dram

    items = [(kind, j) for kind in ("r", "k", "v") for j in range(4)] + [("wa", 0), ("gl", 0)]
    items += [(kind, j) for kind in ("q", "lw", "la", "lg", "f", "kk", "i", "bonus", "vt", "g") for j in range(4)]
    at = {it: n for n, it in enumerate(items)}
    by_dve = [at["bonus", j] for j in range(4)]
    loads = ["r", "k", "v", "wa", "q", "f", "i", "g"]
    last_of_load = [at[kind, 3] if kind != "wa" else at["gl", 0] for kind in loads]

    with nc.Block() as block:
        w_sem = [b.sem("even_w_in0"), b.sem("even_w_in1")]
        lora_sem = b.sem("even_lora_in")
        made, evac, evac_dve = b.sem("even_made"), b.sem("even_evac"), b.sem("even_evac_dve")
        mixed, kkr_ready, squares = b.sem("even_mixed"), b.sem("even_kkr"), b.sem("even_squares")
        lora_act, rk_ready, exponents = b.sem("even_lora_act"), b.sem("even_rk"), b.sem("even_exponents")
        r_decayed = b.sem("even_r_decayed")
        exps, ln_done = b.sem("even_exps"), b.sem("even_ln")

        def evacuated(eng, n):
            if n in by_dve:
                eng.wait_ge(evac_dve, by_dve.index(n) + 1)
            else:
                eng.wait_ge(evac, n + 1 - sum(x < n for x in by_dve))

        @block.sync
        def _(sp):
            for n in range(2, len(EVEN_LOADS)):
                sp.wait_ge(made, last_of_load[n - 2] + 1)
                even_load(b, sp, m, n)

        @block.tensor
        def _(pe):
            for n, (kind, j) in enumerate(items):
                bank = b.bank[n % 8][:, :]
                if n >= 8:
                    evacuated(pe, n - 8)
                if kind in ("r", "k", "v", "wa", "gl", "q", "f", "i", "g"):
                    load = loads.index("wa" if kind == "gl" else kind)
                    if j == 0:
                        pe.wait_ge(w_sem[load % 2], 16 * (load // 2 + 1))
                    w = m.w[:, load % 2, :, :]
                    jj = 1 if kind == "gl" else j
                    for k in range(KD):
                        if kind == "i":
                            last = nc.tensor.matmul(bank, m.hT[:, k, P * j:P * j + P], w[:, k, :],
                                                    start=(k == 0), stop=(k == KD - 1))
                        else:
                            last = nc.tensor.matmul(bank, w[:, k, P * jj:P * jj + P], m.hT[:, k, :],
                                                    start=(k == 0), stop=(k == KD - 1))
                elif kind == "lw":
                    pe.wait_ge(lora_sem, 48)
                    pe.wait_ge(lora_act, 1)
                    last = nc.tensor.matmul(bank, m.lora2[0:64, P * j:P * j + P], m.WA[0:64, :], start=True, stop=True)
                elif kind == "la":
                    last = nc.tensor.matmul(bank, m.lora2[64:128, P * j:P * j + P], m.WA[64:128, :],
                                            start=True, stop=True)
                elif kind == "lg":
                    pe.wait_ge(lora_act, 2)
                    last = nc.tensor.matmul(bank, m.g2[:, P * j:P * j + P], m.GL[:, :], start=True, stop=True)
                elif kind == "kk":
                    pe.wait_ge(squares, j + 1)
                    last = nc.tensor.matmul(bank, b.halves[:, :], m.TMP[:, j, :], start=True, stop=True)
                elif kind == "bonus":
                    pe.wait_ge(rk_ready, j + 1)
                    last = nc.tensor.matmul(bank, b.halves[:, :], m.TMP2[:, j, :], start=True, stop=True)
                elif kind == "vt":
                    pe.wait_ge(mixed, 12)
                    for c in range(NT):
                        last = nc.tensor.transpose(bank[:, P * c:P * c + P], m.V[:, j, P * c:P * c + P], b.ident[:, :])
                last.then_inc(made, 1)

        @block.scalar
        def _(act):
            def evacuate(n):
                kind, j = items[n]
                bank = b.bank[n % 8][:, :]
                act.wait_ge(made, n + 1)
                if n < 14:
                    if n >= 2:
                        act.wait_ge(mixed, n - 1)
                    ins = nc.scalar.activation(m.raw[:, n % 2, 1:T + 1], bank, ACT.Copy)
                elif kind in ("q", "g"):
                    ins = nc.scalar.activation((m.Q if kind == "q" else m.GG)[:, j, :], bank, ACT.Silu)
                elif kind == "f":
                    ins = nc.scalar.activation(m.F[:, j, :], bank, ACT.Sigmoid)
                elif kind == "lw":
                    ins = nc.scalar.activation(m.DEC[:, j, :], bank, ACT.Sigmoid, bias=b.col("rw_w0", j))
                elif kind == "la":
                    ins = nc.scalar.activation(m.A[:, j, :], bank, ACT.Sigmoid, bias=b.col("rw_a0", j))
                elif kind == "kk":
                    nc.scalar.activation(m.TMP[:, j, :], bank, ACT.Ln, bias=b.eps[:, 0:1]).then_inc(ln_done, 1)
                    act.wait_ge(ln_done, j + 1)
                    ins = nc.scalar.activation(m.TMP[:, j, :], m.TMP[:, j, :], ACT.Exp, scale=-0.5)
                elif kind == "vt":
                    act.wait_ge(r_decayed, 1)
                    ins = nc.scalar.activation(m.Vt[:, :, P * j:P * j + P],
                                               bank.rearrange("p (c f) -> p c f", c=NT), ACT.Copy)
                else:
                    ins = nc.scalar.activation((m.G if kind == "lg" else m.I)[:, j, :], bank, ACT.Copy)
                ins.then_inc(evac, 1)

            for n in range(at["q", 1]):
                evacuate(n)
            act.wait_ge(mixed, 13)
            nc.scalar.activation(m.WA[0:64, :], m.WA[0:64, :], ACT.Tanh).then_inc(lora_act, 1)
            act.wait_ge(mixed, 14)
            nc.scalar.activation(m.GL[:, :], m.GL[:, :], ACT.Sigmoid).then_inc(lora_act, 1)
            act.wait_ge(kkr_ready, 4)
            for j in range(4):
                nc.scalar.activation(m.TMP[:, j, :], m.KK[:, j, :], ACT.Square).then_inc(squares, 1)
            for n in range(at["q", 1], at["f", 0]):
                evacuate(n)
            act.wait_ge(exponents, 2)
            nc.scalar.activation(flat(m.EP), flat(m.EN), ACT.Exp, scale=-DECAY_RATE).then_inc(exps, 1)
            act.wait_ge(exps, 1)
            nc.scalar.activation(flat(m.EN), flat(m.EN), ACT.Exp, scale=DECAY_RATE).then_inc(exps, 1)
            nc.scalar.activation(flat(m.EA), flat(m.EA), ACT.Exp, scale=-DECAY_RATE).then_inc(exps, 1)
            nc.scalar.activation(m.EM[:, :, :], chunks(m.TMP2)[:, :, :, 63], ACT.Exp, scale=-DECAY_RATE).then_inc(exps, 1)
            nc.scalar.activation(m.EL[:, :, :], chunks(m.TMP2)[:, :, :, 127], ACT.Exp, scale=-DECAY_RATE).then_inc(exps, 1)
            nc.scalar.activation(m.ELM[:, :, :], chunks(m.EP)[:, :, :, 127], ACT.Copy).then_inc(exps, 1)
            for n in range(at["f", 0], len(items)):
                if n not in by_dve:
                    evacuate(n)

        @block.vector
        def _(dve):
            link = b.link(dve, "dve_steps")
            link(nc.vector.memset(m.raw[:, :, 0:1], 0.0))
            dsts = [m.R[:, j, :] for j in range(4)] + [m.K[:, j, :] for j in range(4)]
            dsts += [m.V[:, j, :] for j in range(4)] + [m.WA[:, :], m.GL[:, :]]
            for n, dst in enumerate(dsts):
                dve.wait_ge(evac, n + 1)
                raw = m.raw[:, n % 2, :]
                link(nc.vector.tensor_tensor(dst, raw[:, 0:T], raw[:, 1:T + 1], ALU.subtract))
                nc.vector.scalar_tensor_tensor(dst, dst, b.col("ev_mu", n), raw[:, 1:T + 1], ALU.mult,
                                               ALU.add).then_inc(mixed, 1)
                if 4 <= n < 8:
                    dve.wait_ge(mixed, n + 1)
                    nc.vector.tensor_scalar(m.KK[:, n - 4, :], dst, b.col("rw_k_k", n - 4), None,
                                            ALU.mult).then_inc(kkr_ready, 1)
            for j in range(4):
                evacuated(dve, at["lw", j])
                for c in range(NT):
                    last = nc.vector.tensor_tensor_scan(m.TMP2[:, j, P * c:P * c + P], b.ones[:, :],
                                                        m.DEC[:, j, P * c:P * c + P], 0.0, ALU.mult, ALU.add)
                link(last)
            middle = chunks(m.TMP2)[:, :, :, 63:64].broadcast_to([P, 4, NT, P])
            for j in range(4):
                last = nc.vector.tensor_tensor(chunks(m.EN)[:, j, :, :], chunks(m.TMP2)[:, j, :, :],
                                               middle[:, j, :, :], ALU.subtract)
            last.then_inc(exponents, 1)
            dve.wait_ge(exponents, 1)
            nc.vector.tensor_tensor(flat(m.EA), flat(m.EN), flat(m.DEC), ALU.subtract).then_inc(exponents, 1)
            evacuated(dve, at["la", 3])
            dve.wait_ge(exps, 6)
            for j in range(4):
                link(nc.vector.tensor_scalar(m.TMP2[:, j, :], m.A[:, j, :], 1.0, b.col("rw_k_a", j),
                                             ALU.subtract, ALU.mult))
                link(nc.vector.scalar_tensor_tensor(m.K[:, j, :], m.TMP2[:, j, :], 1.0, m.K[:, j, :],
                                                    ALU.add, ALU.mult))
                nc.vector.scalar_tensor_tensor(m.TMP2[:, j, :], m.R[:, j, :], b.col("rw_r_k", j), m.K[:, j, :],
                                               ALU.mult, ALU.mult).then_inc(rk_ready, 1)
            dve.wait_ge(rk_ready, 4)
            nc.vector.tensor_tensor(flat(m.R), flat(m.R), flat(m.EP), ALU.mult).then_inc(r_decayed, 1)
            nc.vector.tensor_tensor(flat(m.K), flat(m.K), flat(m.EN), ALU.mult)
            evacuated(dve, at["kk", 3])
            link(nc.vector.tensor_tensor(flat(m.KK), flat(m.KK), flat(m.TMP), ALU.mult))
            nc.vector.scalar_tensor_tensor(flat(m.EA), flat(m.KK), -1.0, flat(m.EA), ALU.mult, ALU.mult)
            link(nc.vector.tensor_tensor(flat(m.A), flat(m.A), flat(m.KK), ALU.mult))
            nc.vector.tensor_tensor(flat(m.A), flat(m.A), flat(m.EN), ALU.mult)
            for j in range(4):
                dve.wait_ge(made, at["bonus", j] + 1)
                nc.vector.tensor_tensor(m.BON[:, j, :], b.bank[at["bonus", j] % 8][:, :], m.V[:, j, :],
                                        ALU.mult).then_inc(evac_dve, 1)


EXP_TOP = 80.0


def rwkv_chunks(b, m):
    nc = b.nc
    w = m.w[:, :, :, :].rearrange("p a k n -> p (a k n)")

    def mats(i):
        return w[:, 8 * P * i:8 * P * (i + 1)].rearrange("p (h s) -> p h s", h=RW_H)

    MT, X, XT, PR, AkT, RbT, RkT = (mats(i) for i in range(7))
    Bs, SAs = w[:, 7 * 1024:7 * 1024 + 512], w[:, 7 * 1024 + 512:8 * 1024]
    Bt = m.hT[:, 0:4, :]
    Kt = m.hT[:, 4:8, :]
    Yt = m.Yt = m.TMP
    S = m.TMP2[:, 0, 0:256].rearrange("p (j v) -> p j v", j=4)
    SP = m.TMP2[:, 1, 0:256].rearrange("p (j v) -> p j v", j=4)
    NEW = m.TMP2[:, 2, 0:256].rearrange("p (j v) -> p j v", j=4)
    alpha, beta, k_, r_ = m.EA, m.A, m.K, m.R

    fills = [(name, g) for name in ("MT", "AkT", "RbT", "RkT", "X0") for g in range(2)] + doubling_fills()
    fills += [("B", 0), ("B", 1), ("SA", 0), ("Y", 0), ("Y", 1), ("dS", 0)]
    acts = [f for f in fills if f[0] in ("X0", "B", "SA", "Y")]
    dves = [f for f in fills if f not in acts]

    def bank_of(name, g):
        first = {"MT": 4, "AkT": 2, "RbT": 0, "RkT": 6, "X0": 2, "B": 6, "Y": 6, "SA": 0, "dS": 1}
        if name in first:
            return b.bank[first[name] + g]
        return b.bank[doubling_bank(name) + g]

    with nc.Block() as block:
        turned, turned_out = b.sem("rw_turned"), b.sem("rw_turned_out")
        filled, by_act, by_dve = b.sem("rw_filled"), b.sem("rw_by_act"), b.sem("rw_by_dve")
        first_x, state_ready = b.sem("rw_first_x"), b.sem("rw_state_ready")
        order = Order(fills, acts, dves, filled, by_act, by_dve)
        wait_filled, wait_taken = order.wait_filled, order.wait_taken
        bound_in, bound, logs_in, logs = (b.sem(f"hg_{x}") for x in ("bound_in", "bound", "logs_in", "logs"))
        block_in, block_exps = b.sem("hg_block_in"), b.sem("hg_block_exps")

        @block.tensor
        def _(pe):
            for i in range(8):
                for c in range(NT):
                    src = (beta if i < 4 else k_)[:, i % 4, P * c:P * c + P]
                    last = nc.tensor.transpose(b.bank[i][:, P * c:P * c + P], src, b.ident[:, :])
                last.then_inc(turned, 1)
            pe.wait_ge(turned_out, 8)
            for c in range(NT):
                tok = slice(P * c, P * c + P)

                def fm(t, g, i):
                    return t[64 * g:64 * g + 64, i, tok]

                def vt(g, i):
                    h = 2 * i + g
                    return m.Vt[:, c, 64 * h:64 * h + 64]

                before = {"RbT": (("SA", 0), ("dS", 0)), "AkT": (("X5", 0), ("X5", 1)),
                          "MT": (("XT6", 0), ("XT6", 1)), "RkT": (("Y", 0), ("Y", 1))}
                for name, left, right in (("MT", beta, alpha), ("AkT", k_, alpha), ("RbT", beta, r_), ("RkT", k_, r_)):
                    if c:
                        for f in before[name]:
                            wait_taken(pe, c - 1, f)
                    for i in range(4):
                        for g in range(2):
                            last = nc.tensor.matmul(bank_of(name, g)[:, P * i:P * i + P], fm(left, g, i),
                                                    fm(right, g, i), start=True, stop=True)
                            if i == 3:
                                last.then_inc(filled, 1)
                for g in range(2):
                    pe.wait_ge(first_x, 2 * c + g + 1)
                    wait_taken(pe, c, ("AkT", g))
                    for i in range(4):
                        last = nc.tensor.transpose(bank_of("X0", g)[:, P * i:P * i + P], XT[:, 4 * g + i, :], b.ident[:, :])
                    last.then_inc(filled, 1)
                wait_taken(pe, c, ("RbT", 0))
                wait_taken(pe, c, ("RbT", 1))
                pe_doubling(nc, pe, order, c, bank_of, MT, X, XT, PR)
                pe.wait_ge(state_ready, c + 1)
                wait_taken(pe, c, ("RkT", 0))
                wait_taken(pe, c, ("RkT", 1))
                for i in range(4):
                    for g in range(2):
                        nc.tensor.matmul(bank_of("B", g)[:, 64 * i:64 * i + 64], fm(alpha, g, i),
                                         SP[64 * g:64 * g + 64, i, :], start=True, stop=False)
                    for g in range(2):
                        last = nc.tensor.matmul(bank_of("B", g)[:, 64 * i:64 * i + 64], AkT[:, 4 * g + i, :], vt(g, i),
                                                start=False, stop=True)
                        if i == 3:
                            last.then_inc(filled, 1)
                wait_taken(pe, c, ("P6", 0))
                wait_taken(pe, c, ("XT6", 1))
                for g in range(2):
                    wait_taken(pe, c, ("B", g))
                    for i in range(4):
                        at = 64 * (4 * g + i)
                        last = nc.tensor.matmul(bank_of("SA", 0)[:, at:at + 64], XT[:, 4 * g + i, :], Bs[:, at:at + 64],
                                                start=True, stop=True)
                last.then_inc(filled, 1)
                wait_taken(pe, c, ("SA", 0))
                for i in range(4):
                    for g in range(2):
                        nc.tensor.matmul(bank_of("Y", g)[:, 64 * i:64 * i + 64], fm(r_, g, i),
                                         SP[64 * g:64 * g + 64, i, :], start=True, stop=False)
                    for g in range(2):
                        o = bank_of("Y", g)[:, 64 * i:64 * i + 64]
                        at = 64 * (4 * g + i)
                        nc.tensor.matmul(o, RkT[:, 4 * g + i, :], vt(g, i), start=False, stop=False)
                        last = nc.tensor.matmul(o, RbT[:, 4 * g + i, :], SAs[:, at:at + 64], start=False, stop=True)
                        if i == 3:
                            last.then_inc(filled, 1)
                for i in range(4):
                    for g in range(2):
                        h = 2 * i + g
                        at = 64 * (4 * g + i)
                        o = bank_of("dS", 0)[64 * g:64 * g + 64, 64 * i:64 * i + 64]
                        nc.tensor.matmul(o, Kt[:, c, 64 * h:64 * h + 64], vt(g, i), start=True, stop=False)
                        last = nc.tensor.matmul(o, Bt[:, c, 64 * h:64 * h + 64], SAs[:, at:at + 64],
                                                start=False, stop=True)
                last.then_inc(filled, 1)

        @block.scalar
        def _(act):
            for i in range(1, 8, 2):
                act.wait_ge(turned, i + 1)
                nc.scalar.activation((Bt if i < 4 else Kt)[:, :, P * (i % 4):P * (i % 4) + P],
                                     b.bank[i][:, :].rearrange("p (c f) -> p c f", c=NT), ACT.Copy).then_inc(turned_out, 1)
            act.wait_ge(bound_in, 1)
            nc.scalar.activation(m.lb[:, :], m.lb[:, :], ACT.Sigmoid).then_inc(bound, 1)
            for c in range(NT):
                if c == 1:
                    act.wait_ge(logs_in, 1)
                    nc.scalar.activation(flat(m.LF), flat(m.F), ACT.Ln).then_inc(logs, 1)
                if c == 3:
                    act.wait_ge(block_in, 1)
                    nc.scalar.activation(flat(m.QD), flat(m.QD), ACT.Exp).then_inc(block_exps, 1)
                    act.wait_ge(block_in, 2)
                    nc.scalar.activation(flat(m.KD_), flat(m.KD_), ACT.Exp).then_inc(block_exps, 1)
                for f in acts:
                    name, g = f
                    wait_filled(act, c, f)
                    bank = bank_of(name, g)
                    if name == "X0":
                        dst, src = X[:, 4 * g:4 * g + 4, :].rearrange("p h s -> p (h s)"), bank[:, :]
                    elif name == "B":
                        dst, src = Bs[:, 256 * g:256 * g + 256], bank[:, 0:256]
                    elif name == "SA":
                        dst, src = SAs, bank[:, :]
                    else:
                        dst = Yt[:, c, :].rearrange("p (i g v) -> p g i v", g=2, v=64)[:, g, :, :]
                        src = bank[:, 0:256].rearrange("p (i v) -> p i v", v=64)
                    nc.scalar.activation(dst, src, ACT.Copy).then_inc(by_act, 1)

        @block.vector
        def _(dve):
            link = b.link(dve, "dve_steps")
            for i in range(0, 8, 2):
                dve.wait_ge(turned, i + 1)
                nc.vector.tensor_copy((Bt if i < 4 else Kt)[:, :, P * (i % 4):P * (i % 4) + P],
                                      b.bank[i][:, :].rearrange("p (c f) -> p c f", c=NT)).then_inc(turned_out, 1)
            link(nc.vector.memset(S, 0.0))
            nc.vector.memset(SP, 0.0).then_inc(state_ready, 1)
            at = PAR_AT["hg_lb_logits"]
            nc.vector.tensor_tensor(m.lb[:, :], b.par[:, at:at + 4], b.par[:, at + 4:at + 8], ALU.subtract).then_inc(bound_in, 1)

            def hgrn_step(c):
                if c == 0:
                    dve.wait_ge(bound, 1)
                    link(nc.vector.tensor_scalar(m.oml[:, :], m.lb[:, :], -1.0, 1.0, ALU.mult, ALU.add))
                    for j in range(4):
                        last = nc.vector.tensor_scalar(m.F[:, j, :], m.F[:, j, :], m.oml[:, j:j + 1], m.lb[:, j:j + 1],
                                                       ALU.mult, ALU.add)
                    last.then_inc(logs_in, 1)
                if c == 1:
                    dve.wait_ge(logs, 1)
                    nc.vector.tensor_scalar(flat(m.KH), flat(m.F), -1.0, 1.0, ALU.mult, ALU.add)
                    for j in range(4):
                        for t in range(0, T, P):
                            last = nc.vector.tensor_tensor_scan(m.CB[:, j, t:t + P], b.ones[:, :], m.LF[:, j, t:t + P],
                                                                0.0, ALU.mult, ALU.add)
                    link(last)
                if c == 2:
                    difference = m.KD_
                    link(minus_at(nc, difference, m.CB, 32, 15))
                    nc.vector.tensor_scalar(flat(m.QD), flat(difference), EXP_TOP, None, ALU.min).then_inc(block_in, 1)
                    nc.vector.tensor_scalar(flat(m.KD_), flat(difference), -1.0, EXP_TOP, ALU.mult, ALU.min).then_inc(block_in, 1)
                if c == 3:
                    dve.wait_ge(block_exps, 2)
                    nc.vector.tensor_tensor(flat(m.QD), flat(m.QD), flat(m.Q), ALU.mult)
                    nc.vector.tensor_tensor(flat(m.KD_), flat(m.KD_), flat(m.KH), ALU.mult)

            def all_heads(mask):
                return mask.rearrange("p (o s) -> p o s", o=1).broadcast_to([P, 4, P])

            for c in range(NT):
                for f in dves:
                    name, g = f
                    bank = bank_of(name, g)
                    four = bank[:, :].rearrange("p (h s) -> p h s", h=4)
                    hs = slice(4 * g, 4 * g + 4)
                    wait_filled(dve, c, f)
                    if name == "dS":
                        link(nc.vector.tensor_tensor(NEW, bank[:, 0:256].rearrange("p (j v) -> p j v", j=4),
                                                     m.ELM[:, :, c:c + 1].broadcast_to([P, 4, 64]), ALU.mult))
                        link(nc.vector.tensor_tensor(S, S, m.EL[:, :, c:c + 1].broadcast_to([P, 4, 64]), ALU.mult))
                        nc.vector.tensor_tensor(S, S, NEW, ALU.add).then_inc(by_dve, 1)
                        if c + 1 < NT:
                            wait_taken(dve, c, f)
                            nc.vector.tensor_tensor(SP, S, m.EM[:, :, c + 1:c + 2].broadcast_to([P, 4, 64]),
                                                    ALU.mult).then_inc(state_ready, 1)
                        continue
                    if name in ("MT", "AkT"):
                        ins = nc.vector.tensor_tensor((MT if name == "MT" else AkT)[:, hs, :], four,
                                                      all_heads(b.before[:, :]), ALU.mult)
                    elif name in ("RbT", "RkT"):
                        ins = nc.vector.tensor_tensor((RbT if name == "RbT" else RkT)[:, hs, :], four,
                                                      all_heads(b.causal[:, :]), ALU.mult)
                    else:
                        ins = take_doubling(nc, b, name, g, four, X, XT, PR)
                    ins.then_inc(by_dve, 1)
                    if name == "MT":
                        wait_taken(dve, c, f)
                        first_inverse(nc, b, link, MT[:, hs, :], XT[:, hs, :]).then_inc(first_x, 1)
                    if name == "XT6" and g == 1:
                        hgrn_step(c)


def block_view(t, size):
    return flat(t).rearrange("p (n s) -> p n s", s=size)


def minus_at(nc, dst, sums, size, place):
    v = block_view(sums, size)
    return nc.vector.tensor_tensor(block_view(dst, size), v,
                                   v[:, :, place:place + 1].broadcast_to([P, 4 * T // size, size]), ALU.subtract)


def hgrn(b, m):
    nc, d = b.nc, b.dram
    w_out = d["ev_w_out"][0].rearrange("(k p) n -> p k n", p=P)
    KH, CB, QD, KD = m.KH, m.CB, m.QD, m.KD_
    S32, S64, QE, KE = m.EP, m.A, m.R, m.K
    KEt = m.hT[:, 0:4, :]
    AT = m.hT[:, 4:8, :].rearrange("p (two a) (i s) -> p two (a i) s", two=2, s=P)
    S = m.WA[:, 0:256].rearrange("p (i v) -> p i v", i=4)
    Ot = m.K
    m.YB = m.F
    Yt = m.Yt
    m.YA = m.EA
    y3 = flat(Yt).rearrange("p (g v) -> p g v", v=64)
    mean, var = m.GL[:, 0:32], m.GL[:, 32:64]
    y_squares = m.TMP2
    EL = m.EL
    sq, ss = m.TMP2, m.stat[:, :]

    with nc.Block() as block:
        exponent, exped, factors, ke_ready = (b.sem(f"hg_{x}") for x in ("exponent", "exped", "factors", "ke_ready"))
        turned, turned_out, zeroed = (b.sem(f"hg_{x}") for x in ("turned", "turned_out", "zeroed"))
        at_made, at_taken, o_made, o_taken = (b.sem(f"hg_{x}") for x in ("at_made", "at_taken", "o_made", "o_taken"))
        ds_made, state = b.sem("hg_ds_made"), b.sem("hg_state")
        squared, var_in, var_out, normed, y_turned = (b.sem(f"hg_{x}") for x in ("sq", "var_in", "var_out", "normed", "yt"))
        y_centred, y_squared, y_var_in, y_var_out, y_normed, ya_turned, ya_ready = (
            b.sem(f"rwo_{x}") for x in ("centred", "squared", "var_in", "var_out", "normed", "turned", "ready"))
        w_out_in = b.sem("even_w_out_in")

        @block.sync
        def _(sp):
            for i in range(2):
                sp.dma_start(m.w[:, i, :, :], w_out[:, :, 512 * i:512 * i + 512]).then_inc(w_out_in, 16)

        @block.scalar
        def _(act):
            nc.scalar.activation(flat(QE), flat(CB), ACT.Exp).then_inc(exped, 1)
            act.wait_ge(exponent, 1)
            nc.scalar.activation(flat(KE), flat(KE), ACT.Exp, scale=-1.0).then_inc(exped, 1)
            for n, (t, size) in enumerate(((S32, 64), (S64, 128))):
                act.wait_ge(exponent, 2 + n)
                v = block_view(t, size)
                nc.scalar.activation(v[:, :, 0:size // 2], v[:, :, 0:size // 2], ACT.Exp, scale=-1.0).then_inc(exped, 1)
                nc.scalar.activation(v[:, :, size // 2:size], v[:, :, size // 2:size], ACT.Exp).then_inc(exped, 1)
            nc.scalar.activation(EL[:, :, :], chunks(CB)[:, :, :, 127], ACT.Exp).then_inc(exped, 1)
            for j in range(4):
                act.wait_ge(turned, j + 1)
                nc.scalar.activation(KEt[:, :, P * j:P * j + P], b.bank[6 + j % 2][:, :].rearrange("p (c f) -> p c f", c=NT),
                                     ACT.Copy).then_inc(turned_out, 1)
            for c in range(NT):
                for g in range(2):
                    act.wait_ge(o_made, 2 * c + g + 1)
                    nc.scalar.activation(Ot[:, c, :].rearrange("p (i g v) -> p g i v", g=2, v=64)[:, g, :, :],
                                         b.bank[4 + g][:, 0:256].rearrange("p (i v) -> p i v", v=64),
                                         ACT.Copy).then_inc(o_taken, 1)
                if c == 1:
                    act.wait_ge(y_centred, 1)
                    nc.scalar.activation(flat(y_squares), flat(Yt), ACT.Square).then_inc(y_squared, 1)
                if c == 2:
                    act.wait_ge(y_var_in, 1)
                    nc.scalar.activation(var, var, ACT.Sqrt).then_inc(y_var_out, 1)
            act.wait_ge(o_taken, 2 * NT)
            nc.scalar.activation(flat(sq), flat(Ot), ACT.Square).then_inc(squared, 1)
            act.wait_ge(var_in, 1)
            nc.scalar.activation(ss, ss, ACT.Sqrt).then_inc(var_out, 1)

        @block.vector
        def _(dve):
            link = b.link(dve, "dve_steps")
            for i in range(4):
                last = nc.vector.memset(b.bank[i][:, :], 0.0)
            last.then_inc(zeroed, 1)
            nc.vector.memset(S, 0.0).then_inc(state, 1)
            minus_at(nc, KE, CB, 128, 127).then_inc(exponent, 1)
            minus_at(nc, S32, CB, 64, 31).then_inc(exponent, 1)
            minus_at(nc, S64, CB, 128, 63).then_inc(exponent, 1)
            dve.wait_ge(exped, 2)
            nc.vector.tensor_tensor(flat(KE), flat(KE), flat(KH), ALU.mult).then_inc(ke_ready, 1)
            for n, (t, size) in enumerate(((S32, 64), (S64, 128))):
                v, q, k = block_view(t, size), block_view(m.Q, size), block_view(KH, size)
                dve.wait_ge(exped, 3 + 2 * n)
                nc.vector.tensor_tensor(v[:, :, 0:size // 2], v[:, :, 0:size // 2], k[:, :, 0:size // 2], ALU.mult)
                dve.wait_ge(exped, 4 + 2 * n)
                nc.vector.tensor_tensor(v[:, :, size // 2:], v[:, :, size // 2:], q[:, :, size // 2:],
                                        ALU.mult).then_inc(factors, 1)
            mask = b.causal[:, :].rearrange("p (o s) -> p o s", o=1).broadcast_to([P, 4, P])

            def take_weights(c):
                for g in range(2):
                    dve.wait_ge(at_made, c + 1)
                    if c >= 2:
                        dve.wait_ge(ds_made, c - 1)
                    nc.vector.tensor_tensor(AT[:, c % 2, 4 * g:4 * g + 4, :],
                                            b.bank[2 * (c % 2) + g][:, :].rearrange("p (i s) -> p i s", i=4), mask,
                                            ALU.mult).then_inc(at_taken, 1)

            def by_head(t):
                return t.rearrange("p (g o) -> p g o", o=1).broadcast_to([P, 32, 64])

            def rwkv_norm_step(c):
                if c == 0:
                    link(nc.vector.reduce_sum(mean, y3, AX.X))
                    link(nc.vector.tensor_scalar(mean, mean, 1.0 / 64, None, ALU.mult))
                if c == 1:
                    nc.vector.tensor_tensor(y3, y3, by_head(mean), ALU.subtract).then_inc(y_centred, 1)
                if c == 2:
                    dve.wait_ge(y_squared, 1)
                    link(nc.vector.reduce_sum(var, flat(y_squares).rearrange("p (g v) -> p g v", v=64), AX.X))
                    nc.vector.tensor_scalar(var, var, 1.0 / 64, RW_LN_EPS, ALU.mult, ALU.add).then_inc(y_var_in, 1)
                if c == 3:
                    dve.wait_ge(y_var_out, 1)
                    link(nc.vector.reciprocal(var, var))
                    nc.vector.tensor_tensor(y3, y3, by_head(var), ALU.mult).then_inc(y_normed, 1)

            take_weights(0)
            nc.vector.tensor_tensor(flat(QE), flat(QE), flat(m.Q), ALU.mult).then_inc(factors, 1)
            dve.wait_ge(exped, 7)
            for c in range(NT):
                if c + 1 < NT:
                    take_weights(c + 1)
                rwkv_norm_step(c)
                dve.wait_ge(ds_made, c + 1)
                link(nc.vector.tensor_tensor(S, S, EL[:, :, c:c + 1].broadcast_to([P, 4, 64]), ALU.mult))
                nc.vector.tensor_tensor(S, S, b.bank[6][:, 0:256].rearrange("p (i v) -> p i v", i=4),
                                        ALU.add).then_inc(state, 1)
                dve.wait_ge(state, c + 2)
            for j in range(4):
                dve.wait_ge(ya_turned, j + 1)
                link(nc.vector.tensor_scalar(m.YA[:, j, :], b.bank[j][:, :], b.col("rw_ln_w", j), b.col("rw_ln_b", j),
                                             ALU.mult, ALU.add))
                link(nc.vector.tensor_tensor(m.YA[:, j, :], m.YA[:, j, :], m.BON[:, j, :], ALU.add))
                nc.vector.tensor_tensor(m.YA[:, j, :], m.YA[:, j, :], m.G[:, j, :], ALU.mult).then_inc(ya_ready, 1)
            dve.wait_ge(squared, 1)
            ss32 = ss.rearrange("p (g o) -> p g o", o=1)
            link(nc.vector.reduce_sum(ss, flat(sq).rearrange("p (g v) -> p g v", v=64), AX.X))
            nc.vector.tensor_scalar(ss, ss, 1.0 / 64, NORM_EPS, ALU.mult, ALU.add).then_inc(var_in, 1)
            dve.wait_ge(var_out, 1)
            link(nc.vector.reciprocal(ss, ss))
            o3 = flat(Ot).rearrange("p (g v) -> p g v", v=64)
            nc.vector.tensor_tensor(o3, o3, ss32.broadcast_to([P, 32, 64]), ALU.mult).then_inc(normed, 1)
            for j in range(4):
                dve.wait_ge(y_turned, j + 1)
                nc.vector.scalar_tensor_tensor(m.YB[:, j, :], b.bank[j][:, :], b.col("hg_norm"), m.GG[:, j, :],
                                               ALU.mult, ALU.mult)

        @block.tensor
        def _(pe):
            pe.wait_ge(ke_ready, 1)
            for j in range(4):
                if j >= 2:
                    pe.wait_ge(turned_out, j - 1)
                for c in range(NT):
                    last = nc.tensor.transpose(b.bank[6 + j % 2][:, P * c:P * c + P], KE[:, j, P * c:P * c + P], b.ident[:, :])
                last.then_inc(turned, 1)

            def weights(c):
                if c >= 2:
                    pe.wait_ge(at_taken, 2 * (c - 1))
                banks = [b.bank[2 * (c % 2) + g] for g in range(2)]

                def square(t_left, t_right, i, g, s0, t0, size):
                    rows = slice(64 * g, 64 * g + 64)
                    return nc.tensor.matmul(banks[g][s0:s0 + size, P * i + t0:P * i + t0 + size],
                                            t_left[rows, i, P * c + s0:P * c + s0 + size],
                                            t_right[rows, i, P * c + t0:P * c + t0 + size], start=True, stop=True)

                for i in range(4):
                    for g in range(2):
                        for s0 in range(0, P, 32):
                            square(KD, QD, i, g, s0, s0, 32)
                        for s0 in (0, 64):
                            square(S32, S32, i, g, s0, s0 + 32, 32)
                for i in range(4):
                    for g in range(2):
                        last = square(S64, S64, i, g, 0, 64, 64)
                last.then_inc(at_made, 1)

            pe.wait_ge(zeroed, 1)
            pe.wait_ge(factors, 2)
            weights(0)
            pe.wait_ge(turned_out, 4)
            pe.wait_ge(factors, 3)
            for c in range(NT):
                if c + 1 < NT:
                    weights(c + 1)
                pe.wait_ge(at_taken, 2 * c + 2)
                pe.wait_ge(state, c + 1)
                if c:
                    pe.wait_ge(o_taken, 2 * c)
                for i in range(4):
                    for g in range(2):
                        nc.tensor.matmul(b.bank[4 + g][:, 64 * i:64 * i + 64], QE[64 * g:64 * g + 64, i, P * c:P * c + P],
                                         S[64 * g:64 * g + 64, i, :], start=True, stop=False)
                    for g in range(2):
                        h = 2 * i + g
                        last = nc.tensor.matmul(b.bank[4 + g][:, 64 * i:64 * i + 64], AT[:, c % 2, 4 * g + i, :],
                                                m.I[:, c, 64 * h:64 * h + 64], start=False, stop=True)
                        if i == 3:
                            last.then_inc(o_made, 1)
                for i in range(4):
                    for g in range(2):
                        h = 2 * i + g
                        last = nc.tensor.matmul(b.bank[6][64 * g:64 * g + 64, 64 * i:64 * i + 64],
                                                KEt[:, c, 64 * h:64 * h + 64], m.I[:, c, 64 * h:64 * h + 64],
                                                start=True, stop=True)
                last.then_inc(ds_made, 1)
            pe.wait_ge(o_taken, 2 * NT)
            pe.wait_ge(state, NT + 1)
            pe.wait_ge(y_normed, 1)
            for j in range(4):
                for c in range(NT):
                    last = nc.tensor.transpose(b.bank[j][:, P * c:P * c + P], Yt[:, c, P * j:P * j + P], b.ident[:, :])
                last.then_inc(ya_turned, 1)
            pe.wait_ge(ya_ready, 4)
            project_out_early(b, pe, m.w, w_out_in, lambda k: m.YA[:, k, :])
            pe.wait_ge(normed, 1)
            for j in range(4):
                for c in range(NT):
                    last = nc.tensor.transpose(b.bank[j][:, P * c:P * c + P], Ot[:, c, P * j:P * j + P], b.ident[:, :])
                last.then_inc(y_turned, 1)


def project_out_early(b, pe, w, w_in, y):
    pe.wait_ge(w_in, 32)
    for i in range(NT):
        for k in range(KD // 2):
            b.nc.tensor.matmul(b.bank[4 + i][:, :], y(k)[:, P * i:P * i + P], w[:, 1, k, :], start=(k == 0), stop=False)


def project_out(b, layer, w, w_in, y, waste):
    nc = b.nc
    with nc.Block() as block:
        made, added, squared = (b.sem(f"out_{x}") for x in ("made", "added", "squared"))

        @block.sync
        def _(sp):
            first_experts(b, sp, layer)

        @block.tensor
        def _(pe):
            pe.wait_ge(w_in, 32)
            for n in range(2):
                for i in range(NT):
                    for k in range(KD // 2 * n, KD):
                        last = nc.tensor.matmul(b.bank[4 * n + i][:, :], y(k)[:, P * i:P * i + P], w[:, n, k, :],
                                                start=(k == 0), stop=(k == KD - 1))
                    last.then_inc(made, 1)

        @block.vector
        def _(dve):
            for n in range(2):
                for i in range(NT):
                    dve.wait_ge(made, 4 * n + i + 1)
                    part = b.h[:, i, 512 * n:512 * n + 512]
                    nc.vector.tensor_tensor(part, part, b.bank[4 * n + i][:, :], ALU.add).then_inc(added, 1)

        @block.scalar
        def _(act):
            for i in range(NT):
                act.wait_ge(added, NT + i + 1)
                if i:
                    act.wait_ge(squared, i)
                square_tile(b, i, waste).then_inc(squared, 1)


def even_layer(b):
    with ExitStack() as ctx:
        m = Even(b, ctx)
        norm_into(b, "mix0", PAR_AT["norm_mix"], m.xn, m.hT, lambda sp: even_first_loads(b, sp, m))
        even_project(b, m)
        rwkv_chunks(b, m)
        hgrn(b, m)
        project_out(b, 0, m.w, b.sem("even_w_out_in"), lambda k: (m.YA if k < 4 else m.YB)[:, k % 4, :],
                    flat(m.TMP)[:, 0:D])


NW = 4 + E


def expert_places(b):
    in_ring = b.carver()
    gate, up, down = (in_ring(RING, KD * DE) for _ in range(3))
    return (gate.rearrange("p s (k f) -> p s k f", k=KD), up.rearrange("p s (k f) -> p s k f", k=KD),
            down.rearrange("p s (j n) -> p s j n", j=2))


def expert_weights(b, layer, e):
    d = b.dram
    return (d["moe_w_gate"][layer, e].rearrange("(p k) f -> p k f", k=KD),
            d["moe_w_up"][layer, e].rearrange("(p k) f -> p k f", k=KD),
            d["moe_w_down"][layer, e].rearrange("(j p) n -> p j n", p=P))


def first_experts(b, sp, layer):
    b.arrived[layer] = [[b.nc.alloc_semaphore(name=f"moe{layer}_{n}{s}_in") for n in ("gate", "up", "down")]
                        for s in range(RING)]
    places = expert_places(b)
    for s in range(RING):
        for part, src in enumerate(expert_weights(b, layer, s)):
            sp.dma_start(places[part][:, s], src).then_inc(b.arrived[layer][s][part], 16)


def moe(b, layer):
    nc, d = b.nc, b.dram
    tag = f"moe{layer}"
    sem = lambda name: b.sem(f"{tag}_{name}")
    with ExitStack() as ctx:
        def sb(name, *shape, dt=F32):
            return b.sb(ctx, f"{tag}_{name}", [P, *shape], dt)

        xn, hT = sb("xn", NT, D), sb("hT", KD, T)
        w_gate, w_up, w_down = expert_places(b)
        xs = sb("xs", KD, SLOTS + WIN)
        spare = sb("spare", 4, D)
        staged = [hT[:, 2 * n:2 * n + 2, :].rearrange("p a t -> p (a t)") for n in range(4)] + [spare[:, n, :] for n in range(4)]
        def routing(k, at, rows, cols):
            return xs[:, k, at:at + rows * cols].rearrange("p (r c) -> p r c", r=rows)

        router, bias = routing(1, 0, KD, NW), sb("bias", NW)
        logits, scores = routing(2, 0, NT, NW), xs[:, 5, 0:T]
        windows_int = xs[:, 4, 0:2 * E].bitcast(I32)
        fine, key, one1, one2 = (routing(3, NT * E * i, NT, E) for i in range(4))
        both = xs[:, 6, 0:NT * E // 2].bitcast(BF16).rearrange("p (i e) -> p i e", i=NT)
        before, ones = (xs[:, 6, 128 * n:128 * n + P // 2].bitcast(BF16) for n in (1, 2))
        rev = sb("rev", E)
        gmax, gsum, gone, best1, best2 = (sb(n, NT) for n in ("gmax", "gsum", "gone", "best1", "best2"))
        gexp, grp = sb("gexp", NT, GROUPS), sb("grp", NT, GROUPS)
        e2, gate1, gate2, slot1, slot2, kmax = (sb(n, NT) for n in ("e2", "gate1", "gate2", "slot1", "slot2", "kmax"))
        count, incl, off = sb("count", E), sb("incl", E), sb("off", E)
        edges, over = sb("edges", 8), sb("over", E, 8)
        jump, total, windows = sb("jump", E), sb("total", 1), sb("windows", 2 * E)
        table_f, table = sb("table_f", 5 * E), sb("table", 5 * E, dt=I32)
        CNT, BASE, START, TOTAL = 0, E, 2 * E, 4 * E
        x_rows = nc.dram_tensor(f"{tag}_x_rows", (SLOTS, D), F32, kind="Internal").ap()
        rows = nc.dram_tensor(f"{tag}_rows", (SLOTS + WIN, D), F32, kind="Internal").ap()
        silu, hid = spare[:, 0, 0:P], spare[:, 0, P:2 * P]
        xw = spare[:, 1, 0:KD * WIN].rearrange("p (k s) -> p k s", k=KD)
        hid_T = spare[:, 0, 2 * P:3 * P].rearrange("p (f s) -> p f s", f=2)
        y = spare[:, 2, :].rearrange("p (b c) -> p b c", b=2)
        slot_rows = sb("slot_rows", 2 * NT, dt=U32)
        gains = b.par[:, PAR_AT["norm_ffn"] + 8 * layer:PAR_AT["norm_ffn"] + 8 * layer + 8]

        arrived = b.arrived[layer]
        router_in = sem("router_in")
        def first_loads(sp):
            sp.dma_start(router[:, :, 0:GROUPS], d["moe_w_group"][layer].rearrange("(p k) n -> p k n", k=KD)).then_inc(router_in, 16)
            sp.dma_start(router[:, :, GROUPS:NW], d["moe_w_router"][layer].rearrange("(p k) n -> p k n", k=KD)).then_inc(router_in, 16)
            for name, c, width in (("moe_b_group", 0, GROUPS), ("moe_b_router", GROUPS, E)):
                sp.dma_start(bias[:, c:c + width],
                             d[name][layer].rearrange("(o n) -> o n", o=1).broadcast_to([P, width])).then_inc(router_in, 16)

        norm_into(b, tag, PAR_AT["norm_ffn"] + 8 * layer, xn, hT, first_loads)
        with nc.Block() as block:
            ids, scored, turned_in, exps, ranked = (sem(n) for n in ("ids", "scored", "turned_in", "exps", "ranked"))
            chosen, e1 = sem("chosen"), sem("e1")
            low_out, high_out, masks = sem("low_out"), sem("high_out"), sem("masks")
            sorted_, rows_known, turned_tile, evacuated, tile_in = (
                sem("sorted"), sem("rows_known"), sem("turned_tile"), sem("evacuated"), [sem(f"tile{n}_in") for n in range(8)])

            @block.sync
            def _(sp):
                sp.wait_ge(sorted_, 16 * 2 * NT)
                for n in range(8):
                    sp.dma_start(staged[n], x_rows[P * n:P * n + P, :]).then_inc(tile_in[n], 16)

            @block.gpsimd
            def _(pool):
                nc.gpsimd.iota(key[:, 0, :].bitcast(I32), [[-1, E]], base=E, channel_multiplier=0).then_inc(ids, 1)
                nc.gpsimd.iota(key[:, 1, 0:8].bitcast(I32), [[WIN, 8]], base=0, channel_multiplier=0).then_inc(ids, 1)
                nc.gpsimd.iota(windows_int, [[1, 2 * E]], base=0, channel_multiplier=0).then_inc(ids, 1)
                nc.gpsimd.tensor_copy(before, b.before[:, :]).then_inc(masks, 1)
                nc.gpsimd.tensor_copy(ones, b.ones[:, :]).then_inc(masks, 1)
                pool.wait_ge(rows_known, 2)
                for which in range(2):
                    for i in range(NT):
                        slot = slot_rows[:, NT * which + i:NT * which + i + 1]
                        nc.gpsimd.indirect_dma_start(x_rows, bass.IndirectOffsetOnAxis(slot, 0), xn[:, i, :], None).then_inc(sorted_, 16)

            @block.tensor
            def _(pe):
                pe.wait_ge(router_in, 64)
                for k in range(KD // 2):
                    for half in range(2):
                        last = nc.tensor.matmul(b.bank[2 + half][64 * half:64 * half + NW, :], router[:, 4 * half + k, :],
                                                hT[:, 4 * half + k, :], start=(k == 0), stop=(k == KD // 2 - 1))
                        if k == KD // 2 - 1:
                            last.then_inc(scored, 1)
                pe.wait_ge(high_out, 1)
                for i in range(NT):
                    last = nc.tensor.transpose(b.bank[0][:, NW * i:NW * i + NW], scores[0:NW, P * i:P * i + P], b.ident[0:NW, 0:NW])
                last.then_inc(turned_in, 1)
                pe.wait_ge(masks, 2)
                pe.wait_ge(chosen, 1)
                for i in range(NT):
                    for n in range(i + 1):
                        nc.tensor.matmul(b.bank[1][:, E * i:E * i + E], before if n == i else ones, both[:, n, :],
                                         start=(n == 0), stop=(n == i))
                for n in range(NT):
                    last = nc.tensor.matmul(b.bank[1][:, E * NT:E * NT + E], ones, both[:, n, :],
                                            start=(n == 0), stop=(n == NT - 1))
                last.then_inc(ranked, 1)
                for n in range(8):
                    pe.wait_ge(tile_in[n], 16)
                    for half in range(2):
                        item = 2 * n + half
                        if item >= 6:
                            pe.wait_ge(evacuated, item - 5)
                        for q in range(4):
                            last = nc.tensor.transpose(b.bank[2 + item % 6][:, P * q:P * q + P],
                                                       staged[n].rearrange("p (q k) -> p k q", k=KD)[:, 4 * half + q, :], b.ident[:, :])
                        last.then_inc(turned_tile, 1)

            @block.scalar
            def _(act):
                act.wait_ge(scored, 2)
                nc.scalar.activation(scores[0:NW, :], b.bank[2][0:NW, :], ACT.Copy).then_inc(low_out, 1)
                act.wait_ge(e1, 1)
                nc.scalar.activation(gexp[:, :, :], gexp[:, :, :], ACT.Exp).then_inc(exps, 1)
                act.wait_ge(e1, 2)
                nc.scalar.activation(e2[:, :], e2[:, :], ACT.Exp).then_inc(exps, 1)

            @block.vector
            def _(dve):
                link = b.link(dve, "dve_steps")
                V = nc.vector

                def spread(t, n):
                    return t[:, :].rearrange("p (i o) -> p i o", o=1).broadcast_to([P, NT, n])

                def over_tiles(t, n):
                    return t.rearrange("p (o e) -> p o e", o=1).broadcast_to([P, NT, n])

                dve.wait_ge(ids, 3)
                V.tensor_copy(windows[:, :], windows_int)
                V.tensor_copy(rev[:, :], key[:, 0, :].bitcast(I32))
                link(V.tensor_copy(edges[:, :], key[:, 1, 0:8].bitcast(I32)))
                link(V.tensor_scalar(edges[:, 0:1], edges[:, 0:1], 1.0, None, ALU.subtract))
                dve.wait_ge(low_out, 1)
                V.tensor_tensor(scores[0:NW, :], scores[0:NW, :], b.bank[3][64:64 + NW, :], ALU.add).then_inc(high_out, 1)
                dve.wait_ge(turned_in, 1)
                link(V.tensor_tensor(logits[:, :, :], b.bank[0][:, 0:NT * NW].rearrange("p (i n) -> p i n", i=NT),
                                     over_tiles(bias[:, :], NW), ALU.add))
                groups = logits[:, :, 0:GROUPS]
                link(V.reduce_max(gmax[:, :], groups, AX.X))
                V.tensor_tensor(gexp[:, :, :], groups, spread(gmax, GROUPS), ALU.subtract).then_inc(e1, 1)

                def first_of_largest(dst, values, largest, keys, n):
                    link(V.tensor_tensor(keys, values, spread(largest, n), ALU.is_equal))
                    link(V.tensor_tensor(keys, keys, over_tiles(rev[:, 0:n], n), ALU.mult))
                    link(V.reduce_max(kmax[:, :], keys, AX.X))
                    link(V.tensor_tensor(dst, keys, spread(kmax, n), ALU.is_equal))

                first_of_largest(grp[:, :, :], groups, gmax, key[:, :, 0:GROUPS], GROUPS)
                link(V.tensor_scalar(grp[:, :, :], grp[:, :, :], 1.0, BIG, ALU.subtract, ALU.mult))
                link(V.tensor_tensor(fine[:, :, :].rearrange("p i (g e) -> p i g e", g=GROUPS),
                                     logits[:, :, GROUPS:NW].rearrange("p i (g e) -> p i g e", g=GROUPS),
                                     grp[:, :, :].rearrange("p i (g o) -> p i g o", o=1).broadcast_to([P, NT, GROUPS, EPG]),
                                     ALU.add))
                link(V.reduce_max(best1[:, :], fine[:, :, :], AX.X))
                first_of_largest(one1[:, :, :], fine[:, :, :], best1, key[:, :, :], E)
                link(V.scalar_tensor_tensor(fine[:, :, :], one1[:, :, :], -2.0 * BIG, fine[:, :, :], ALU.mult, ALU.add))
                link(V.reduce_max(best2[:, :], fine[:, :, :], AX.X))
                V.tensor_tensor(e2[:, :], best2[:, :], best1[:, :], ALU.subtract).then_inc(e1, 1)
                first_of_largest(one2[:, :, :], fine[:, :, :], best2, key[:, :, :], E)
                V.tensor_tensor(both[:, :, :], one1[:, :, :], one2[:, :, :], ALU.add).then_inc(chosen, 1)
                dve.wait_ge(ranked, 1)
                link(V.tensor_copy(count[:, :], b.bank[1][:, E * NT:E * NT + E]))
                link(V.tensor_tensor_scan(incl[:, :], b.ones[:, 0:E], count[:, :], 0.0, ALU.mult, ALU.add))
                link(V.tensor_tensor(off[:, :], incl[:, :], count[:, :], ALU.subtract))
                link(V.tensor_tensor(fine[:, :, :], b.bank[1][:, 0:E * NT].rearrange("p (i e) -> p i e", i=NT),
                                     over_tiles(off[:, :], E), ALU.add))
                for one, slot in ((one1, slot1), (one2, slot2)):
                    link(V.tensor_tensor(key[:, :, :], one[:, :, :], fine[:, :, :], ALU.mult))
                    link(V.reduce_sum(slot[:, :], key[:, :, :], AX.X))
                for which, slot in enumerate((slot1, slot2)):
                    V.tensor_copy(slot_rows[:, NT * which:NT * which + NT], slot[:, :]).then_inc(rows_known, 1)
                link(V.tensor_tensor(over[:, :, :], count[:, :].rearrange("p (e o) -> p e o", o=1).broadcast_to([P, E, 8]),
                                     edges[:, :].rearrange("p (o j) -> p o j", o=1).broadcast_to([P, E, 8]), ALU.is_gt))
                link(V.reduce_sum(table_f[:, CNT:CNT + E], over[:, :, :], AX.X))
                link(V.tensor_tensor_scan(incl[:, :], b.ones[:, 0:E], table_f[:, CNT:CNT + E], 0.0, ALU.mult, ALU.add))
                V.tensor_copy(total[:, :], incl[:, E - 1:E])
                link(V.tensor_tensor(table_f[:, BASE:BASE + E], incl[:, :], table_f[:, CNT:CNT + E], ALU.subtract))
                link(V.scalar_tensor_tensor(jump[:, :], table_f[:, BASE:BASE + E], -float(WIN), off[:, :], ALU.mult, ALU.add))
                link(V.tensor_tensor(incl[:, 1:E], jump[:, 1:E], jump[:, 0:E - 1], ALU.subtract))
                reached = xs[:, :, :].rearrange("p k s -> p (k s)")[:, 0:2 * E * E].rearrange("p (w e) -> p w e", w=2 * E)

                def over_windows(t):
                    return t.rearrange("p (o e) -> p o e", o=1).broadcast_to([P, 2 * E, E])

                link(V.tensor_tensor(reached, windows[:, :].rearrange("p (w o) -> p w o", o=1).broadcast_to([P, 2 * E, E]),
                                     over_windows(table_f[:, BASE:BASE + E]), ALU.is_ge))
                V.tensor_copy(table_f[:, TOTAL:TOTAL + 1], total[:, :])
                link(V.tensor_copy(incl[:, 0:1], jump[:, 0:1]))
                link(V.tensor_tensor(reached, reached, over_windows(incl[:, :]), ALU.mult))
                link(V.reduce_sum(table_f[:, START:START + 2 * E], reached, AX.X))
                link(V.scalar_tensor_tensor(table_f[:, START:START + 2 * E], windows[:, :], float(WIN),
                                            table_f[:, START:START + 2 * E], ALU.mult, ALU.add))
                V.tensor_copy(table[:, 0:TOTAL + 1], table_f[:, 0:TOTAL + 1])
                V.memset(xs[:, :, SLOTS:], 0.0)
                for n in range(8):
                    for half in range(2):
                        item = 2 * n + half
                        dve.wait_ge(turned_tile, item + 1)
                        V.tensor_tensor(xs[:, 4 * half:4 * half + 4, P * n:P * n + P],
                                        b.bank[2 + item % 6].rearrange("p (q s) -> p q s", q=4),
                                        gains[:, 4 * half:4 * half + 4].rearrange("p (q o) -> p q o", o=1).broadcast_to([P, 4, P]),
                                        ALU.mult).then_inc(evacuated, 1)
                dve.wait_ge(exps, 2)
                link(V.reduce_sum(gsum[:, :], gexp[:, :, :], AX.X))
                link(V.tensor_scalar(gone[:, :], e2[:, :], 1.0, None, ALU.add))
                link(V.tensor_tensor(gone[:, :], gone[:, :], gsum[:, :], ALU.mult))
                link(V.reciprocal(gate1[:, :], gone[:, :]))
                link(V.tensor_tensor(gate2[:, :], gate1[:, :], e2[:, :], ALU.mult))

        with nc.Block() as block:
            xw_ready, gate_made, up_made, silu_ready, hid_ready, hid_turned, hid_T_ready, y_low, y_high, y_ready, stored, all_stored = (
                sem(n) for n in ("xw_ready", "gate_made", "up_made", "silu_ready", "hid_ready", "hid_turned",
                                 "hid_T_ready", "y_low", "y_high", "y_ready", "stored", "all_stored"))
            in_gate, in_up, in_turned, in_y = b.bank[0:4]

            def look_up(eng, at, e, low, high):
                return eng.value_load(table[0:1, bass.ds(at + e, 1)], min_val=low, max_val=high)

            @block.sync
            def _(sp):
                with sp.Fori(1, E // RING) as i:
                    for s in range(RING):
                        used = look_up(sp, BASE, RING * i + (s + 1 - RING), 1, E * 8)
                        src = expert_weights(b, layer, RING * i + s)
                        sp.wait_ge(up_made, 2 * used + 2)
                        sp.dma_start(w_gate[:, s], src[0]).then_inc(arrived[s][0], 16)
                        sp.dma_start(w_up[:, s], src[1]).then_inc(arrived[s][1], 16)
                        sp.wait_ge(y_low, used)
                        sp.wait_ge(y_high, used)
                        sp.dma_start(w_down[:, s], src[2]).then_inc(arrived[s][2], 16)

            @block.gpsimd
            def _(pool):
                with pool.Fori(0, look_up(pool, TOTAL, 0, E, E * 2)) as w:
                    at = look_up(pool, START, w, 0, SLOTS)
                    pool.wait_ge(up_made, 2 * w + 2)
                    nc.gpsimd.tensor_copy(xw[:, :, :], xs[:, :, bass.ds(at, WIN)]).then_inc(xw_ready, 1)

            @block.tensor
            def _(pe):
                pe.sem_inc(up_made, 2)
                with pe.Fori(0, E // RING) as i:
                    for s in range(RING):
                        base, count_ = look_up(pe, BASE, RING * i + s, 0, E * 8), look_up(pe, CNT, RING * i + s, 1, 8)
                        arrival = pe.snap(16 * i + 16)
                        with pe.Fori(0, count_) as n:
                            here = pe.snap(base + n + 1)
                            pe.wait_ge(xw_ready, here)
                            for w, part, bank, is_made in ((w_gate, 0, in_gate, gate_made), (w_up, 1, in_up, up_made)):
                                pe.wait_ge(arrived[s][part], arrival)
                                for k in range(KD):
                                    for f in range(2):
                                        made = nc.tensor.matmul(bank[WIN * f:WIN * f + WIN, 0:P], xw[:, k, :], w[:, s, k, P * f:P * f + P],
                                                                start=(k == 0), stop=(k == KD - 1))
                                        if k == KD - 1:
                                            made.then_inc(is_made, 1)
                            pe.wait_ge(hid_ready, here)
                            nc.tensor.transpose(in_turned[:, 0:P], hid[:, :], b.ident[:, :]).then_inc(hid_turned, 1)
                            pe.wait_ge(arrived[s][2], arrival)
                            pe.wait_ge(y_ready, here)
                            pe.wait_ge(hid_T_ready, here)
                            for f in range(2):
                                for half, is_made in ((0, y_low), (1, y_high)):
                                    made = nc.tensor.matmul(in_y[WIN * half:WIN * half + WIN, :], hid_T[:, f, :],
                                                            w_down[:, s, f, 512 * half:512 * half + 512], start=(f == 0), stop=(f == 1))
                                    if f == 1:
                                        made.then_inc(is_made, 1)

            @block.scalar
            def _(act):
                total = look_up(act, TOTAL, 0, E, E * 2)

                def store(w, at):
                    act.wait_ge(y_ready, w + 1)
                    act.wait_ge(stored, 16 * w + 16)
                    act.dma_start(rows[bass.ds(at, WIN), :].rearrange("s (h c) -> h s c", h=2),
                                  y[:, bass.ds((w + 1) % 2, 1), :].rearrange("p o c -> p (o c)")).then_inc(stored, 16)

                act.wait_ge(gate_made, 2)
                nc.scalar.activation(silu, in_gate[:, 0:P], ACT.Silu).then_inc(silu_ready, 1)
                with act.Fori(1, total) as w:
                    act.wait_ge(gate_made, 2 * w + 2)
                    nc.scalar.activation(silu, in_gate[:, 0:P], ACT.Silu).then_inc(silu_ready, 1)
                    store(w, look_up(act, START, w - 1, 0, SLOTS))
                store(total, look_up(act, START, total - 1, 0, SLOTS))
                act.wait_ge(stored, 16 * total + 32)
                act.sem_inc(all_stored, 1)

            @block.vector
            def _(dve):
                dve.sem_inc(stored, 32)
                dve.sem_inc(y_ready, 1)
                total = look_up(dve, TOTAL, 0, E, E * 2)
                with dve.Fori(0, total) as w:
                    dve.wait_ge(silu_ready, w + 1)
                    dve.wait_ge(up_made, 2 * w + 4)
                    nc.vector.tensor_tensor(hid[:, :], silu[:, :], in_up[:, 0:P], ALU.mult).then_inc(hid_ready, 1)
                    dve.wait_ge(hid_turned, w + 1)
                    nc.vector.tensor_copy(hid_T[:, :, :], in_turned[:, 0:P].rearrange("p (f s) -> p f s", f=2)).then_inc(hid_T_ready, 1)
                    dve.wait_ge(y_low, w + 1)
                    dve.wait_ge(y_high, w + 1)
                    dve.wait_ge(stored, 16 * w + 16)
                    nc.vector.tensor_copy(y[:, bass.ds(w % 2, 1), :].rearrange("p o c -> p (o c)"), in_y).then_inc(y_ready, 1)

        results = xn[:, :, :], hT[:, :, :].rearrange("p (i a) t -> p i (a t)", i=NT)
        fetched, added, squared = [sem(f"fetched{i}") for i in range(NT)], sem("added"), sem("squared")
        with nc.Block() as block:
            @block.gpsimd
            def _(pool):
                pool.wait_ge(all_stored, 1)
                for i in range(NT):
                    for which, result in enumerate(results):
                        row = slot_rows[:, NT * which + i:NT * which + i + 1]
                        nc.gpsimd.indirect_dma_start(result[:, i, :], None, rows[0:SLOTS, :],
                                                     bass.IndirectOffsetOnAxis(row, 0)).then_inc(fetched[i], 16)

            @block.vector
            def _(dve):
                for i in range(NT):
                    dve.wait_ge(fetched[i], 32)
                    for which, (result, gate) in enumerate(zip(results, (gate1, gate2))):
                        nc.vector.scalar_tensor_tensor(b.h[:, i, :], result[:, i, :], gate[:, i:i + 1], b.h[:, i, :],
                                                       ALU.mult, ALU.add).then_inc(added, 1)
                        if which == 0:
                            dve.wait_ge(added, 2 * i + 1)

            @block.scalar
            def _(act):
                for i in range(NT):
                    act.wait_ge(added, 2 * i + 2)
                    if i:
                        act.wait_ge(squared, i)
                    square_tile(b, i, spare[:, 0, :]).then_inc(squared, 1)


NH, HD = 4, 128
CONV_K = 4
GD_IN = 4 * NH * HD + 2 * NH
BETA, DECAY, IGATE, FGATE = 0, 32, 64, 96
ODD_LOADS = [0, 512, 1024, 1536, GD_IN, GD_IN + 512, GD_IN + 1024, GD_IN + 1536]


class Odd:

    def __init__(self, b, ctx):
        def sb(name, *shape):
            return b.sb(ctx, name, [P, *shape])

        self.w = sb("w_odd", 2, KD, 512)
        in_ring = b.carver()
        self.hT = in_ring(KD, T)
        self.QKx = in_ring(8, T)
        self.Q, self.K = self.QKx[:, 0:4, :], self.QKx[:, 4:8, :]
        self.xn = self.QKx[:, :, :].rearrange("p (i a) t -> p i (a t)", i=NT)
        self.V, self.Z = sb("Vo", 4, T), in_ring(4, T)
        self.BB, self.EG, self.GM = in_ring(4, T), in_ring(4, T), sb("GM", 4, T)
        self.KB, self.KW, self.QG, self.KD = sb("KB", 4, T), in_ring(4, T), in_ring(4, T), in_ring(4, T)
        self.mq, self.mk, self.og, self.GB = in_ring(4, T), in_ring(4, T), sb("og", 4, T), sb("GB", 4, T)
        self.raw = flat(self.og)[:, 0:2 * (T + 3)].rearrange("p (a t) -> p a t", a=2)
        self.VO = sb("VO", NT, NH, HD + 1)
        self.wg = flat(self.GB)[:, 0:KD * P].rearrange("p (k f) -> p k f", k=KD)
        self.rows, self.grow = sb("rows", T), sb("grow", T)
        self.Y = self.Z[:, 0, :]
        self.cols = sb("cols", NT, P)
        self.gcol = sb("gcol", 8)
        self.gl = sb("gl", 4, NT)
        self.stat = sb("stat_o", 64)


def odd_load(b, sp, m, n):
    w_all = b.dram["od_w_in"][0].rearrange("(p k) n -> p k n", k=KD)
    sp.dma_start(m.w[:, n % 2, :, :], w_all[:, :, ODD_LOADS[n]:ODD_LOADS[n] + 512]).then_inc(b.sem(f"odd_w_in{n % 2}"), 16)


def odd_first_loads(b, sp, m):
    w_all = b.dram["od_w_in"][0].rearrange("(p k) n -> p k n", k=KD)
    odd_load(b, sp, m, 0)
    sp.wait_ge(b.sem("odd_wg_zero"), 1)
    with b.nc.allow_non_contiguous_dma(reason="gate columns"):
        for row, c in ((BETA, 2048), (DECAY, 2052), (IGATE, GD_IN + 2048), (FGATE, GD_IN + 2052)):
            sp.dma_start(m.wg[:, :, row:row + NH], w_all[:, :, c:c + NH]).then_inc(b.sem("odd_wg_in"), 16)
    odd_load(b, sp, m, 1)


def odd_project(b, m):
    nc, d = b.nc, b.dram
    items = [("gates", 0)] + [(kind, j) for kind in ("gq", "gk", "gv", "z") for j in range(4)] + [("cols", 0)]
    items += [(kind, j) for kind in ("bb", "gb", "Gb", "nq", "nk", "mq", "mk", "mv", "mo") for j in range(4)]
    at = {it: n for n, it in enumerate(items)}
    loads = ["gq", "gk", "gv", "z", "mq", "mk", "mv", "mo"]
    bias, sign, coef, alog = (m.gcol[:, i:i + 1] for i in range(4))

    with nc.Block() as block:
        w_sem = [b.sem("odd_w_in0"), b.sem("odd_w_in1")]
        wg_in, bias_zero, bias_in = (b.sem(f"odd_{x}") for x in ("wg_in", "bias_zero", "bias_in"))
        made, evac, conved, silued = (b.sem(f"odd_{x}") for x in ("made", "evac", "conved", "silued"))
        y_ready, row_act, row_dve, squares = (b.sem(f"odd_{x}") for x in ("y_ready", "row_act", "row_dve", "squares"))
        ln_done, kd_in, kd_out, raw_zero, alog_exp = (b.sem(f"odd_{x}") for x in ("ln_done", "kd_in", "kd_out", "raw_zero", "alog_exp"))

        def evacuated(eng, n):
            if n == 0:
                eng.wait_ge(y_ready, 1)
            else:
                eng.wait_ge(evac, n)

        @block.sync
        def _(sp):
            for n in range(2, len(ODD_LOADS)):
                sp.wait_ge(made, at[loads[n - 2], 3] + 1)
                odd_load(b, sp, m, n)

        @block.gpsimd
        def _(pool):
            with nc.allow_non_contiguous_dma(reason="gate columns"):
                pool.wait_ge(bias_zero, 1)
                for row, name, col in ((DECAY, "gd_dt_bias", bias), (IGATE, "ml_i_bias", bias), (FGATE, "ml_f_bias", bias),
                                       (DECAY, "gd_a_log", alog)):
                    pool.dma_start(col[row:row + NH, :], d[name][0].rearrange("(p o) -> p o", o=1)).then_inc(bias_in, 16)
            nc.gpsimd.memset(m.VO[:, :, :, HD:HD + 1], 1.0)

        @block.tensor
        def _(pe):
            for n, (kind, j) in enumerate(items):
                bank = b.bank[n % 8]
                if n >= 8:
                    evacuated(pe, n - 8)
                if kind == "gates":
                    pe.wait_ge(wg_in, 64)
                    for k in range(KD):
                        last = nc.tensor.matmul(bank, m.wg[:, k, :], m.hT[:, k, :], start=(k == 0), stop=(k == KD - 1))
                elif kind in loads:
                    load = loads.index(kind)
                    if j == 0:
                        pe.wait_ge(w_sem[load % 2], 16 * (load // 2 + 1))
                    w = m.w[:, load % 2, :, :]
                    for k in range(KD):
                        if kind == "mv":
                            last = nc.tensor.matmul(bank, m.hT[:, k, P * j:P * j + P], w[:, k, :],
                                                    start=(k == 0), stop=(k == KD - 1))
                        else:
                            last = nc.tensor.matmul(bank, w[:, k, P * j:P * j + P], m.hT[:, k, :],
                                                    start=(k == 0), stop=(k == KD - 1))
                elif kind == "cols":
                    pe.wait_ge(row_dve, 3)
                    pe.wait_ge(row_act, 5)
                    for c in range(NT):
                        last = nc.tensor.transpose(bank[:, P * c:P * c + P], m.rows[:, P * c:P * c + P], b.ident[:, :])
                elif kind in ("bb", "gb", "Gb"):
                    row = {"bb": BETA, "gb": DECAY, "Gb": FGATE}[kind] + j
                    src = m.grow if kind == "Gb" else m.rows
                    last = nc.tensor.matmul(bank, b.ident[:, row:row + 1].broadcast_to([P, P]), src[:, :],
                                            start=True, stop=True)
                else:
                    pe.wait_ge(squares, (0 if kind == "nq" else 4) + j + 1)
                    src = m.KD if kind == "nq" else m.KW
                    last = nc.tensor.matmul(bank, b.ones[:, :], src[:, j, :], start=True, stop=True)
                last.then_inc(made, 1)

        @block.scalar
        def _(act):
            def evacuate(n):
                kind, j = items[n]
                bank = b.bank[n % 8]
                act.wait_ge(made, n + 1)
                if kind in ("gq", "gk", "gv"):
                    if n <= 2:
                        act.wait_ge(raw_zero, 1)
                    else:
                        act.wait_ge(conved, n - 2)
                    ins = nc.scalar.activation(m.raw[:, (n - 1) % 2, 3:T + 3], bank, ACT.Copy)
                elif kind == "z":
                    ins = nc.scalar.activation(m.Z[:, j, :], bank, ACT.Silu)
                elif kind == "mo":
                    ins = nc.scalar.activation(m.og[:, j, :], bank, ACT.Sigmoid)
                elif kind == "gb":
                    nc.scalar.activation(m.GM[:, j, :], bank, ACT.Copy)
                    ins = nc.scalar.activation(m.EG[:, j, :], bank, ACT.Exp)
                elif kind in ("nq", "nk"):
                    t = (m.KD if kind == "nq" else m.KW)[:, j, :]
                    nc.scalar.activation(t, bank, ACT.Ln, bias=b.eps[:, 0:1]).then_inc(ln_done, 1)
                    act.wait_ge(ln_done, (0 if kind == "nq" else 4) + j + 1)
                    ins = nc.scalar.activation(t, t, ACT.Exp, scale=-0.5, bias=b.eps[:, 2:3] if kind == "nq" else 0.0)
                elif kind == "cols":
                    ins = nc.scalar.activation(m.cols[:, :, :].rearrange("p c f -> p (c f)"), bank, ACT.Copy)
                elif kind == "mv":
                    ins = nc.scalar.activation(m.VO[:, j, :, 0:HD], bank.rearrange("p (h v) -> p h v", h=NH), ACT.Copy)
                else:
                    dst = {"bb": m.BB, "Gb": m.GB, "mq": m.mq, "mk": m.mk}[kind]
                    ins = nc.scalar.activation(dst[:, j, :], bank, ACT.Copy)
                ins.then_inc(evac, 1)

            def silu(i):
                t = (m.Q, m.K, m.V)[i // 4][:, i % 4, :]
                act.wait_ge(conved, i + 1)
                nc.scalar.activation(t, t, ACT.Silu).then_inc(silued, 1)

            act.wait_ge(bias_in, 64)
            nc.scalar.activation(alog[DECAY:DECAY + NH, :], alog[DECAY:DECAY + NH, :], ACT.Exp).then_inc(alog_exp, 1)
            act.wait_ge(y_ready, 2)
            nc.scalar.activation(m.rows[0:32, :], m.Y[0:32, :], ACT.Sigmoid).then_inc(row_act, 1)
            nc.scalar.activation(m.grow[:, :], m.grow[:, :], ACT.Exp, scale=-1.0).then_inc(row_act, 1)
            act.wait_ge(row_act, 2)
            nc.scalar.activation(m.grow[:, :], m.grow[:, :], ACT.Ln, bias=b.ones[:, 0:1]).then_inc(row_act, 1)
            for n in range(1, 13):
                evacuate(n)
                if n >= 2:
                    silu(n - 2)
            silu(11)
            for j in range(4):
                act.wait_ge(silued, 8)
                nc.scalar.activation(m.KD[:, j, :], m.Q[:, j, :], ACT.Square).then_inc(squares, 1)
            for j in range(4):
                nc.scalar.activation(m.KW[:, j, :], m.K[:, j, :], ACT.Square).then_inc(squares, 1)
            nc.scalar.activation(m.KB[FGATE:P, 0, :], m.Y[IGATE:IGATE + 32, :], ACT.Copy).then_inc(row_act, 1)
            act.wait_ge(row_dve, 4)
            nc.scalar.activation(m.rows[IGATE:IGATE + 32, :], m.KB[FGATE:P, 1, :], ACT.Exp, scale=-1.0).then_inc(row_act, 1)
            for n in range(13, at["mq", 0]):
                evacuate(n)
            act.wait_ge(kd_in, 1)
            nc.scalar.activation(flat(m.KD), flat(m.KD), ACT.Exp, scale=-1.0).then_inc(kd_out, 1)
            for n in range(at["mq", 0], len(items)):
                evacuate(n)

        @block.vector
        def _(dve):
            link = b.link(dve, "dve_steps")
            V = nc.vector
            link(V.memset(m.gcol[:, :], 0.0))
            V.memset(coef, -1.0)
            V.memset(sign[0:FGATE, :], 1.0)
            V.memset(sign[FGATE:P, :], -1.0).then_inc(bias_zero, 1)
            V.memset(m.raw[:, :, 0:3], 0.0).then_inc(raw_zero, 1)
            V.memset(m.rows[:, :], 0.0)
            dve.wait_ge(alog_exp, 1)
            dve.wait_ge(bias_zero, 1)
            link(V.tensor_scalar(coef[DECAY:DECAY + NH, :], alog[DECAY:DECAY + NH, :], -1.0, None, ALU.mult))
            dve.wait_ge(made, 1)
            V.tensor_scalar(m.Y[:, :], b.bank[0], bias, sign, ALU.add, ALU.mult).then_inc(y_ready, 1)
            dve.wait_ge(y_ready, 1)
            V.scalar_tensor_tensor(m.grow[:, :], m.Y[:, :], -1.0, m.Y[:, :], ALU.mult, ALU.max).then_inc(y_ready, 1)
            for i in range(12):
                dst = (m.Q, m.K, m.V)[i // 4][:, i % 4, :]
                raw = m.raw[:, i % 2, :]
                dve.wait_ge(evac, i + 1)
                link(V.tensor_scalar(dst, raw[:, 0:T], b.col("gd_conv", i), None, ALU.mult))
                for tap in range(1, CONV_K):
                    ins = V.scalar_tensor_tensor(dst, raw[:, tap:tap + T], b.col("gd_conv", 12 * tap + i), dst, ALU.mult, ALU.add)
                    if tap < CONV_K - 1:
                        link(ins)
                ins.then_inc(conved, 1)
                if i == 1:
                    dve.wait_ge(row_act, 3)
                    sp_ = m.Y[:, :]
                    link(V.tensor_scalar(m.KB[:, 2, :], sp_, 0.0, None, ALU.max))
                    link(V.tensor_tensor(m.KB[:, 2, :], m.KB[:, 2, :], m.grow[:, :], ALU.add))
                    link(V.tensor_scalar(m.KB[:, 2, :], m.KB[:, 2, :], coef, None, ALU.mult))
                    for c in range(NT):
                        ins = V.tensor_tensor_scan(m.rows[DECAY:DECAY + 32, P * c:P * c + P], b.ones[DECAY:DECAY + 32, :],
                                                   m.KB[DECAY:DECAY + 32, 2, P * c:P * c + P], 0.0, ALU.mult, ALU.add)
                    ins.then_inc(row_dve, 1)
            f = slice(FGATE, P)
            B_ = m.KB[f, 3, :]
            one = b.ones[f, 0:1].broadcast_to([32, T])
            link(V.tensor_tensor_scan(B_, one, m.KB[f, 2, :], 0.0, ALU.mult, ALU.add))
            dve.wait_ge(row_act, 4)
            V.tensor_tensor(m.rows[f, :], m.KB[f, 0, :], B_, ALU.subtract).then_inc(row_dve, 1)
            dve.wait_ge(row_dve, 2)
            link(V.memset(m.grow[0:FGATE, :], 0.0))
            V.tensor_tensor_scan(m.grow[f, :], m.rows[f, :], m.rows[f, :], 0.0, ALU.max, ALU.max).then_inc(row_dve, 1)
            dve.wait_ge(row_dve, 3)
            V.tensor_tensor(m.KB[f, 1, :], B_, m.grow[f, :], ALU.add).then_inc(row_dve, 1)
            dve.wait_ge(silued, 12)
            evacuated(dve, at["nk", 3])
            V.tensor_tensor(flat(m.V), flat(m.V), flat(m.BB), ALU.mult)
            V.tensor_tensor(flat(m.Q), flat(m.Q), flat(m.KD), ALU.mult)
            link(V.tensor_tensor(flat(m.K), flat(m.K), flat(m.KW), ALU.mult))
            gm = m.GM[:, :, :].rearrange("p h (c t) -> p (h c) t", c=NT)
            V.tensor_tensor(m.KD[:, :, :].rearrange("p h (c t) -> p (h c) t", c=NT), gm,
                            gm[:, :, P - 1:P].broadcast_to([P, 4 * NT, P]), ALU.subtract).then_inc(kd_in, 1)
            link(V.tensor_tensor(flat(m.KB), flat(m.K), flat(m.BB), ALU.mult))
            V.scalar_tensor_tensor(flat(m.KW), flat(m.KB), -1.0, flat(m.EG), ALU.mult, ALU.mult)
            V.tensor_tensor(flat(m.QG), flat(m.Q), flat(m.EG), ALU.mult)
            V.tensor_copy(m.gl[:, :, :], chunks(m.EG)[:, :, :, P - 1])
            dve.wait_ge(kd_out, 1)
            V.tensor_tensor(flat(m.KD), flat(m.KD), flat(m.K), ALU.mult)


def delta_chunks(b, m):
    nc = b.nc
    w = m.w[:, :, :, :].rearrange("p a k n -> p (a k n)")

    def mats(i):
        return w[:, 8 * P * i:8 * P * (i + 1)].rearrange("p (h s) -> p h s", h=8)

    MT, X, XT, PR, AT, DC, DS = (mats(i) for i in range(7))
    VBt, KDt = m.hT[:, 0:4, :], m.hT[:, 4:8, :]
    Ot = m.Ot = m.BB
    S = m.EG[:, 0, :]
    RHS, VN = m.EG[:, 1, :], m.EG[:, 2, :]

    fills = [("MT", 0), ("MT", 1), ("AT", 0), ("AT", 1), ("X0", 0), ("X0", 1)] + doubling_fills()
    for g in range(2):
        fills += [("KS", g), ("VN", g), ("O", g), ("dS", g)]
    acts = [f for f in fills if f[0] in ("X0", "VN", "O")]
    dves = [f for f in fills if f not in acts]

    def bank_of(name, g):
        first = {"MT": 0, "AT": 6, "X0": 2, "KS": 0, "VN": 2, "O": 4, "dS": 6}
        if name in first:
            return b.bank[first[name] + g]
        return b.bank[doubling_bank(name) + g]

    with nc.Block() as block:
        turned, turned_out = b.sem("gd_turned"), b.sem("gd_turned_out")
        filled, by_act, by_dve = b.sem("gd_filled"), b.sem("gd_by_act"), b.sem("gd_by_dve")
        first_x, state, d_in, d_exp = (b.sem(f"gd_{x}") for x in ("first_x", "state", "d_in", "d_exp"))
        order = Order(fills, acts, dves, filled, by_act, by_dve)

        @block.tensor
        def _(pe):
            for i in range(8):
                src = (m.V if i < 4 else m.KD)[:, i % 4, :]
                for c in range(NT):
                    last = nc.tensor.transpose(b.bank[i][:, P * c:P * c + P], src[:, P * c:P * c + P], b.ident[:, :])
                last.then_inc(turned, 1)
            pe.wait_ge(turned_out, 8)
            for c2 in range(NT // 2):
                for name, right in (("MT", m.KB), ("AT", m.Q)):
                    for g in range(2):
                        if c2:
                            order.wait_taken(pe, c2 - 1, {"MT": ("KS", g), "AT": ("dS", g)}[name])
                        tok = slice(P * (2 * c2 + g), P * (2 * c2 + g) + P)
                        for h in range(NH):
                            last = nc.tensor.matmul(bank_of(name, g)[:, P * h:P * h + P], m.K[:, h, tok], right[:, h, tok],
                                                    start=True, stop=True)
                        last.then_inc(filled, 1)
                for g in range(2):
                    pe.wait_ge(first_x, 2 * c2 + g + 1)
                    if c2:
                        order.wait_taken(pe, c2 - 1, ("VN", g))
                    for h in range(NH):
                        last = nc.tensor.transpose(bank_of("X0", g)[:, P * h:P * h + P], XT[:, 4 * g + h, :], b.ident[:, :])
                    last.then_inc(filled, 1)
                if c2:
                    order.wait_taken(pe, c2 - 1, ("O", 1))
                pe_doubling(nc, pe, order, c2, bank_of, MT, X, XT, PR)
                for g in range(2):
                    c = 2 * c2 + g
                    tok = slice(P * c, P * c + P)
                    pe.wait_ge(state, c + 1)
                    order.wait_taken(pe, c2, ("P6", g))
                    for h in range(NH):
                        last = nc.tensor.matmul(bank_of("KS", g)[:, P * h:P * h + P], m.KW[:, h, tok], S[:, P * h:P * h + P],
                                                start=True, stop=True)
                    last.then_inc(filled, 1)
                    order.wait_taken(pe, c2, ("KS", g))
                    order.wait_taken(pe, c2, ("XT6", g))
                    for h in range(NH):
                        last = nc.tensor.matmul(bank_of("VN", g)[:, P * h:P * h + P], XT[:, 4 * g + h, :], RHS[:, P * h:P * h + P],
                                                start=True, stop=True)
                    last.then_inc(filled, 1)
                    order.wait_taken(pe, c2, ("AT", g))
                    order.wait_taken(pe, c2, ("VN", g))
                    for h in range(NH):
                        o = bank_of("O", g)[:, P * h:P * h + P]
                        nc.tensor.matmul(o, m.QG[:, h, tok], S[:, P * h:P * h + P], start=True, stop=False)
                        last = nc.tensor.matmul(o, AT[:, 4 * g + h, :], VN[:, P * h:P * h + P], start=False, stop=True)
                    last.then_inc(filled, 1)
                    for h in range(NH):
                        last = nc.tensor.matmul(bank_of("dS", g)[:, P * h:P * h + P], KDt[:, c, P * h:P * h + P],
                                                VN[:, P * h:P * h + P], start=True, stop=True)
                    last.then_inc(filled, 1)

        @block.scalar
        def _(act):
            act.wait_ge(d_in, 1)
            nc.scalar.activation(flat(DC), flat(DC), ACT.Exp).then_inc(d_exp, 1)
            for i in range(1, 8, 2):
                act.wait_ge(turned, i + 1)
                nc.scalar.activation((VBt if i < 4 else KDt)[:, :, P * (i % 4):P * (i % 4) + P],
                                     b.bank[i].rearrange("p (c f) -> p c f", c=NT), ACT.Copy).then_inc(turned_out, 1)
            for c2 in range(NT // 2):
                for f in acts:
                    name, g = f
                    order.wait_filled(act, c2, f)
                    dst = {"X0": X[:, 4 * g:4 * g + 4, :].rearrange("p h s -> p (h s)"), "VN": VN,
                           "O": Ot[:, 2 * c2 + g, :]}[name]
                    nc.scalar.activation(dst, bank_of(name, g), ACT.Copy).then_inc(by_act, 1)
                    if f == ("X0", 1) and c2 + 1 < NT // 2:
                        act.wait_ge(d_in, c2 + 2)
                        nc.scalar.activation(flat(DC), flat(DC), ACT.Exp).then_inc(d_exp, 1)

        @block.vector
        def _(dve):
            link = b.link(dve, "dve_steps")
            V = nc.vector
            next_decays = {("XT2", 1): 0, ("XT3", 1): 1, ("XT4", 1): 2}

            def decays(c2, step):
                if step == 0:
                    for g in range(2):
                        c = 2 * c2 + g
                        for h in range(NH):
                            last = V.tensor_scalar(DC[:, 4 * g + h, :], m.GM[:, h, P * c:P * c + P],
                                                   m.cols[:, c, DECAY + h:DECAY + h + 1], 0.0, ALU.subtract, ALU.min)
                    last.then_inc(d_in, 1)
                if step == 1:
                    dve.wait_ge(d_exp, c2 + 1)
                    link(V.scalar_tensor_tensor(DS, DC, -1.0, eight(b.before[:, :]), ALU.mult, ALU.mult))
                if step == 2:
                    link(V.tensor_tensor(DC, DC, eight(b.causal[:, :]), ALU.mult))

            decays(0, 0)
            for i in range(0, 8, 2):
                dve.wait_ge(turned, i + 1)
                V.tensor_copy((VBt if i < 4 else KDt)[:, :, P * (i % 4):P * (i % 4) + P],
                              b.bank[i].rearrange("p (c f) -> p c f", c=NT)).then_inc(turned_out, 1)
            V.memset(S, 0.0).then_inc(state, 1)

            def eight(mask):
                return mask.rearrange("p (o s) -> p o s", o=1).broadcast_to([P, 8, P])

            for step in (1, 2):
                decays(0, step)
            for c2 in range(NT // 2):
                for f in dves:
                    name, g = f
                    bank = bank_of(name, g)
                    four = bank.rearrange("p (h s) -> p h s", h=4)
                    hs = slice(4 * g, 4 * g + 4)
                    order.wait_filled(dve, c2, f)
                    if name == "MT":
                        V.tensor_tensor(MT[:, hs, :], four, DS[:, hs, :], ALU.mult).then_inc(by_dve, 1)
                        order.wait_taken(dve, c2, f)
                        first_inverse(nc, b, link, MT[:, hs, :], XT[:, hs, :]).then_inc(first_x, 1)
                    elif name == "AT":
                        V.tensor_tensor(AT[:, hs, :], four, DC[:, hs, :], ALU.mult).then_inc(by_dve, 1)
                    elif name == "KS":
                        V.tensor_tensor(RHS, bank, VBt[:, 2 * c2 + g, :], ALU.add).then_inc(by_dve, 1)
                    elif name == "dS":
                        c = 2 * c2 + g
                        for h in range(NH):
                            s = S[:, P * h:P * h + P]
                            last = V.scalar_tensor_tensor(s, s, m.gl[:, h, c:c + 1], bank[:, P * h:P * h + P],
                                                          ALU.mult, ALU.add)
                        last.then_inc(by_dve, 1)
                        order.wait_taken(dve, c2, f)
                        V.tensor_copy(m.stat[:, 0:1], S[:, 0:1]).then_inc(state, 1)
                    else:
                        take_doubling(nc, b, name, g, four, X, XT, PR).then_inc(by_dve, 1)
                        if f in next_decays and c2 + 1 < NT // 2:
                            decays(c2 + 1, next_decays[f])


def mlstm(b, m):
    nc, d = b.nc, b.dram
    w_out = d["od_w_out"][0].rearrange("(k p) n -> p k n", p=P)
    at, n = {}, 0
    for h in range(NH):
        for j in range(NT):
            at[h, j] = n
            n += NT - j
    SC = m.QKx[:, :, :].rearrange("p a t -> p (a t)")
    SC2 = flat(m.KB)

    def weights(h, j, i, width=1):
        if h < 3:
            return SC[:, P * (at[h, j] + i - j):P * (at[h, j] + i - j + width)]
        return SC2[:, P * (at[h, j] - 30 + i - j):P * (at[h, j] - 30 + i - j + width)]

    D_ = flat(m.KW)
    NUM = m.hT[:, :, :].rearrange("p k t -> p (k t)")[:, 0:NT * NH * (HD + 1)].rearrange("p (c h v) -> p c h v", c=NT, h=NH)
    Ht = m.QG[:, :, :]
    den = m.stat[:, 0:16].rearrange("p (c h) -> p c h", c=NT)
    m.YC, m.YD = m.GM, m.V
    pairs = [(h, j) for h in range(NH) for j in range(NT)]
    with nc.Block() as block:
        s_made, s_taken, d_in, d_exp, n_made, n_taken = (b.sem(f"ml_{x}") for x in ("s", "s_taken", "d_in", "d_exp", "n", "n_taken"))
        squared, var_in, var_out, normed, turned, turned_taken, h_ready = (
            b.sem(f"ml_{x}") for x in ("squared", "var_in", "var_out", "normed", "turned", "turned_taken", "h_ready"))
        w_out_in, yc_ready = b.sem("odd_w_out_in"), b.sem("ml_yc_ready")

        @block.sync
        def _(sp):
            for i in range(2):
                sp.dma_start(m.w[:, i, :, :], w_out[:, :, 512 * i:512 * i + 512]).then_inc(w_out_in, 16)

        @block.tensor
        def _(pe):
            for n, (h, j) in enumerate(pairs):
                if n >= 4:
                    pe.wait_ge(s_taken, n - 3)
                nc.tensor.matmul(b.bank[n % 4][:, 0:T - P * j], m.mk[:, h, P * j:P * j + P], m.mq[:, h, P * j:T],
                                 start=True, stop=True).then_inc(s_made, 1)
            for i in range(NT):
                for half in range(2):
                    n = 2 * i + half
                    if n >= 4:
                        pe.wait_ge(n_taken, n - 3)
                    pe.wait_ge(s_taken, 16)
                    for hh in range(2):
                        h = 2 * half + hh
                        for j in range(i + 1):
                            last = nc.tensor.matmul(b.bank[4 + n % 4][:, (HD + 1) * hh:(HD + 1) * (hh + 1)], weights(h, j, i),
                                                    m.VO[:, j, h, :], start=(j == 0), stop=(j == i))
                    last.then_inc(n_made, 1)
            for i, src in enumerate((m.Ot, Ht)):
                pe.wait_ge(normed, i + 1)
                for j in range(4):
                    for c in range(NT):
                        last = nc.tensor.transpose(b.bank[j][:, P * c:P * c + P], src[:, c, P * j:P * j + P], b.ident[:, :])
                    last.then_inc(turned, 1)
                if i == 0:
                    pe.wait_ge(n_taken, 8)
                    pe.wait_ge(yc_ready, 4)
                    project_out_early(b, pe, m.w, w_out_in, lambda k: m.YC[:, k, :])

        @block.scalar
        def _(act):
            nc.scalar.activation(flat(m.KD), flat(m.Ot),
                                 ACT.Square).then_inc(squared, 1)
            for n, (h, j) in enumerate(pairs):
                act.wait_ge(d_in, n + 1)
                t = D_[:, 512 * (n % 4):512 * (n % 4) + T - P * j]
                nc.scalar.activation(t, t, ACT.Exp, scale=-1.0).then_inc(d_exp, 1)
            act.wait_ge(var_in, 1)
            nc.scalar.activation(m.stat[:, 16:32], m.stat[:, 16:32], ACT.Sqrt).then_inc(var_out, 1)
            for n in range(8):
                act.wait_ge(n_made, n + 1)
                nc.scalar.activation(NUM[:, n // 2, 2 * (n % 2):2 * (n % 2) + 2, :],
                                     b.bank[4 + n % 4][:, 0:2 * (HD + 1)].rearrange("p (h v) -> p h v", h=2), ACT.Copy).then_inc(n_taken, 1)
            act.wait_ge(h_ready, 1)
            nc.scalar.activation(m.mq[:, :, :].rearrange("p a t -> p (a t)"), flat(Ht), ACT.Square).then_inc(squared, 1)
            act.wait_ge(var_in, 2)
            nc.scalar.activation(m.stat[:, 32:48], m.stat[:, 32:48], ACT.Sqrt).then_inc(var_out, 1)

        @block.vector
        def _(dve):
            link = b.link(dve, "dve_steps")
            V = nc.vector
            lag = 2

            def exponent(n):
                h, j = pairs[n]
                if n >= 4:
                    dve.wait_ge(s_taken, n - 3)
                V.tensor_scalar(D_[:, 512 * (n % 4):512 * (n % 4) + T - P * j], m.GB[:, h, P * j:T],
                                m.cols[:, j, FGATE + h:FGATE + h + 1], 0.0, ALU.subtract, ALU.max).then_inc(d_in, 1)

            def mean_square(i, squares):
                ssq = m.stat[:, 16 + 16 * i:32 + 16 * i]
                link(V.reduce_sum(ssq, flat(squares).rearrange("p (g v) -> p g v", v=HD), AX.X))
                V.tensor_scalar(ssq, ssq, 1.0 / HD, NORM_EPS, ALU.mult, ALU.add).then_inc(var_in, 1)

            def normalise(i, t):
                ssq = m.stat[:, 16 + 16 * i:32 + 16 * i]
                dve.wait_ge(var_out, i + 1)
                link(V.reciprocal(ssq, ssq))
                t3 = flat(t).rearrange("p (g v) -> p g v", v=HD)
                V.tensor_tensor(t3, t3, ssq.rearrange("p (g o) -> p g o", o=1).broadcast_to([P, 16, HD]),
                                ALU.mult).then_inc(normed, 1)

            for n in range(lag):
                exponent(n)
            for n, (h, j) in enumerate(pairs):
                if n + lag < 16:
                    exponent(n + lag)
                dve.wait_ge(d_exp, n + 1)
                dve.wait_ge(s_made, n + 1)
                t = D_[:, 512 * (n % 4):512 * (n % 4) + T - P * j]
                link(V.tensor_tensor(t[:, 0:P], t[:, 0:P], b.causal[:, :], ALU.mult))
                V.scalar_tensor_tensor(weights(h, j, j, NT - j), b.bank[n % 4][:, 0:T - P * j], HD ** -0.5, t,
                                       ALU.mult, ALU.mult).then_inc(s_taken, 1)
            dve.wait_ge(squared, 1)
            mean_square(0, m.KD)
            normalise(0, m.Ot)
            dve.wait_ge(n_taken, 8)
            dn = NUM[:, :, :, HD]
            link(V.scalar_tensor_tensor(den, dn, -1.0, dn, ALU.mult, ALU.max))
            link(V.tensor_tensor(den, den, m.cols[:, :, IGATE:IGATE + NH], ALU.max))
            link(V.reciprocal(den, den))
            V.tensor_tensor(Ht.rearrange("p c (h v) -> p c h v", h=NH), NUM[:, :, :, 0:HD],
                            m.stat[:, 0:16].rearrange("p (c h o) -> p c h o", c=NT, o=1).broadcast_to([P, NT, NH, HD]),
                            ALU.mult).then_inc(h_ready, 1)
            for j in range(4):
                dve.wait_ge(turned, j + 1)
                V.scalar_tensor_tensor(m.YC[:, j, :], b.bank[j], b.col("gd_norm"), m.Z[:, j, :],
                                       ALU.mult, ALU.mult).then_inc(yc_ready, 1)
            dve.wait_ge(squared, 2)
            mean_square(1, m.mq)
            normalise(1, Ht)
            for j in range(4):
                dve.wait_ge(turned, 4 + j + 1)
                V.scalar_tensor_tensor(m.YD[:, j, :], b.bank[j], b.col("ml_norm", j), m.og[:, j, :], ALU.mult, ALU.mult)


def odd_layer(b):
    with ExitStack() as ctx:
        m = Odd(b, ctx)
        norm_into(b, "mix1", PAR_AT["norm_mix"] + 8, m.xn, m.hT, lambda sp: odd_first_loads(b, sp, m),
                  lambda: b.nc.gpsimd.memset(m.wg[:, :, :], 0.0).then_inc(b.sem("odd_wg_zero"), 1))
        odd_project(b, m)
        delta_chunks(b, m)
        mlstm(b, m)
        project_out(b, 1, m.w, b.sem("odd_w_out_in"), lambda k: (m.YC if k < 4 else m.YD)[:, k % 4, :],
                    flat(m.KB)[:, 0:D])


def final_norm(b):
    nc, d = b.nc, b.dram
    with ExitStack() as ctx:
        gain, y = b.sb(ctx, "final_gain", [P, D]), b.sb(ctx, "final_y", [P, NT, D])
        ss = b.ss
        with nc.Block() as block:
            gain_in, mean, root, ready, stored = (b.sem(f"final_{x}") for x in ("gain_in", "mean", "root", "ready", "stored"))

            @block.sync
            def _(sp):
                sp.dma_start(gain[:, :], d["norm_final"].rearrange("(o n) -> o n", o=1).broadcast_to([P, D])).then_inc(gain_in, 16)
                for i in range(NT):
                    sp.wait_ge(ready, i + 1)
                    sp.dma_start(b.out[0, P * i:P * i + P, :], y[:, i, :]).then_inc(stored, 16)
                sp.wait_ge(stored, 16 * NT)

            @block.scalar
            def _(act):
                act.wait_ge(mean, 1)
                nc.scalar.activation(ss[:, :], ss[:, :], ACT.Sqrt).then_inc(root, 1)

            @block.vector
            def _(dve):
                link = b.link(dve, "dve_steps")
                nc.vector.tensor_scalar(ss[:, :], ss[:, :], 1.0 / D, NORM_EPS, ALU.mult, ALU.add).then_inc(mean, 1)
                dve.wait_ge(root, 1)
                link(nc.vector.reciprocal(ss[:, :], ss[:, :]))
                dve.wait_ge(gain_in, 16)
                for i in range(NT):
                    nc.vector.scalar_tensor_tensor(y[:, i, :], b.h[:, i, :], ss[:, i:i + 1], gain[:, :],
                                                   ALU.mult, ALU.mult).then_inc(ready, 1)


def program(nc, dram, out):
    with ExitStack() as ctx:
        b = Build(nc, dram, out, ctx)
        constants(b)
        even_layer(b)
        b.end_layer()
        moe(b, 0)
        b.end_layer()
        odd_layer(b)
        b.end_layer()
        moe(b, 1)
        b.end_layer()
        final_norm(b)
        b.end_layer()


def kernel(**inputs):
    import numpy as _np
    import concourse.bacc as _bacc
    from concourse import mybir as _mybir
    from concourse.bass_utils import run_bass_kernel_spmd as _run

    nc = _bacc.Bacc("TRN2", target_bir_lowering=False, num_devices=1)
    arrays, dram = {}, {}
    for name in inputs:
        a = _np.ascontiguousarray(inputs[name])
        arrays[f"in_{name}"] = a
        dram[name] = nc.dram_tensor(f"in_{name}", a.shape, _mybir.dt.from_np(a.dtype), kind="ExternalInput").ap()
    out = nc.dram_tensor("out_0", (1, T, D), F32, kind="ExternalOutput").ap()
    program(nc, dram, out)
    r = _run(nc, [arrays], core_ids=[0])
    return r.results[0]["out_0"]
```
